# Optimizing a Trainium2 kernel written in Bass

```python
import jax
import jax.numpy as jnp
from jax import lax
import numpy as np

D_MODEL = 1024
BATCH = 1
SEQ = 128
DEPTH = 2
DEC_BATCH = 1
DEC_SEQ = 512
PAST_LEN = 128

GRID_W = 64
HEAD_DIM = 64
A_HEADS = 6
A_KV = 2
A_GRP = A_HEADS // A_KV
C_HEADS = 6
C_KV = 2
C_GRP = C_HEADS // C_KV
B_GROUPS = 4
B_GROUP_CH = 64
B_WIDTH = B_GROUPS * B_GROUP_CH
A_Q = A_HEADS * HEAD_DIM
A_KVW = A_KV * HEAD_DIM
C_Q = C_HEADS * HEAD_DIM
C_KVW = C_KV * HEAD_DIM
N_BRANCH = 3
WINDOW = 128
BLOCK = 128
CHUNK = 128
N_EXPERTS = 16
EXPERT_FF = 1024
CAP_FACTOR = 2
ROPE_THETA = 10000.0
ROPE_FREQS = HEAD_DIM // 4
EPS = 1e-6
SPLIT_SIZES = (A_Q, A_KVW, A_KVW, B_WIDTH, B_WIDTH, C_Q, C_KVW, C_KVW, N_BRANCH * D_MODEL)
SPLIT_IDX = tuple(int(i) for i in np.cumsum(SPLIT_SIZES)[:-1])
IN_WIDTH = sum(SPLIT_SIZES)

kernel_name = 'hybrid_diffusion_prefix_step'

def rmsnorm(x, g):
    xf = x.astype(jnp.float32)
    y = xf * lax.rsqrt(jnp.mean(xf * xf, axis=-1, keepdims=True) + EPS)
    return (y * g.astype(jnp.float32)).astype(x.dtype)

def axial_angles(n_tok):
    rows = n_tok // GRID_W
    r = jnp.repeat(jnp.arange(rows, dtype=jnp.float32), GRID_W)
    col = jnp.tile(jnp.arange(GRID_W, dtype=jnp.float32), rows)
    freq = ROPE_THETA ** (-jnp.arange(ROPE_FREQS, dtype=jnp.float32) / ROPE_FREQS)
    return r[:, None] * freq, col[:, None] * freq

def rope_1d(x, ang):
    x1, x2 = x[..., :ROPE_FREQS], x[..., ROPE_FREQS:]
    cos, sin = jnp.cos(ang), jnp.sin(ang)
    return jnp.concatenate([x1 * cos - x2 * sin, x1 * sin + x2 * cos], axis=-1)

def axial_rope(x, ang_r, ang_c):
    shp = (ang_r.shape[0],) + (1,) * (x.ndim - 3) + (ROPE_FREQS,)
    xf = x.astype(jnp.float32)
    half = HEAD_DIM // 2
    out = jnp.concatenate([rope_1d(xf[..., :half], ang_r.reshape(shp)),
                           rope_1d(xf[..., half:], ang_c.reshape(shp))], axis=-1)
    return out.astype(x.dtype)

def softmax_with_sink(s, sink):
    if sink is None:
        return jax.nn.softmax(s, axis=-1)
    sk = sink.astype(jnp.float32)[:, :, None, None]
    m = jnp.maximum(jnp.max(s, axis=-1, keepdims=True), sk)
    e = jnp.exp(s - m)
    return e / (jnp.sum(e, axis=-1, keepdims=True) + jnp.exp(sk - m))

def block_attention(q, k, v, sink):
    b, s, kv, g, hd = q.shape
    nb = s // BLOCK
    qb = jnp.moveaxis(q.reshape(b, nb, BLOCK, kv, g, hd), 1, 0)

    def one_block(qi):
        sc = jnp.einsum('bqkgd,btkd->bkgqt', qi, k).astype(jnp.float32) * (HEAD_DIM ** -0.5)
        p = softmax_with_sink(sc, sink).astype(v.dtype)
        return jnp.einsum('bkgqt,btkd->bqkgd', p, v)

    out = lax.map(one_block, qb)
    return jnp.moveaxis(out, 0, 1).reshape(b, s, kv, g, hd)

def windowed_attention(q, k, v, ck, cv, sink):
    b, s, kv, g, hd = q.shape
    nb = s // BLOCK
    pad = ((0, 0), (BLOCK, BLOCK), (0, 0), (0, 0))
    kp = jnp.pad(k, pad).reshape(b, nb + 2, BLOCK, kv, hd)
    vp = jnp.pad(v, pad).reshape(b, nb + 2, BLOCK, kv, hd)
    kb = jnp.concatenate([kp[:, :-2], kp[:, 1:-1], kp[:, 2:]], axis=2)
    vb = jnp.concatenate([vp[:, :-2], vp[:, 1:-1], vp[:, 2:]], axis=2)
    qb = q.reshape(b, nb, BLOCK, kv, g, hd)
    scale = HEAD_DIM ** -0.5
    s_loc = jnp.einsum('bnqkgd,bnskd->bnkgqs', qb, kb).astype(jnp.float32) * scale
    qi = jnp.arange(BLOCK)[:, None]
    si = jnp.arange(3 * BLOCK)[None, :]
    band = jnp.abs(si - BLOCK - qi) <= WINDOW
    kpos = jnp.arange(nb)[:, None] * BLOCK - BLOCK + jnp.arange(3 * BLOCK)[None, :]
    inside = (kpos >= 0) & (kpos < s)
    mask = band[None] & inside[:, None, :]
    s_loc = jnp.where(mask[None, :, None, None], s_loc, -jnp.inf)
    s_ctx = jnp.einsum('bnqkgd,btkd->bnkgqt', qb, ck).astype(jnp.float32) * scale
    p = softmax_with_sink(jnp.concatenate([s_loc, s_ctx], axis=-1), sink).astype(v.dtype)
    o = (jnp.einsum('bnkgqs,bnskd->bnqkgd', p[..., :3 * BLOCK], vb)
         + jnp.einsum('bnkgqt,btkd->bnqkgd', p[..., 3 * BLOCK:], cv))
    return o.reshape(b, s, kv, g, hd)

def chunk_gmlp(u, v, v_norm_g, w_s, b_s):
    b, n, _ = u.shape
    nc = n // CHUNK
    u = jax.nn.gelu(u).reshape(b, nc, CHUNK, B_GROUPS, B_GROUP_CH)
    v = rmsnorm(jax.nn.gelu(v).reshape(b, nc, CHUNK, B_GROUPS, B_GROUP_CH), v_norm_g.reshape(B_GROUPS, B_GROUP_CH))
    sv = jnp.einsum('gpq,bnqgc->bnpgc', w_s, v) + b_s.T[:, :, None]
    return (u * sv).reshape(b, n, B_WIDTH)

def expert_choice_moe(h, w_router, b_router, w_gate, w_up, w_down):
    b, n, d = h.shape
    cap = CAP_FACTOR * n // N_EXPERTS
    aff = jax.nn.softmax((h @ w_router + b_router).astype(jnp.float32), axis=-1)
    vals, idx = lax.top_k(jnp.swapaxes(aff, 1, 2), cap)
    xg = jax.vmap(lambda xb, ib: xb[ib])(h, idx)
    hh = jax.nn.silu(jnp.einsum('becd,edf->becf', xg, w_gate)) * jnp.einsum('becd,edf->becf', xg, w_up)
    out = jnp.einsum('becf,efd->becd', hh, w_down) * vals[..., None].astype(h.dtype)
    return jax.vmap(lambda ib, ob: jnp.zeros((n, d), ob.dtype).at[ib.reshape(-1)].add(ob.reshape(-1, d)))(idx, out)

def trunk_layer(x, cond, P, l, ctx):
    b, s, _ = x.shape
    mod = (jax.nn.silu(cond) @ P['w_mod'][l] + P['b_mod'][l])[:, None, :]
    sh1, sc1, g1, sh2, sc2, g2 = jnp.split(mod, 6, axis=-1)
    h = rmsnorm(x, P['norm1_g'][l]) * (1 + sc1) + sh1
    aq, ak, av, bu, bv, cq, ck, cv, gl = jnp.split(h @ P['w_in'][l], SPLIT_IDX, axis=-1)
    aq = rmsnorm(aq.reshape(b, s, A_KV, A_GRP, HEAD_DIM), P['a_q_norm'][l])
    ak = rmsnorm(ak.reshape(b, s, A_KV, HEAD_DIM), P['a_k_norm'][l])
    av = av.reshape(b, s, A_KV, HEAD_DIM)
    cq = rmsnorm(cq.reshape(b, s, C_KV, C_GRP, HEAD_DIM), P['c_q_norm'][l])
    ck = rmsnorm(ck.reshape(b, s, C_KV, HEAD_DIM), P['c_k_norm'][l])
    cv = cv.reshape(b, s, C_KV, HEAD_DIM)
    sink = P['a_sink'][l].reshape(A_KV, A_GRP)
    ob = chunk_gmlp(bu, bv, P['b_v_norm'][l], P['b_ws'][l], P['b_bs'][l])
    if ctx is None:
        oa = block_attention(aq, ak, av, sink)
        oc = block_attention(cq, ck, cv, None)
        new = (ak, av, ck, cv)
    else:
        cak, cav, cck, ccv = ctx
        ang_r, ang_c = axial_angles(s)
        oa = windowed_attention(axial_rope(aq, ang_r, ang_c), axial_rope(ak, ang_r, ang_c), av, cak, cav, sink)
        oc = block_attention(axial_rope(cq, ang_r, ang_c),
                             jnp.concatenate([axial_rope(ck, ang_r, ang_c), cck], axis=1),
                             jnp.concatenate([cv, ccv], axis=1), None)
        new = None
    gates = jax.nn.sigmoid(gl.astype(jnp.float32)).astype(x.dtype).reshape(b, s, N_BRANCH, D_MODEL)
    merged = (gates[:, :, 0] * (oa.reshape(b, s, A_Q) @ P['w_a_o'][l])
              + gates[:, :, 1] * (ob @ P['w_b_o'][l])
              + gates[:, :, 2] * (oc.reshape(b, s, C_Q) @ P['w_c_o'][l]))
    x = x + g1 * (merged @ P['w_out'][l])
    h2 = rmsnorm(x, P['norm2_g'][l]) * (1 + sc2) + sh2
    x = x + g2 * expert_choice_moe(h2, P['w_router'][l], P['b_router'][l], P['w_gate'][l], P['w_up'][l], P['w_down'][l])
    return x, new

def setup_inputs(seed: int = 0) -> dict:
    key = jax.random.key(seed)
    ks = iter(jax.random.split(key, 40))

    def nrm(shape, scale=1.0):
        return jax.random.normal(next(ks), shape, jnp.float32) * scale

    def gain(shape):
        return 1.0 + nrm(shape, 0.02)

    D, E, F = D_MODEL, N_EXPERTS, EXPERT_FF
    return {
        'x_prompt': nrm((BATCH, SEQ, D)),
        'x_sample': nrm((DEC_BATCH, DEC_SEQ, D)),
        'cache_a_k': nrm((DEC_BATCH, DEPTH, PAST_LEN, A_KV, HEAD_DIM)),
        'cache_a_v': nrm((DEC_BATCH, DEPTH, PAST_LEN, A_KV, HEAD_DIM)),
        'cache_c_k': nrm((DEC_BATCH, DEPTH, PAST_LEN, C_KV, HEAD_DIM)),
        'cache_c_v': nrm((DEC_BATCH, DEPTH, PAST_LEN, C_KV, HEAD_DIM)),
        'c': nrm((DEC_BATCH, D)),
        'c_ctx': nrm((D,)),
        'norm1_g': gain((DEPTH, D)),
        'w_mod': nrm((DEPTH, D, 6 * D), 0.5 * D ** -0.5),
        'b_mod': nrm((DEPTH, 6 * D), 0.01),
        'w_in': nrm((DEPTH, D, IN_WIDTH), D ** -0.5),
        'a_q_norm': gain((DEPTH, HEAD_DIM)),
        'a_k_norm': gain((DEPTH, HEAD_DIM)),
        'a_sink': nrm((DEPTH, A_HEADS), 0.5),
        'b_v_norm': gain((DEPTH, B_WIDTH)),
        'b_ws': nrm((DEPTH, B_GROUPS, CHUNK, CHUNK), CHUNK ** -0.5),
        'b_bs': gain((DEPTH, B_GROUPS, CHUNK)),
        'c_q_norm': gain((DEPTH, HEAD_DIM)),
        'c_k_norm': gain((DEPTH, HEAD_DIM)),
        'w_a_o': nrm((DEPTH, A_Q, D), A_Q ** -0.5),
        'w_b_o': nrm((DEPTH, B_WIDTH, D), B_WIDTH ** -0.5),
        'w_c_o': nrm((DEPTH, C_Q, D), C_Q ** -0.5),
        'w_out': nrm((DEPTH, D, D), D ** -0.5),
        'norm2_g': gain((DEPTH, D)),
        'w_router': nrm((DEPTH, D, E), D ** -0.5),
        'b_router': nrm((DEPTH, E), 0.01),
        'w_gate': nrm((DEPTH, E, D, F), D ** -0.5),
        'w_up': nrm((DEPTH, E, D, F), D ** -0.5),
        'w_down': nrm((DEPTH, E, F, D), F ** -0.5),
    }

def reference(x_prompt, x_sample, cache_a_k, cache_a_v, cache_c_k, cache_c_v, c, c_ctx,
              norm1_g, w_mod, b_mod, w_in, a_q_norm, a_k_norm, a_sink, b_v_norm, b_ws, b_bs,
              c_q_norm, c_k_norm, w_a_o, w_b_o, w_c_o, w_out, norm2_g, w_router, b_router,
              w_gate, w_up, w_down):
    P = dict(norm1_g=norm1_g, w_mod=w_mod, b_mod=b_mod, w_in=w_in, a_q_norm=a_q_norm, a_k_norm=a_k_norm,
             a_sink=a_sink, b_v_norm=b_v_norm, b_ws=b_ws, b_bs=b_bs, c_q_norm=c_q_norm, c_k_norm=c_k_norm,
             w_a_o=w_a_o, w_b_o=w_b_o, w_c_o=w_c_o, w_out=w_out, norm2_g=norm2_g, w_router=w_router,
             b_router=b_router, w_gate=w_gate, w_up=w_up, w_down=w_down)
    y_prompt = x_prompt
    a_ks, a_vs, c_ks, c_vs = [], [], [], []
    for l in range(DEPTH):
        y_prompt, (ak, av, ck, cv) = trunk_layer(y_prompt, c_ctx[None, :], P, l, None)
        a_ks.append(ak)
        a_vs.append(av)
        c_ks.append(ck)
        c_vs.append(cv)
    y_sample = x_sample
    for l in range(DEPTH):
        y_sample, _ = trunk_layer(y_sample, c, P, l,
                                  (cache_a_k[:, l], cache_a_v[:, l], cache_c_k[:, l], cache_c_v[:, l]))
    new_a_k = jnp.stack(a_ks, axis=1)
    new_a_v = jnp.stack(a_vs, axis=1)
    new_c_k = jnp.stack(c_ks, axis=1)
    new_c_v = jnp.stack(c_vs, axis=1)
    return (y_prompt, y_sample, new_a_k, new_a_v, new_c_k, new_c_v)


_drawn_inputs = setup_inputs


def setup_inputs(seed=0):
    import zlib

    import numpy as np

    out = dict(_drawn_inputs(seed))
    spreads = {}
    factors = {'cache_a_k': 5.161,
     'cache_a_v': 4.39,
     'cache_c_k': 7.808,
     'cache_c_v': 7.114,
     'norm1_g': 2.931,
     'b_mod': 3.751,
     'a_q_norm': 8.0,
     'a_k_norm': 2.729,
     'a_sink': 8.0,
     'b_v_norm': 8.0,
     'b_bs': 8.0,
     'c_q_norm': 8.0,
     'c_k_norm': 2.906,
     'norm2_g': 6.106,
     'b_router': 8.0}
    for name, (base, spread) in spreads.items():
        noise = np.random.default_rng([zlib.crc32(name.encode()), seed]).standard_normal(out[name].shape)
        drawn = base * np.exp(spread * noise) if base else spread * noise
        out[name] = jnp.asarray(drawn.astype(out[name].dtype))
    for name, factor in factors.items():
        out[name] = (out[name] * factor).astype(out[name].dtype)
    return out
```

```python
from contextlib import ExitStack

import concourse.bass as bass
from concourse import mybir

D = 1024
KB = D // 128
NS = 4
NT = NS + 1
DEPTH = 2
HD = 64
QKV = 1792
AQ, AK, AV, BU, BV, CQ, CK, CV = 0, 384, 512, 640, 896, 1152, 1536, 1664
NQC, QW = 4, QKV // 4
NMOD = 6 * D // 512
NGC = 6
E = 16
PAIRS = E // 2
CS, CP = 64, 16
FFC = 6
RING = 3
C_QKV = NMOD
C_GATE = C_QKV + NQC
C_OUT = C_GATE + NGC
C_WO = C_OUT + 2
C_ROUT = C_WO + 2
C_MOE = C_ROUT + 1
CHUNKS = C_MOE + E * FFC
assert CHUNKS % RING == 0 and FFC % RING == 0 and C_MOE % RING == 0
LOADS = CHUNKS // RING

G_QKV = NMOD
G_GATE = G_QKV + NQC * NT
G_WO = G_GATE + NGC * NT
GROUPS = G_WO + 2 * NT
T_MOD, T_WS, T_CK, T_QK = 0, 1, 2, 3
T_MLP = T_QK + 2 * NT
T_O = T_MLP + NT
TQ = T_O + 2 * NT
H_M = 2 * NT
H_2 = 4 * NT
HQ = 6 * NT
UNITS = NT * 12
EPS = 1e-6
SCALE = HD ** -0.5

PRE = 8
HALVES = 2 * (NGC * NT - PRE)


def halves_until(i):
    return (i + 1) * HALVES // (UNITS + 2)


def unit(u):
    t, r = divmod(u, 12)
    br, h = divmod(r, 6)
    kv, g = divmod(h, 3)
    if t == NS:
        blocks = [NS]
    elif br == 0:
        blocks = [b for b in (t - 1, t, t + 1) if 0 <= b < NS] + [NT]
    else:
        blocks = list(range(NS)) + [NT]
    return t, br, kv, g, blocks


def build(nc, A, outs, scratch):
    f32 = mybir.dt.float32
    u32 = mybir.dt.uint32
    ALU = mybir.AluOpType
    ACT = mybir.ActivationFunctionType
    AX = mybir.AxisListType
    y_prompt, y_sample, new_a_k, new_a_v, new_c_k, new_c_v = outs
    xs_d, xn_d, g_d = scratch

    ctx = ExitStack()
    with ctx:
        def sb(name, shape, dt=f32):
            return ctx.enter_context(nc.sbuf_tensor(name, shape, dt))

        def sem(name):
            return ctx.enter_context(nc.semaphore(name))

        ring = sb("ring", [128, RING, KB, 512])
        XG = sb("XG", [128, NT * NGC * 512])
        HT = sb("HT", [128, KB, NT * 128])
        Y = sb("Y", [128, NT * QKV])
        QK = sb("QK", [128, 8 * 640 + 2 * 768])
        EP = sb("EP", [128, 3 * 640])

        x = XG[:, 0:NT * D].rearrange("p (t d) -> p t d", t=NT)
        gates = XG[:, :].rearrange("p (t c n) -> p t c n", t=NT, c=NGC)
        bmod = XG[0:2, NT * D:NT * D + 6 * D]
        nrow = XG[0:2, NT * D + 6 * D:NT * D + 8 * D].rearrange("p (a d) -> p a d", a=2)
        modrow = Y[0:2, 0:6 * D]
        xn = Y[:, 6144:8192].rearrange("p (b d) -> p b d", b=2)
        y = Y[:, :].rearrange("p (t c) -> p t c", t=NT)
        merged = Y[:, 0:NT * D].rearrange("p (t d) -> p t d", t=NT)
        qoT = QK[:, 0:8 * 640].rearrange("p (s n) -> p s n", s=8)
        kT = QK[:, 8 * 640:8 * 640 + 2 * 768].rearrange("p (b n) -> p b n", b=2)
        g1bc = QK[:, 0:2 * D].rearrange("p (s d) -> p s d", s=2)
        prob = EP[:, 0:640]
        probT = EP[:, 640:1920].rearrange("p (b n) -> p b n", b=2)
        qpair = EP[:, 512:1280].rearrange("p (b n) -> p b n", b=2)
        tmp = [EP[:, 512 * i:512 * i + 512] for i in range(3)]
        xg = Y[:, 0:2 * D].rearrange("p (b d) -> p b d", b=2)
        xgT = Y[:, 2048:4096].rearrange("p (b k n) -> p b k n", b=2, k=KB)
        hh = Y[:, 4096:5120]
        sil = Y[:, 5120:6144].rearrange("p (b n) -> p b n", b=2)
        hhT = Y[:, 6144:7168].rearrange("p (k n) -> p k n", k=KB)
        osam = Y[:, 7168:8192]
        hotp = Y[:, 8192:8320]
        affT = Y[0:E, 8320:8960]
        opro = QK[:, 2048:3072]
        hots = QK[:, 3072:3584]
        iota = QK[:, 3584:4096]
        g2bc = QK[:, 4096:6144].rearrange("p (b d) -> p b d", b=2)
        aff = EP[:, 0:NT * E].rearrange("p (t e) -> p t e", t=NT)
        slots = EP[0:E, 128:640].rearrange("p (a n) -> p a n", a=4)
        topv = EP[0:E, 640:704]
        slotT = EP[:, 768:832].rearrange("p (a e) -> p a e", a=4)
        rmax = EP[:, 832:837]
        rsum = EP[:, 840:845]
        rrec = EP[:, 848:853]

        ident = sb("ident", [128, 128])
        mask = sb("mask", [128, 2, 128])
        rope = sb("rope", [128, 2, NT, HD])
        gain = sb("gain", [128, 2, 2, HD])
        vgain = sb("vgain", [128, 256])
        wsT = sb("wsT", [128, 4, 128])
        cacheV = sb("cacheV", [128, 2, 128])
        condT = sb("condT", [128, 2 * KB])
        modcol = sb("modcol", [128, 4, KB, 2])
        bs = sb("bs", [128, 4])
        sink = sb("sink", [128, 6])
        nsink = sb("nsink", [128, 6])
        brt = sb("brt", [128, E])
        topi = sb("topi", [E, CS], u32)
        idxs = sb("idxs", [128, E], u32)
        idxp = sb("idxp", [128, E], u32)
        cols = sb("cols", [128, PAIRS])
        colp = sb("colp", [128, PAIRS])
        colv = sb("colv", [128, E])
        st5 = sb("st5", [128, NT])
        rs5 = sb("rs5", [128, NT])
        st100 = sb("st100", [128, NT, 20])
        rs100 = sb("rs100", [128, NT, 20])
        mx = sb("mx", [128, 1])
        nm = sb("nm", [128, 2])
        sm = sb("sm", [128, 2])
        es = sb("es", [128, 2])
        den = sb("den", [128, 1])
        rden = sb("rden", [128, 2])
        wsraw = EP[:, 0:512].rearrange("p (g q) -> p g q", g=4)
        ckraw = EP[:, 512:768].rearrange("p (b q) -> p b q", b=2)
        condrow = EP[0:16, 1024:1152]

        ps = ctx.enter_context(nc.psum_tensor("ps", [128, 8, 512], f32))

        ring_ready = [sem(f"ring_ready{s}") for s in range(RING)]
        ring_free = sem("ring_free")
        in_ready = sem("in_ready")
        const_ready = sem("const_ready")
        par_ready = sem("par_ready")
        PARS = 14
        x_saved = sem("x_saved")
        x_back = sem("x_back")
        g_saved = sem("g_saved")
        g1_ready = sem("g1_ready")
        g2_ready = sem("g2_ready")
        kv_saved = sem("kv_saved")
        xn_saved = [sem(f"xn_saved{b}") for b in range(2)]
        out_saved = sem("out_saved")
        cond_silu = sem("cond_silu")
        cond_done = sem("cond_done")
        cond_ready = sem("cond_ready")
        g_done = sem("g_done")
        g_free = [sem(f"g_free{b}") for b in range(2)]
        tq_done = sem("tq_done")
        tq_free = sem("tq_free")
        hq_done = sem("hq_done")
        hq_free = [sem(f"hq_free{b}") for b in range(2)]
        ss_ready = sem("ss_ready")
        ms_ready = sem("ms_ready")
        sd_ready = sem("sd_ready")
        xn_ready = sem("xn_ready")
        mod_ready = sem("mod_ready")
        gelu_ready = sem("gelu_ready")
        qk_ready = sem("qk_ready")
        v_ready = sem("v_ready")
        s_done = sem("s_done")
        nm_ready = sem("nm_ready")
        e_ready = sem("e_ready")
        es_ready = sem("es_ready")
        pt_done = sem("pt_done")
        pt_evac = sem("pt_evac")
        pv_done = sem("pv_done")
        o_evac = sem("o_evac")
        opj_done = sem("opj_done")
        opj_free = sem("opj_free")
        merged_ready = sem("merged_ready")
        x_ready = sem("x_ready")
        rt_done = sem("rt_done")
        lg_ready = sem("lg_ready")
        pe_ready = sem("pe_ready")
        aff_ready = sem("aff_ready")
        afft_done = sem("afft_done")
        slots_ready = sem("slots_ready")
        slott_done = sem("slott_done")
        idx_ready = sem("idx_ready")
        hot_ready = sem("hot_ready")
        moe_init = sem("moe_init")
        xg_ready = [sem(f"xg_ready{b}") for b in range(2)]
        xt_done = sem("xt_done")
        mq_done = sem("mq_done")
        mq_free = [sem(f"mq_free{b}") for b in range(2)]
        gu_done = sem("gu_done")
        sil_ready = sem("sil_ready")
        hh_ready = sem("hh_ready")
        dn_done = sem("dn_done")
        out_evac = [sem(f"out_evac{b}") for b in range(2)]
        sc_done = sem("sc_done")
        sc_free = [sem(f"sc_free{b}") for b in range(2)]
        act_step = sem("act_step")
        dve_step = sem("dve_step")
        pool_step = sem("pool_step")
        waited = [sem(f"waited{i}") for i in range(3)]

        def settle(engine, i):
            engine.sem_inc(waited[i], 1)

        ACT_STEPS = 10
        DVE_STEPS = (4
                     + NT * (6 + 12 + 1) + 1
                     + UNITS * 2 + UNITS // 2
                     + 2 * NT * 3
                     + 4 + 3
                     + 3 * (CS + CP) // 8 - 2 + 4 + 3)

        def chunk_src(l, c, e=None):
            if e is not None:
                w = (A["w_gate"], A["w_up"], A["w_gate"], A["w_up"], A["w_down"], A["w_down"])[c]
                n = (0, 0, 1, 1, 0, 1)[c]
                return w[l, e].rearrange("(k p) n -> p k n", p=128)[:, :, 512 * n:512 * n + 512]
            if c < C_QKV:
                w, lo, n = A["w_mod"], 512 * c, 512
            elif c < C_GATE:
                w, lo, n = A["w_in"], QW * (c - C_QKV), QW
            elif c < C_OUT:
                half, br = divmod(c - C_GATE, 3)
                w, lo, n = A["w_in"], QKV + D * br + 512 * half, 512
            elif c < C_WO:
                w, lo, n = A["w_o"], 512 * (c - C_OUT), 512
            elif c < C_ROUT:
                w, lo, n = A["w_out"], 512 * (c - C_WO), 512
            else:
                w, lo, n = A["w_router"], 0, E
            return w[l].rearrange("(k p) n -> p k n", p=128)[:, :, lo:lo + n]

        block = ctx.enter_context(nc.Block())

        @block.sync
        def _(sp):
            sp.dma_start(x[:, 0:NS], A["x_sample"][0].rearrange("(t p) d -> p t d", p=128)).then_inc(in_ready, 16)
            sp.dma_start(x[:, NS], A["x_prompt"][0]).then_inc(in_ready, 16)
            sp.dma_start(condrow[0:KB], A["c"][0].rearrange("(k p) -> k p", p=128)).then_inc(in_ready, 16)
            sp.dma_start(condrow[KB:2 * KB], A["c_ctx"].rearrange("(k p) -> k p", p=128)).then_inc(in_ready, 16)
            sp.dma_start(rope[:, :, :, :], A["rope"]).then_inc(in_ready, 16)
            with sp.Fori(0, DEPTH) as l:
                for c in range(C_MOE):
                    src = chunk_src(l, c)
                    sp.wait_ge(ring_free, l * CHUNKS + c + 1)
                    sp.dma_start(ring[:, c % RING, :, 0:src.shape[2]], src).then_inc(ring_ready[c % RING], 16)
                with sp.Fori(0, E) as e:
                    for c in range(FFC):
                        sp.wait_ge(ring_free, l * CHUNKS + e * FFC + (C_MOE + c + 1))
                        sp.dma_start(ring[:, c % RING], chunk_src(l, c, e)).then_inc(ring_ready[c % RING], 16)
            sp.wait_ge(sc_free[0], DEPTH * 5 * PAIRS + 1)
            sp.wait_ge(sc_free[1], DEPTH * 5 * PAIRS + 1)
            sp.dma_start(y_sample[0].rearrange("(t p) d -> p t d", p=128), x[:, 0:NS]).then_inc(out_saved, 16)
            sp.dma_start(y_prompt[0], x[:, NS]).then_inc(out_saved, 16)
            sp.wait_ge(out_saved, 32)

        @block.gpsimd
        def _(pool):
            pool.memset(ident[:, :], 0.0).then_inc(pool_step, 1)
            pool.memset(mask[:, :, :], 0.0).then_inc(pool_step, 1)
            pool.wait_ge(pool_step, 2)
            pool.affine_select(out=ident[:, :], in_=ident[:, :], compare_op=ALU.not_equal, fill=1.0, base=0,
                               pattern=[[-1, 128]], channel_multiplier=1).then_inc(const_ready, 1)
            pool.affine_select(out=mask[:, 0], in_=mask[:, 0], compare_op=ALU.is_ge, fill=-1.0e30, base=0,
                               pattern=[[1, 128]], channel_multiplier=-1).then_inc(const_ready, 1)
            pool.affine_select(out=mask[:, 1], in_=mask[:, 1], compare_op=ALU.is_ge, fill=-1.0e30, base=0,
                               pattern=[[-1, 128]], channel_multiplier=1).then_inc(const_ready, 1)
            pool.sem_inc(xt_done, 2)
            pool.wait_ge(in_ready, 80)
            pool.wait_ge(cond_ready, 1)
            with pool.Fori(0, DEPTH) as l:
                pool.dma_start(xs_d.rearrange("(t p) d -> p t d", p=128), x).then_inc(x_saved, 16)

                def par(dst, src):
                    pool.dma_start(dst, src).then_inc(par_ready, 16)

                for s in range(2):
                    par(bmod[s:s + 1], A["b_mod"][bass.ds(l, 1)])
                    par(nrow[s:s + 1, 0], A["norm1_g"][bass.ds(l, 1)])
                    par(nrow[s:s + 1, 1], A["norm2_g"][bass.ds(l, 1)])
                par(wsraw, A["b_ws"][l].rearrange("g p q -> p g q"))
                par(gain.rearrange("p a b d -> p (a b d)"), A["qk_gain"][bass.ds(l, 1)].to_broadcast([128, 256]))
                par(vgain[:, :], A["b_v_norm"][bass.ds(l, 1)].to_broadcast([128, 256]))
                par(sink[:, :], A["a_sink"][bass.ds(l, 1)].to_broadcast([128, 6]))
                par(brt[:, :], A["b_router"][bass.ds(l, 1)].to_broadcast([128, E]))
                par(bs[:, :], A["b_bs"][l])
                par(cacheV[:, :, :], A["cache_v"][l])
                par(ckraw, A["cache_k"][l])
                pool.wait_ge(mod_ready, l + 1)
                settle(pool, 2)
                pool.dma_start(g_d[:, 0, :], modrow[:, 2 * D:3 * D]).then_inc(g_saved, 16)
                pool.dma_start(g_d[:, 1, :], modrow[:, 5 * D:6 * D]).then_inc(g_saved, 16)
                pool.wait_ge(qk_ready, l * 2 * NT + 2 * NT)
                settle(pool, 2)
                for dst, c in ((new_a_k, AK), (new_a_v, AV), (new_c_k, CK), (new_c_v, CV)):
                    pool.dma_start(dst[0, l].rearrange("s k d -> s (k d)"), y[:, NS, c:c + 128]).then_inc(kv_saved, 16)
                pool.wait_ge(opj_free, l * 2 * NT + 2 * NT + 2)
                settle(pool, 2)
                pool.dma_start(x, xs_d.rearrange("(t p) d -> p t d", p=128)).then_inc(x_back, 16)
                pool.wait_ge(g_saved, l * 32 + 32)
                settle(pool, 2)
                for s in range(2):
                    pool.dma_start(g1bc[:, s], g_d[s, 0:1, :].to_broadcast([128, D])).then_inc(g1_ready, 16)
                for s in range(2):
                    for h in range(2):
                        pool.dma_start(g2bc[64 * h:64 * h + 64, (s + h) % 2],
                                       g_d[s, 1:2, :].to_broadcast([64, D])).then_inc(g2_ready, 16)
                for t in range(NT):
                    pool.wait_ge(xn_ready, l * 2 * NT + NT + t + 1)
                    settle(pool, 2)
                    pool.dma_start(xn_d[128 * t:128 * t + 128, :], xn[:, t % 2]).then_inc(xn_saved[t % 2], 16)
                for b, n in ((0, NT - NT // 2), (1, NT // 2)):
                    pool.wait_ge(xn_saved[b], l * (16 * n) + 16 * n)
                pool.wait_ge(hq_free[0], l * 3 * NT + 3 * NT + 1)
                pool.wait_ge(hq_free[1], l * 3 * NT + 3 * NT + 1)
                settle(pool, 2)
                pool.iota(iota, pattern=[[1, 512]], base=0, channel_multiplier=0,
                          allow_small_or_imprecise_dtypes=True).then_inc(moe_init, 1)
                pool.memset(xg, 0.0).then_inc(moe_init, 1)
                pool.wait_ge(moe_init, l * 2 + 2)
                pool.wait_ge(idx_ready, l + 1)
                settle(pool, 2)

                def gather(j, b):
                    e = 2 * j + b
                    lat, pro = (0, 64) if b == 0 else (64, 0)
                    pool.wait_ge(xt_done, l * E + 2 * j + (b + 1))
                    settle(pool, 2)
                    pool.indirect_dma_start(xg[lat:lat + CS, b], None, xn_d,
                                            bass.IndirectOffsetOnAxis(ap=idxs[0:CS, bass.ds(e, 1)], axis=0)
                                            ).then_inc(xg_ready[b], 16)
                    pool.indirect_dma_start(xg[pro:pro + CP, b], None, xn_d,
                                            bass.IndirectOffsetOnAxis(ap=idxp[0:CP, bass.ds(e, 1)], axis=0)
                                            ).then_inc(xg_ready[b], 16)

                for j in range(PAIRS):
                    gather(j, 0)
                    gather(j, 1)
                pool.wait_ge(sc_free[0], l * 5 * PAIRS + 5 * PAIRS + 1)
                pool.wait_ge(sc_free[1], l * 5 * PAIRS + 5 * PAIRS + 1)
            pool.wait_ge(kv_saved, DEPTH * 64)
            pool.wait_ge(x_saved, DEPTH * 16)

        @block.tensor
        def _(pe):
            pe.sem_inc(ring_free, RING)
            pe.sem_inc(pt_done, 1)
            pe.sem_inc(pv_done, 2)
            pe.wait_ge(const_ready, 3)
            pe.wait_ge(cond_silu, 1)
            nc.tensor.transpose(ps[:, 7, 0:16], condrow, ident[0:16, 0:16]).then_inc(cond_done, 1)
            pe.wait_ge(cond_ready, 1)

            def transposes(bank, srcs, done):
                for i, s in enumerate(srcs):
                    last = nc.tensor.transpose(ps[:, bank, 128 * i:128 * i + 128], s, ident[:, :])
                last.then_inc(done, 1)

            with pe.Fori(0, DEPTH) as l:
                def arrived(c):
                    pe.wait_ge(ring_ready[c % RING], l * (16 * LOADS) + 16 * (c // RING + 1))

                def group(g, lhs, c, n, k0=0, k1=KB, release=False):
                    if k0 == 0:
                        pe.wait_ge(g_free[g % 2], l * (GROUPS // 2) + g // 2 + 1)
                    for k in range(k0, k1):
                        last = nc.tensor.matmul(ps[:, g % 2, 0:n] if lhs(k).shape[1] == 128 else ps[0:2, g % 2, 0:n],
                                                lhs(k), ring[:, c % RING, k, 0:n], start=k == 0, stop=k == KB - 1)
                    return last

                def tile(t):
                    return lambda k: HT[:, k, 128 * t:128 * t + 128]

                for c in range(NMOD):
                    arrived(c)
                    group(c, lambda k: condT.rearrange("p (s k) -> p k s", s=2)[:, k], c, 512).then_inc(g_done, 1)
                    pe.wait_ge(g_done, l * GROUPS + c + 1)
                    pe.sem_inc(ring_free, 1)
                pe.wait_ge(mod_ready, l + 1)
                pe.wait_ge(tq_free, l * TQ + T_MOD + 1)
                settle(pe, 1)
                for i, lo in enumerate((0, D, 3 * D, 4 * D)):
                    for k in range(KB):
                        last = nc.tensor.transpose(ps[:, 7, 2 * (KB * i + k):2 * (KB * i + k) + 2],
                                                   modrow[:, lo + 128 * k:lo + 128 * k + 128], ident[0:2, 0:2])
                last.then_inc(tq_done, 1)

                def h_tiles(first, src, ready, per, half_of=None):
                    for t in range(NT):
                        ready(t)
                        for h in range(2):
                            pe.wait_ge(hq_free[h], l * (HQ // 2) + (first // 2 + t) + 1)
                            transposes(2 + h, [src(t)[:, 128 * k:128 * k + 128] for k in range(4 * h, 4 * h + 4)],
                                       hq_done)

                h_tiles(0, lambda t: xn[:, t % 2], lambda t: pe.wait_ge(xn_ready, l * 2 * NT + t + 1), None)

                pe.wait_ge(par_ready, l * 16 * PARS + 16 * PARS)
                pe.wait_ge(tq_free, l * TQ + T_WS + 1)
                transposes(7, [wsraw[:, g] for g in range(4)], tq_done)
                pe.wait_ge(tq_free, l * TQ + T_CK + 1)
                transposes(7, [ckraw[:, b] for b in range(2)], tq_done)

                for c in range(NQC):
                    arrived(C_QKV + c)
                    for t in range(NT):
                        if c == 0:
                            for h in range(2):
                                pe.wait_ge(hq_free[h], l * (HQ // 2) + t + 2)
                        g = G_QKV + c * NT + t
                        group(g, tile(t), C_QKV + c, QW).then_inc(g_done, 1)
                    pe.wait_ge(g_done, l * GROUPS + g + 1)
                    pe.sem_inc(ring_free, 1)

                def gate_half(i):
                    q, h = divmod(i, 2)
                    c, t = divmod(q, NT)
                    if t == 0 and h == 0:
                        arrived(C_GATE + c)
                    last = group(G_GATE + q, tile(t), C_GATE + c, 512, 4 * h, 4 * h + 4)
                    if h:
                        last.then_inc(g_done, 1)
                        if t == NT - 1:
                            pe.wait_ge(g_done, l * GROUPS + G_GATE + q + 1)
                            pe.sem_inc(ring_free, 1)

                def gate(q):
                    gate_half(2 * q)
                    gate_half(2 * q + 1)

                gate(0)
                gate(1)
                for i in range(2 * NT):
                    t, br = divmod(i, 2)
                    kbase = (AK, CK)[br]
                    pe.wait_ge(qk_ready, l * 2 * NT + i + 1)
                    pe.wait_ge(tq_free, l * TQ + T_QK + i + 1)
                    transposes(7, [qpair[:, br, 128 * g:128 * g + 128] for g in range(3)] + [y[:, t, kbase:kbase + 128]],
                               tq_done)
                    if i % 2:
                        gate(2 + i // 2)
                gate(PRE - 1)
                for t in range(NT):
                    pe.wait_ge(v_ready, l * NT + t + 1)
                    pe.wait_ge(tq_free, l * TQ + T_MLP + t + 1)
                    for g in range(4):
                        last = nc.tensor.matmul(ps[:, 7, 64 * g:64 * g + 64], wsT[:, g],
                                                y[:, t, BV + 64 * g:BV + 64 * g + 64], start=True, stop=True)
                    last.then_inc(tq_done, 1)

                def scores(u):
                    t, br, kv, g, blocks = unit(u)
                    pe.wait_ge(e_ready, l * UNITS + u + 1)
                    r = slice(64 * kv, 64 * kv + 64)
                    q = qoT[r, 3 * br + g, 128 * t:128 * t + 128]
                    for i, b in enumerate(blocks):
                        last = nc.tensor.matmul(ps[:, 2 + i // 4, 128 * (i % 4):128 * (i % 4) + 128], q,
                                                kT[r, br, 128 * b:128 * b + 128], start=i % 4 == 0, stop=True,
                                                skip_group_check=True)
                        if br == 0 and t < NS and b in (t - 1, t + 1):
                            last = nc.tensor.matmul(ps[:, 2, 128 * i:128 * i + 128], ident[:, :],
                                                    mask[:, 0 if b < t else 1], start=False, stop=True,
                                                    skip_group_check=True)
                    last.then_inc(s_done, 1)

                def turn(u):
                    blocks = unit(u)[4]
                    pe.wait_ge(e_ready, l * UNITS + u + 2)
                    pe.wait_ge(pt_evac, l * UNITS + u + 1)
                    for i in range(len(blocks)):
                        last = nc.tensor.transpose(ps[:, 4 + i // 4, 128 * (i % 4):128 * (i % 4) + 128],
                                                   prob[:, 128 * i:128 * i + 128], ident[:, :])
                    last.then_inc(pt_done, 1)

                def weigh(u):
                    t, br, kv, g, blocks = unit(u)
                    pe.wait_ge(pt_evac, l * UNITS + u + 2)
                    pe.wait_ge(o_evac, l * UNITS + u + 1)
                    for i, b in enumerate(blocks):
                        v = cacheV[:, br, 64 * kv:64 * kv + 64] if b == NT else \
                            y[:, b, (AV, CV)[br] + 64 * kv:(AV, CV)[br] + 64 * kv + 64]
                        last = nc.tensor.matmul(ps[:, 6, 0:64], probT[:, u % 2, 128 * i:128 * i + 128], v,
                                                start=i == 0, stop=i == len(blocks) - 1)
                    last.then_inc(pv_done, 1)

                pe.wait_ge(tq_free, l * TQ + T_MLP + 1)
                for i in range(UNITS + 2):
                    if i < UNITS:
                        scores(i)
                    if 1 <= i <= UNITS:
                        turn(i - 1)
                    if i >= 2:
                        weigh(i - 2)
                    for n in range(halves_until(i - 1), halves_until(i)):
                        gate_half(2 * PRE + n)
                pe.wait_ge(o_evac, l * UNITS + UNITS + 1)
                for t in range(NT):
                    parts = [y[:, t, AQ + 128 * i:AQ + 128 * i + 128] for i in range(3)] + \
                            [y[:, t, CQ + 128 * i:CQ + 128 * i + 128] for i in range(3)] + \
                            [y[:, t, BU + 128 * i:BU + 128 * i + 128] for i in range(2)]
                    for h in range(2):
                        pe.wait_ge(tq_free, l * TQ + T_O + 2 * t + h + 1)
                        transposes(7, parts[4 * h:4 * h + 4], tq_done)
                pe.wait_ge(tq_free, l * TQ + TQ + 1)
                pe.wait_ge(pt_evac, l * UNITS + UNITS + 1)
                for n in range(2):
                    arrived(C_OUT + n)
                    for t in range(NT):
                        o = n * NT + t
                        pe.wait_ge(opj_free, l * 2 * NT + o + 1)
                        for b, ks in enumerate(((0, 1, 2), (6, 7), (3, 4, 5))):
                            for k in ks:
                                last = nc.tensor.matmul(ps[:, 2 + 3 * (o % 2) + b], qoT[:, k, 128 * t:128 * t + 128],
                                                        ring[:, (C_OUT + n) % RING, k], start=k == ks[0], stop=k == ks[-1])
                        last.then_inc(opj_done, 1)
                    pe.wait_ge(opj_done, l * 2 * NT + o + 1)
                    pe.sem_inc(ring_free, 1)
                pe.wait_ge(merged_ready, l * 2 * NT + 2 * NT)
                h_tiles(H_M, lambda t: merged[:, t], lambda t: None, None)
                for c in range(2):
                    arrived(C_WO + c)
                    for t in range(NT):
                        if c == 0:
                            for h in range(2):
                                pe.wait_ge(hq_free[h], l * (HQ // 2) + NT + t + 2)
                        g = G_WO + c * NT + t
                        group(g, tile(t), C_WO + c, 512).then_inc(g_done, 1)
                    pe.wait_ge(g_done, l * GROUPS + g + 1)
                    pe.sem_inc(ring_free, 1)
                h_tiles(H_2, lambda t: xn[:, t % 2], lambda t: pe.wait_ge(xn_ready, l * 2 * NT + NT + t + 1), None)
                for h in range(2):
                    pe.wait_ge(hq_free[h], l * (HQ // 2) + 3 * NT + 1)
                arrived(C_ROUT)
                for t in range(NT):
                    for k in range(KB):
                        last = nc.tensor.matmul(ps[:, 6, E * t:E * t + E], HT[:, k, 128 * t:128 * t + 128],
                                                ring[:, C_ROUT % RING, k, 0:E], start=k == 0, stop=k == KB - 1)
                last.then_inc(rt_done, 1)
                pe.wait_ge(rt_done, l + 1)
                pe.sem_inc(ring_free, 1)
                pe.wait_ge(aff_ready, l + 1)
                for t in range(NT):
                    last = nc.tensor.transpose(ps[0:E, 7 if t < NS else 6, 128 * (t % NS):128 * (t % NS) + 128],
                                               aff[:, t], ident[:, :])
                last.then_inc(afft_done, 1)
                pe.wait_ge(slots_ready, l + 1)
                settle(pe, 1)
                for a in range(4):
                    last = nc.tensor.transpose(ps[:, 7, E * a:E * a + E], slots[:, a], ident[0:E, 0:E])
                last.then_inc(slott_done, 1)

                def turn_rows(j, b, idx):
                    pe.wait_ge(xg_ready[b], l * (32 * PAIRS) + (j * 32 + 32))
                    for h in range(2):
                        pe.wait_ge(mq_free[h], l * 32 + (idx // 2 + 1) if isinstance(idx, int) else l * 32 + idx(h))
                        for i in range(4):
                            last = nc.tensor.transpose(ps[:, 4 + h, 128 * i:128 * i + 128],
                                                       xg[:, b, 512 * h + 128 * i:512 * h + 128 * i + 128], ident[:, :])
                        last.then_inc(mq_done, 1)
                    pe.wait_ge(mq_done, (l * 64 + (idx + 2)) if isinstance(idx, int) else l * 64 + idx(2))
                    pe.sem_inc(xt_done, 1)

                def products(j, b, c, lhs, bank, done):
                    pe.wait_ge(ring_ready[c % RING], l * (16 * LOADS) + j * 64 + 16 * ((C_MOE + FFC * b + c) // RING + 1))
                    for k in range(KB):
                        last = nc.tensor.matmul(ps[:, bank], lhs[:, k], ring[:, c % RING, k],
                                                start=k == 0, stop=k == KB - 1)
                    last.then_inc(done, 1)

                def scatter(j):
                    pe.wait_ge(hot_ready, l * PAIRS + j + 1)
                    for b in range(2):
                        pe.wait_ge(out_evac[b], l * E + (2 * j + 3))
                    for t in range(NT):
                        for h in range(2):
                            pe.wait_ge(sc_free[h], l * (5 * PAIRS) + (j * 5 + t + 1))
                            lhs, src = (hots[:, 128 * t:128 * t + 128], osam) if t < NS else (hotp, opro)
                            nc.tensor.matmul(ps[:, 6 + h], lhs, src[:, 512 * h:512 * h + 512],
                                             start=True, stop=True).then_inc(sc_done, 1)

                def pair(j, first, last_pair):
                    for b in range(2):
                        for c in range(4):
                            if c % 2 == 0:
                                pe.wait_ge(out_evac[c // 2], l * E + (2 * j + b + 1))
                            if c == 0:
                                for h in range(2):
                                    pe.wait_ge(mq_free[h], l * 32 + (4 * j + 2 * b + (2 if b == 0 and first else 1)) if b == 0 and first
                                               else l * 32 + (4 * j + 2 * b + 1))
                            products(j, b, c, xgT[:, b], c // 2 + 2 * (c % 2), gu_done)
                            pe.wait_ge(gu_done, l * 64 + (8 * j + 4 * b + c + 1))
                            pe.sem_inc(ring_free, 1)
                        if b == 0 and not first:
                            scatter(j - 1)
                        if b == 0 or not last_pair:
                            turn_rows(j + b, 1 - b, lambda h, b=b: (4 * j + 2 * b + 2) if h < 2 else (8 * j + 4 * b + 4))
                        for h in range(2):
                            skip = 1 if b and last_pair else 0
                            pe.wait_ge(hh_ready, l * 32 + (4 * j + 2 * b + h + 1))
                            pe.wait_ge(mq_free[h], l * 32 + (4 * j + 2 * b + 3 - skip))
                            transposes(4 + h, [hh[:, 512 * h + 128 * i:512 * h + 128 * i + 128] for i in range(4)], mq_done)
                        for h in range(2):
                            pe.wait_ge(mq_free[h], l * 32 + (4 * j + 2 * b + 4 - skip))
                        for h in range(2):
                            products(j, b, 4 + h, hhT, h, dn_done)
                            pe.wait_ge(dn_done, l * 32 + (4 * j + 2 * b + h + 1))
                            pe.sem_inc(ring_free, 1)

                turn_rows(0, 0, 0)
                pair(0, True, False)
                with pe.Fori(1, PAIRS - 1) as j:
                    pair(j, False, False)
                pair(PAIRS - 1, False, True)
                scatter(PAIRS - 1)

        @block.scalar
        def _(act):
            act.sem_inc(e_ready, 1)
            steps = [0]
            act.wait_ge(in_ready, 80)
            nc.scalar.activation(condrow, condrow, ACT.Silu).then_inc(cond_silu, 1)
            act.wait_ge(cond_ready, 1)
            with act.Fori(0, DEPTH) as l:
                def link(ins):
                    steps[0] += 1
                    ins.then_inc(act_step, 1)
                    act.wait_ge(act_step, l * ACT_STEPS + steps[0])

                def squares(n):
                    for t in range(NT):
                        ins = nc.scalar.activation(Y[:, 8192:8193].to_broadcast([128, D]) if False else hsq(t),
                                                   x[:, t], ACT.Square, accum_out=st5[:, t:t + 1])
                        link(ins)
                    act.sem_inc(ss_ready, 1)

                def hsq(t):
                    return HT[:, 0:2, 0:512].rearrange("p a n -> p a n")

                def root(i, out, src):
                    act.wait_ge(ms_ready, l * 3 + i + 1)
                    nc.scalar.activation(out, src, ACT.Sqrt).then_inc(sd_ready, 1)

                def h_evac(first, which):
                    for t in range(NT):
                        s = 0 if t < NS else 1
                        act.wait_ge(hq_done, l * HQ + first + 2 * t + 1)
                        for k in range(4):
                            last = nc.scalar.activation(HT[:, k, 128 * t:128 * t + 128], ps[:, 2, 128 * k:128 * k + 128],
                                                        ACT.Identity, bias=modcol[:, which, k, s:s + 1],
                                                        scale=modcol[:, which + 1, k, s:s + 1])
                        last.then_inc(hq_free[0], 1)

                act.wait_ge(sc_free[0], l * 5 * PAIRS + 1)
                act.wait_ge(sc_free[1], l * 5 * PAIRS + 1)
                squares(0)
                root(0, rs5[:, :], st5[:, :])
                act.wait_ge(tq_free, l * TQ + T_MOD + 2)
                h_evac(0, 0)
                act.wait_ge(tq_done, l * TQ + T_WS + 1)
                nc.scalar.activation(wsT.rearrange("p g n -> p (g n)"), ps[:, 7], ACT.Copy).then_inc(tq_free, 1)
                act.wait_ge(tq_done, l * TQ + T_CK + 1)
                nc.scalar.activation(kT[:, :, 640:768], ps[:, 7, 0:256].rearrange("p (b n) -> p b n", b=2),
                                     ACT.Copy).then_inc(tq_free, 1)
                for g in range(G_QKV, G_GATE):
                    c, t = divmod(g - G_QKV, NT)
                    if g % 2 == 0:
                        act.wait_ge(g_done, l * GROUPS + g + 1)
                        if g == G_QKV:
                            act.wait_ge(g_saved, l * 32 + 32)
                        nc.scalar.activation(y[:, t, QW * c:QW * c + QW], ps[:, 0, 0:QW], ACT.Copy).then_inc(g_free[0], 1)
                for b in range(2):
                    act.wait_ge(g_free[b], l * (GROUPS // 2) + G_GATE // 2 + 1)
                for t in range(NT):
                    nc.scalar.activation(y[:, t, BU:BU + 512], y[:, t, BU:BU + 512], ACT.Gelu_apprx_tanh).then_inc(gelu_ready, 1)

                def gate(q):
                    c, t = divmod(q, NT)
                    g = G_GATE + q
                    act.wait_ge(g_done, l * GROUPS + g + 1)
                    if q == 0:
                        act.wait_ge(x_saved, l * 16 + 16)
                    nc.scalar.activation(gates[:, t, c], ps[:, g % 2], ACT.Tanh, scale=0.5).then_inc(g_free[g % 2], 1)

                gate(0)
                gate(1)
                root(1, rs100[:, :, :], st100[:, :, :])
                for i in range(2 * NT):
                    t, br = divmod(i, 2)
                    act.wait_ge(tq_done, l * TQ + T_QK + i + 1)
                    nc.scalar.activation(qoT[:, 3 * br:3 * br + 3, 128 * t:128 * t + 128],
                                         ps[:, 7, 0:384].rearrange("p (s n) -> p s n", s=3), ACT.Copy)
                    nc.scalar.activation(kT[:, br, 128 * t:128 * t + 128], ps[:, 7, 384:512], ACT.Copy).then_inc(tq_free, 1)
                    if i % 2:
                        gate(2 + i // 2)
                gate(PRE - 1)
                for i in range(UNITS + 2):
                    if i < UNITS:
                        t, br, kv, g, blocks = unit(i)
                        n = 128 * len(blocks)
                        act.wait_ge(nm_ready, l * UNITS + i + 1)
                        act.wait_ge(pt_done, l * UNITS + i + 1)
                        nc.scalar.activation(prob[:, 0:n], ps[:, 2:4].rearrange("p b n -> p (b n)")[:, 0:n], ACT.Exp,
                                             bias=nm[:, i % 2:i % 2 + 1], scale=SCALE,
                                             accum_out=sm[:, i % 2:i % 2 + 1]).then_inc(e_ready, 1)
                        if br == 0:
                            h = 3 * kv + g
                            nc.scalar.activation(es[:, i % 2:i % 2 + 1], sink[:, h:h + 1], ACT.Exp,
                                                 bias=nm[:, i % 2:i % 2 + 1]).then_inc(es_ready, 1)
                    u = i - 1
                    if 0 <= u < UNITS and u % 2:
                        n = 128 * len(unit(u)[4])
                        act.wait_ge(pt_done, l * UNITS + u + 2)
                        act.wait_ge(pv_done, l * UNITS + u + 1)
                        nc.scalar.activation(probT[:, 1, 0:n], ps[:, 4:6].rearrange("p b n -> p (b n)")[:, 0:n],
                                             ACT.Copy).then_inc(pt_evac, 1)
                    for n in range(halves_until(i - 1), halves_until(i)):
                        if n % 2:
                            gate(PRE + n // 2)
                for i in range(2 * NT):
                    t, h = divmod(i, 2)
                    act.wait_ge(tq_done, l * TQ + T_O + i + 1)
                    nc.scalar.activation(qoT[:, 4 * h:4 * h + 4, 128 * t:128 * t + 128],
                                         ps[:, 7].rearrange("p (s n) -> p s n", s=4), ACT.Copy).then_inc(tq_free, 1)
                for t in range(NT):
                    act.wait_ge(hq_done, l * HQ + H_M + 2 * t + 1)
                    nc.scalar.activation(HT[:, 0:4, 128 * t:128 * t + 128], ps[:, 2].rearrange("p (s n) -> p s n", s=4),
                                         ACT.Copy, scale=0.5).then_inc(hq_free[0], 1)
                act.wait_ge(x_ready, l * 2 * NT + 2 * NT)
                squares(1)
                root(2, rs5[:, :], st5[:, :])
                h_evac(H_2, 2)
                act.wait_ge(lg_ready, l + 1)
                nc.scalar.activation(aff, aff, ACT.Exp).then_inc(pe_ready, 1)
                if steps[0] != ACT_STEPS:
                    raise ValueError(f"ACT_STEPS {steps[0]}")

                def rows_evac(b, n):
                    act.wait_ge(mq_done, n)
                    nc.scalar.activation(xgT[:, b, 0:4], ps[:, 4].rearrange("p (k n) -> p k n", k=4), ACT.Identity) \
                        if False else None

                def modulate(b, j, idx):
                    act.wait_ge(mq_done, idx)
                    for k in range(4):
                        for h in range(2):
                            s = (h + b) % 2
                            last = nc.scalar.activation(xgT[:, b, k, 64 * h:64 * h + 64],
                                                        ps[:, 4, 128 * k + 64 * h:128 * k + 64 * h + 64], ACT.Identity,
                                                        bias=modcol[:, 2, k, s:s + 1], scale=modcol[:, 3, k, s:s + 1])
                    last.then_inc(mq_free[0], 1)

                def pair(j, last_pair):
                    for b in range(2):
                        for h in range(2):
                            act.wait_ge(gu_done, l * 64 + (8 * j + 4 * b + 2 * h + 1))
                            nc.scalar.activation(sil[:, h], ps[:, h], ACT.Silu).then_inc(sil_ready, 1)
                        skip = 2 if b and last_pair else 0
                        if not skip:
                            modulate(1 - b, j, l * 64 + (8 * j + 4 * b + 3))
                        act.wait_ge(mq_done, l * 64 + (8 * j + 4 * b + 5 - skip))
                        nc.scalar.activation(hhT[:, 0:4], ps[:, 4].rearrange("p (k n) -> p k n", k=4),
                                             ACT.Copy).then_inc(mq_free[0], 1)

                modulate(0, 0, l * 64 + 1)
                with act.Fori(0, PAIRS - 1) as j:
                    pair(j, False)
                pair(PAIRS - 1, True)

        @block.vector
        def _(dve):
            for s in (g_free[0], g_free[1], tq_free, hq_free[0], hq_free[1], pt_evac, o_evac, mq_free[0], mq_free[1],
                      out_evac[0], out_evac[1]):
                dve.sem_inc(s, 1)
            dve.sem_inc(opj_free, 2)
            dve.wait_ge(in_ready, 80)
            dve.sem_inc(sc_free[0], 1)
            dve.sem_inc(sc_free[1], 1)
            dve.wait_ge(cond_done, 1)
            nc.vector.tensor_copy(condT[:, :], ps[:, 7, 0:16]).then_inc(cond_ready, 1)
            steps = [0]
            TT, TS, STT = nc.vector.tensor_tensor, nc.vector.tensor_scalar, nc.vector.scalar_tensor_tensor
            with dve.Fori(0, DEPTH) as l:
                def link(ins):
                    steps[0] += 1
                    ins.then_inc(dve_step, 1)
                    dve.wait_ge(dve_step, l * DVE_STEPS + steps[0])

                def link_top(ins):
                    link(ins)
                    settle(dve, 0)

                dve.wait_ge(par_ready, l * 16 * PARS + 16 * PARS)
                for c in range(NMOD):
                    dve.wait_ge(g_done, l * GROUPS + c + 1)
                    TT(modrow[:, 512 * c:512 * c + 512], ps[0:2, c % 2], bmod[:, 512 * c:512 * c + 512],
                       ALU.add).then_inc(g_free[c % 2], 1)
                for b in range(2):
                    dve.wait_ge(g_free[b], l * (GROUPS // 2) + NMOD // 2 + 1)
                link(STT(modrow[:, D:2 * D], modrow[:, D:2 * D], 1.0, nrow[:, 0], ALU.add, ALU.mult))
                STT(modrow[:, 4 * D:5 * D], modrow[:, 4 * D:5 * D], 1.0, nrow[:, 1], ALU.add, ALU.mult).then_inc(mod_ready, 1)
                link(TS(nsink[:, :], sink[:, :], -1.0, None, ALU.mult))
                dve.wait_ge(tq_done, l * TQ + T_MOD + 1)
                nc.vector.tensor_copy(modcol.rearrange("p a k s -> p (a k s)"), ps[:, 7, 0:64]).then_inc(tq_free, 1)

                def norm_rows(i, first, hq, saved):
                    dve.wait_ge(ss_ready, l * 2 + (i + 1))
                    TS(st5[:, :], st5[:, :], 1.0 / D, EPS, ALU.mult, ALU.add).then_inc(ms_ready, 1)
                    dve.wait_ge(sd_ready, l * 3 + (2 * i + 1))
                    link(nc.vector.reciprocal(rs5[:, :], rs5[:, :]))
                    for t in range(NT):
                        if t >= 2:
                            dve.wait_ge(hq_done, l * HQ + hq + 2 * (t - 1))
                            if saved:
                                dve.wait_ge(xn_saved[t % 2], l * (16 * ((NT + 1 - t % 2) // 2)) + 16 * (t // 2))
                        TS(xn[:, t % 2], x[:, t], rs5[:, t:t + 1], None, ALU.mult).then_inc(xn_ready, 1)
                        if t >= 1:
                            h_evac(t - 1, hq, 0 if i == 0 else 2)
                    h_evac(NT - 1, hq, 0 if i == 0 else 2)

                def h_evac(t, hq, which):
                    s = 0 if t < NS else 1
                    dve.wait_ge(hq_done, l * HQ + hq + 2 * t + 2)
                    for k in range(4):
                        last = TS(HT[:, 4 + k, 128 * t:128 * t + 128], ps[:, 3, 128 * k:128 * k + 128],
                                  modcol[:, which + 1, 4 + k, s:s + 1], modcol[:, which, 4 + k, s:s + 1], ALU.mult, ALU.add)
                    last.then_inc(hq_free[1], 1)

                dve.wait_ge(tq_free, l * TQ + T_MOD + 2)
                norm_rows(0, 0, 0, False)
                for g in range(G_QKV, G_GATE):
                    c, t = divmod(g - G_QKV, NT)
                    if g % 2:
                        dve.wait_ge(g_done, l * GROUPS + g + 1)
                        if g == G_QKV + 1:
                            dve.wait_ge(g_saved, l * 32 + 32)
                        nc.vector.tensor_copy(y[:, t, QW * c:QW * c + QW], ps[:, 1, 0:QW]).then_inc(g_free[1], 1)
                for b in range(2):
                    dve.wait_ge(g_free[b], l * (GROUPS // 2) + G_GATE // 2 + 1)
                dve.wait_ge(tq_free, l * TQ + T_CK + 2)
                heads = lambda a, n: a.rearrange("p (h d) -> p h d", h=n)
                for t in range(NT):
                    for br, base in ((0, AQ), (1, CQ)):
                        yb = y[:, t, base:base + 512]
                        link(TT(tmp[0], yb, yb, ALU.mult))
                        link(nc.vector.tensor_reduce(st100[:, t, 8 * br:8 * br + 8], heads(tmp[0], 8), axis=AX.X, op=ALU.add))
                    dve.wait_ge(gelu_ready, l * NT + t + 1)
                    v = y[:, t, BV:BV + 256]
                    link(TT(tmp[1][:, 0:256], v, v, ALU.mult))
                    link(nc.vector.tensor_reduce(st100[:, t, 16:20], heads(tmp[1][:, 0:256], 4), axis=AX.X, op=ALU.add))
                TS(st100[:, :, :], st100[:, :, :], 1.0 / HD, EPS, ALU.mult, ALU.add).then_inc(ms_ready, 1)
                dve.wait_ge(sd_ready, l * 3 + 2)
                link(nc.vector.reciprocal(rs100[:, :, :], rs100[:, :, :]))
                for t in range(NT):
                    for br, base in ((0, AQ), (1, CQ)):
                        yb = y[:, t, base:base + 512]
                        yh = heads(yb, 8)
                        link(TT(yh, yh, rs100[:, t, 8 * br:8 * br + 8, None].to_broadcast([128, 8, HD]), ALU.mult))
                        link(TT(yh[:, 0:6], yh[:, 0:6], gain[:, br, 0:1].to_broadcast([128, 6, HD]), ALU.mult))
                        link(TT(yh[:, 6:8], yh[:, 6:8], gain[:, br, 1:2].to_broadcast([128, 2, HD]), ALU.mult))
                        y4 = yb.rearrange("p (h a b c) -> p h a b c", h=8, a=2, b=2)
                        t4 = tmp[0].rearrange("p (h a b c) -> p h a b c", h=8, a=2, b=2)
                        s4 = rope[:, 1, t].rearrange("p (a b c) -> p a b c", a=2, b=2)
                        for b in range(2):
                            link(TT(t4[:, :, :, b], y4[:, :, :, 1 - b],
                                    s4[:, None, :, b].to_broadcast([128, 8, 2, 16]), ALU.mult))
                        link(TT(yh, yh, rope[:, 0, t:t + 1].to_broadcast([128, 8, HD]), ALU.mult))
                        if t:
                            dve.wait_ge(tq_done, l * TQ + T_QK + 2 * t + br - 1)
                        pair3 = lambda a, o: a.rearrange(o, v=2, g=3)
                        TT(pair3(qpair[:, br], "p (g v d) -> p v g d"), pair3(yb[:, 0:384], "p (v g d) -> p v g d"),
                           pair3(tmp[0][:, 0:384], "p (v g d) -> p v g d"), ALU.add)
                        TT(yb[:, 384:512], yb[:, 384:512], tmp[0][:, 384:512], ALU.add).then_inc(qk_ready, 1)
                        dve.wait_ge(qk_ready, l * 2 * NT + 2 * t + br + 1)
                for t in range(NT):
                    v = y[:, t, BV:BV + 256]
                    link(TT(heads(v, 4), heads(v, 4), rs100[:, t, 16:20, None].to_broadcast([128, 4, HD]), ALU.mult))
                    TT(v, v, vgain[:, :], ALU.mult).then_inc(v_ready, 1)
                for t in range(NT):
                    dve.wait_ge(tq_done, l * TQ + T_MLP + t + 1)
                    for g in range(4):
                        u = y[:, t, BU + 64 * g:BU + 64 * g + 64]
                        last = STT(u, ps[:, 7, 64 * g:64 * g + 64], bs[:, g:g + 1], u, ALU.add, ALU.mult)
                    last.then_inc(tq_free, 1)
                for i in range(UNITS + 2):
                    if i < UNITS:
                        t, br, kv, g, blocks = unit(i)
                        n = 128 * len(blocks)
                        h = 3 * kv + g
                        dve.wait_ge(s_done, l * UNITS + i + 1)
                        link(nc.vector.reduce_max(mx[:, :], ps[:, 2:4].rearrange("p b n -> p (b n)")[:, 0:n], AX.X))
                        if br == 0:
                            TS(nm[:, i % 2:i % 2 + 1], mx[:, :], -SCALE, nsink[:, h:h + 1], ALU.mult, ALU.min).then_inc(nm_ready, 1)
                        else:
                            TS(nm[:, i % 2:i % 2 + 1], mx[:, :], -SCALE, None, ALU.mult).then_inc(nm_ready, 1)
                    u = i - 1
                    if 0 <= u < UNITS:
                        t, br, kv, g, blocks = unit(u)
                        if u % 2 == 0:
                            n = 128 * len(blocks)
                            dve.wait_ge(pt_done, l * UNITS + u + 2)
                            dve.wait_ge(pv_done, l * UNITS + u + 1)
                            nc.vector.tensor_copy(probT[:, 0, 0:n],
                                                  ps[:, 4:6].rearrange("p b n -> p (b n)")[:, 0:n]).then_inc(pt_evac, 1)
                        dve.wait_ge(e_ready, l * UNITS + u + 2)
                        if u >= 2:
                            dve.wait_ge(o_evac, l * UNITS + u)
                        if br == 0:
                            dve.wait_ge(es_ready, l * (NT * 6) + t * 6 + u % 12 + 1)
                            link(TT(den[:, :], sm[:, u % 2:u % 2 + 1], es[:, u % 2:u % 2 + 1], ALU.add))
                            link(nc.vector.reciprocal(rden[:, u % 2:u % 2 + 1], den[:, :]))
                        else:
                            link(nc.vector.reciprocal(rden[:, u % 2:u % 2 + 1], sm[:, u % 2:u % 2 + 1]))
                    u = i - 2
                    if u >= 0:
                        t, br, kv, g, _ = unit(u)
                        h = 3 * kv + g
                        dve.wait_ge(pv_done, l * UNITS + u + 3)
                        TS(y[:, t, (AQ, CQ)[br] + 64 * h:(AQ, CQ)[br] + 64 * h + 64], ps[:, 6, 0:64],
                           rden[:, u % 2:u % 2 + 1], None, ALU.mult).then_inc(o_evac, 1)
                dve.wait_ge(kv_saved, l * 64 + 64)
                for o in range(2 * NT):
                    n, t = divmod(o, NT)
                    m = merged[:, t, 512 * n:512 * n + 512]
                    b = 2 + 3 * (o % 2)
                    dve.wait_ge(opj_done, l * 2 * NT + o + 1)
                    link(STT(m, gates[:, t, 3 * n], 1.0, ps[:, b], ALU.add, ALU.mult))
                    link(STT(tmp[0], gates[:, t, 3 * n + 1], 1.0, ps[:, b + 1], ALU.add, ALU.mult))
                    STT(tmp[1], gates[:, t, 3 * n + 2], 1.0, ps[:, b + 2], ALU.add, ALU.mult).then_inc(opj_free, 1)
                    dve.wait_ge(opj_free, l * 2 * NT + o + 3)
                    link(TT(m, m, tmp[0], ALU.add))
                    TT(m, m, tmp[1], ALU.add).then_inc(merged_ready, 1)
                    dve.wait_ge(merged_ready, l * 2 * NT + o + 1)
                for t in range(NT):
                    dve.wait_ge(hq_done, l * HQ + H_M + 2 * t + 2)
                    TS(HT[:, 4:8, 128 * t:128 * t + 128], ps[:, 3].rearrange("p (s n) -> p s n", s=4), 0.5, None,
                       ALU.mult).then_inc(hq_free[1], 1)
                dve.wait_ge(x_back, l * 16 + 16)
                dve.wait_ge(g1_ready, l * 32 + 32)
                for c in range(2):
                    for t in range(NT):
                        g = G_WO + c * NT + t
                        s = 0 if t < NS else 1
                        dve.wait_ge(g_done, l * GROUPS + g + 1)
                        TT(tmp[0], ps[:, g % 2], g1bc[:, s, 512 * c:512 * c + 512], ALU.mult).then_inc(g_free[g % 2], 1)
                        dve.wait_ge(g_free[g % 2], l * (GROUPS // 2) + g // 2 + 2)
                        TT(x[:, t, 512 * c:512 * c + 512], x[:, t, 512 * c:512 * c + 512], tmp[0], ALU.add).then_inc(x_ready, 1)
                        dve.wait_ge(x_ready, l * 2 * NT + NT * c + t + 1)
                norm_rows(1, NT, H_2, True)

                dve.wait_ge(rt_done, l + 1)
                bc = lambda a: a[:, :, None].to_broadcast([128, NT, E])
                link(TT(aff, ps[:, 6, 0:NT * E].rearrange("p (t e) -> p t e", t=NT), brt[:, None, :].to_broadcast([128, NT, E]), ALU.add))
                link(nc.vector.tensor_reduce(rmax, aff, axis=AX.X, op=ALU.max))
                TT(aff, aff, bc(rmax), ALU.subtract).then_inc(lg_ready, 1)
                dve.wait_ge(pe_ready, l + 1)
                link(nc.vector.tensor_reduce(rsum, aff, axis=AX.X, op=ALU.add))
                link(nc.vector.reciprocal(rrec, rsum))
                TT(aff, aff, bc(rrec), ALU.mult).then_inc(aff_ready, 1)
                dve.wait_ge(afft_done, l + 1)
                nc.vector.tensor_copy(affT[:, 0:512], ps[0:E, 7])
                link(nc.vector.tensor_copy(affT[:, 512:640], ps[0:E, 6, 0:128]))
                link(nc.vector.memset(slots[:, 2], -1.0))
                link_top(nc.vector.memset(slots[:, 3], 0.0))
                for a, lo, n, cap in ((2, 512, 128, CP), (0, 0, 512, CS)):
                    w = affT[:, lo:lo + n]
                    for r in range(0, cap, 8):
                        link_top(nc.vector.max(out=topv[:, r:r + 8], in_=w))
                        link_top(nc.vector.max_index(out=topi[:, r:r + 8], in_max=topv[:, r:r + 8], in_values=w))
                        if r + 8 < cap:
                            link_top(nc.vector.match_replace(out=w, in_to_replace=topv[:, r:r + 8], in_values=w, imm_value=-1.0e30))
                    for h in range(2):
                        nc.vector.tensor_copy(slots[:, a, 64 * h:64 * h + cap], topi[:, 0:cap])
                        link_top(nc.vector.tensor_copy(slots[:, a + 1, 64 * h:64 * h + cap], topv[:, 0:cap]))
                dve.sem_inc(slots_ready, 1)
                dve.wait_ge(slott_done, l + 1)
                link(nc.vector.tensor_copy(slotT.rearrange("p a e -> p (a e)"), ps[:, 7, 0:64]))
                ev = lambda a, h: a.rearrange("p (j b) -> p b j", b=2)[:, h]
                for h in range(2):
                    r = slice(64 * h, 64 * h + 64)
                    nc.vector.tensor_copy(cols[r, :], ev(slotT[r, 0], h))
                    nc.vector.tensor_copy(colp[r, :], ev(slotT[r, 2], 1 - h))
                    nc.vector.tensor_copy(ev(colv[r, :], h), ev(slotT[r, 1], h))
                    link(nc.vector.tensor_copy(ev(colv[r, :], 1 - h), ev(slotT[r, 3], 1 - h)))
                nc.vector.tensor_copy(idxs[0:CS, :], slotT[0:CS, 0])
                TS(idxp[0:CP, :], slotT[0:CP, 2], 512.0, None, ALU.add).then_inc(idx_ready, 1)
                dve.wait_ge(g2_ready, l * 64 + 64)
                dve.wait_ge(moe_init, l * 2 + 2)
                if steps[0] != DVE_STEPS:
                    raise ValueError(f"DVE_STEPS {steps[0]}")

                def modulate(b, idx):
                    dve.wait_ge(mq_done, idx)
                    for k in range(4):
                        for h in range(2):
                            s = (h + b) % 2
                            last = TS(xgT[:, b, 4 + k, 64 * h:64 * h + 64], ps[:, 5, 128 * k + 64 * h:128 * k + 64 * h + 64],
                                      modcol[:, 3, 4 + k, s:s + 1], modcol[:, 2, 4 + k, s:s + 1], ALU.mult, ALU.add)
                    last.then_inc(mq_free[1], 1)

                def gathered(j):
                    for t in range(NT):
                        for h in range(2):
                            dve.wait_ge(sc_done, l * 80 + (10 * j + 2 * t + h + 1))
                            dve.wait_ge(sc_free[h], l * (5 * PAIRS) + (5 * j + t + 1))
                            xt = x[:, t, 512 * h:512 * h + 512]
                            TT(xt, xt, ps[:, 6 + h], ALU.add).then_inc(sc_free[h], 1)

                def pair(j, first, last_pair):
                    for b in range(2):
                        for h in range(2):
                            dve.wait_ge(sil_ready, l * 32 + (4 * j + 2 * b + h + 1))
                            dve.wait_ge(gu_done, l * 64 + (8 * j + 4 * b + 2 * h + 2))
                            TT(hh[:, 512 * h:512 * h + 512], sil[:, h], ps[:, 2 + h], ALU.mult).then_inc(hh_ready, 1)
                        if b == 0:
                            if not first:
                                gathered(j - 1)
                            TS(hots, iota, cols[:, bass.ds(j, 1)], None, ALU.is_equal)
                            TS(hotp, iota[:, 0:128], colp[:, bass.ds(j, 1)], None, ALU.is_equal).then_inc(hot_ready, 1)
                        skip = 2 if b and last_pair else 0
                        if not skip:
                            modulate(1 - b, l * 64 + (8 * j + 4 * b + 4))
                        dve.wait_ge(mq_done, l * 64 + (8 * j + 4 * b + 6 - skip))
                        nc.vector.tensor_copy(hhT[:, 4:8], ps[:, 5].rearrange("p (k n) -> p k n", k=4)).then_inc(mq_free[1], 1)
                        for h in range(2):
                            dve.wait_ge(dn_done, l * 32 + (4 * j + 2 * b + h + 1))
                            n = slice(512 * h, 512 * h + 512)
                            for r, dst in ((slice(0, 64), (osam, opro)[b]), (slice(64, 128), (opro, osam)[b])):
                                last = STT(dst[r, n], ps[r, h], colv[r, bass.ds(2 * j + b, 1)], g2bc[r, b, n], ALU.mult, ALU.mult)
                            last.then_inc(out_evac[h], 1)

                modulate(0, l * 64 + 2)
                pair(0, True, False)
                with dve.Fori(1, PAIRS - 1) as j:
                    pair(j, False, False)
                pair(PAIRS - 1, False, True)
                gathered(PAIRS - 1)


def kernel(**inputs):
    import numpy as np
    import concourse.bacc as bacc
    from concourse.bass_utils import run_bass_kernel_spmd as run

    a = {k: np.asarray(v) for k, v in inputs.items()}
    a["w_o"] = np.concatenate([a.pop("w_a_o"), a.pop("w_c_o"), a.pop("w_b_o")], axis=1)
    a["qk_gain"] = np.concatenate([a.pop("a_q_norm"), a.pop("a_k_norm"), a.pop("c_q_norm"), a.pop("c_k_norm")], axis=1)
    flat = lambda v: v[0].reshape(DEPTH, 128, 128)
    a["cache_k"] = np.stack([flat(a.pop("cache_a_k")), flat(a.pop("cache_c_k"))], axis=2)
    a["cache_v"] = np.stack([flat(a.pop("cache_a_v")), flat(a.pop("cache_c_v"))], axis=2)
    a["b_bs"] = a["b_bs"].transpose(0, 2, 1)
    n = np.arange(512)
    freq = np.float32(10000.0) ** (-np.arange(16, dtype=np.float32) / np.float32(16))
    ang = np.stack([(n // 64).astype(np.float32)[:, None] * freq, (n % 64).astype(np.float32)[:, None] * freq], 1)
    table = np.zeros((128, 2, NT, 2, 2, 16), np.float32)
    table[:, 0] = 1.0
    for t in range(NS):
        for b in range(2):
            table[:, 0, t, :, b] = np.cos(ang[128 * t:128 * t + 128])
            table[:, 1, t, :, b] = np.sin(ang[128 * t:128 * t + 128]) * (1 if b else -1)
    a["rope"] = table.reshape(128, 2, NT, HD)

    nc = bacc.Bacc("TRN2", target_bir_lowering=False, num_devices=1)
    f32 = mybir.dt.float32
    arrays, aps = {}, {}
    for k, v in a.items():
        arrays[f"in_{k}"] = np.ascontiguousarray(v)
        aps[k] = nc.dram_tensor(f"in_{k}", v.shape, f32, kind="ExternalInput").ap()
    shapes = [(1, 128, D), (1, 512, D)] + [(1, DEPTH, 128, 2, HD)] * 4
    outs = [nc.dram_tensor(f"out_{i}", s, f32, kind="ExternalOutput").ap() for i, s in enumerate(shapes)]
    scratch = [nc.dram_tensor(n, s, f32, kind="Internal").ap()
               for n, s in (("x_save", (640, D)), ("x_norm", (640, D)), ("g_rows", (2, 2, D)))]
    build(nc, aps, outs, scratch)
    r = run(nc, [arrays], core_ids=[0])
    return tuple(r.results[0][f"out_{i}"] for i in range(len(shapes)))
```

```python
from contextlib import ExitStack

import concourse.bass as bass
from concourse import mybir

D = 1024
KB = D // 128
NS = 4
NT = NS + 1
DEPTH = 2
HD = 64
QKV = 1792
AQ, AK, AV, BU, BV, CQ, CK, CV = 0, 384, 512, 640, 896, 1152, 1536, 1664
NQC, QW = 4, QKV // 4
NMOD = 6 * D // 512
NGC = 6
E = 16
PAIRS = E // 2
CS, CP = 64, 16
UB = 4
UNITS_E = 2 * 6 * E
AHEAD = 3
FFC = 6
RING = 3
C_QKV = NMOD
C_GATE = C_QKV + NQC
C_OUT = C_GATE + NGC
C_WO = C_OUT + 2
C_ROUT = C_WO + 2
C_MOE = C_ROUT + 1
CHUNKS = C_MOE + E * FFC
assert CHUNKS % RING == 0 and FFC % RING == 0 and C_MOE % RING == 0
LOADS = CHUNKS // RING

G_QKV = NMOD
G_GATE = G_QKV + NQC * NT
G_WO = G_GATE + NGC * NT
GROUPS = G_WO + 2 * NT
T_MOD, T_WS, T_CK, T_QK = 0, 1, 2, 3
T_MLP = T_QK + 2 * NT
T_O = T_MLP + NT
TQ = T_O + 2 * NT
H_M = 2 * NT
H_2 = 4 * NT
HQ = 6 * NT
UNITS = NT * 12
EPS = 1e-6
SCALE = HD ** -0.5

PRE = 8
HALVES = 2 * (NGC * NT - PRE)


def halves_until(i):
    return (i + 1) * HALVES // (UNITS + 2)


def unit(u):
    t, r = divmod(u, 12)
    br, h = divmod(r, 6)
    kv, g = divmod(h, 3)
    if t == NS:
        blocks = [NS]
    elif br == 0:
        blocks = [b for b in (t - 1, t, t + 1) if 0 <= b < NS] + [NT]
    else:
        blocks = list(range(NS)) + [NT]
    return t, br, kv, g, blocks


def build(nc, A, outs, scratch):
    f32 = mybir.dt.float32
    u32 = mybir.dt.uint32
    ALU = mybir.AluOpType
    ACT = mybir.ActivationFunctionType
    AX = mybir.AxisListType
    y_prompt, y_sample, new_a_k, new_a_v, new_c_k, new_c_v = outs
    xs_d, xn_d, g_d = scratch

    ctx = ExitStack()
    with ctx:
        def sb(name, shape, dt=f32):
            return ctx.enter_context(nc.sbuf_tensor(name, shape, dt))

        def sem(name):
            return ctx.enter_context(nc.semaphore(name))

        f32r = mybir.dt.float32r
        ring = sb("ring", [128, RING, KB, 512])
        X = sb("X", [128, NT * D])
        EP = sb("EP", [128, 3 * 640])
        x = X[:, :].rearrange("p (t d) -> p t d", t=NT)
        prob = EP[:, 0:640]
        probT = EP[:, 640:1920].rearrange("p (b n) -> p b n", b=2)
        qpair = EP[:, 512:1280].rearrange("p (b n) -> p b n", b=2)
        tmp = [EP[:, 512 * i:512 * i + 512] for i in range(3)]
        aff = EP[:, 0:NT * E].rearrange("p (t e) -> p t e", t=NT)
        slots = EP[0:E, 128:640].rearrange("p (a n) -> p a n", a=4)
        topv = EP[0:E, 640:704]
        slotT = EP[:, 768:832].rearrange("p (a e) -> p a e", a=4)
        rmax = EP[:, 832:837]
        rsum = EP[:, 840:845]
        rrec = EP[:, 848:853]
        affT = EP[0:E, 1024:1664]

        ident = sb("ident", [128, 128])
        mask = sb("mask", [128, 2, 128])
        rope = sb("rope", [128, 2, NT, HD])
        gain = sb("gain", [128, 2, 2, HD])
        vgain = sb("vgain", [128, 256])
        wsT = sb("wsT", [128, 4, 128])
        cacheV = sb("cacheV", [128, 2, 128])
        condT = sb("condT", [128, 2 * KB])
        modcol = sb("modcol", [128, 2, KB, 2])
        bs = sb("bs", [128, 4])
        sink = sb("sink", [128, 6])
        nsink = sb("nsink", [128, 6])
        brt = sb("brt", [128, E])
        topi = sb("topi", [E, CS], u32)
        idxs = sb("idxs", [128, E], u32)
        idxp = sb("idxp", [128, E], u32)
        cols = sb("cols", [128, PAIRS])
        colp = sb("colp", [128, PAIRS])
        colv = sb("colv", [128, E])
        st5 = sb("st5", [128, NT])
        rs5 = sb("rs5", [128, NT])
        st100 = sb("st100", [128, NT, 20])
        rs100 = sb("rs100", [128, NT, 20])
        mx = sb("mx", [128, 1])
        nm = sb("nm", [128, 2])
        sm = sb("sm", [128, 2])
        es = sb("es", [128, 2])
        den = sb("den", [128, 1])
        rden = sb("rden", [128, 2])

        with ExitStack() as first:
            def sa(name, shape):
                return first.enter_context(nc.sbuf_tensor(name, shape, f32))

            G = sa("G", [128, NT * 4 * 512])
            HT = sa("HT", [128, KB, NT * 128])
            Y = sa("Y", [128, NT * QKV])
            QK = sa("QK", [128, 8 * 640 + 2 * 768])
        with ExitStack() as second:
            def sm_(name, shape, dt=f32):
                return second.enter_context(nc.sbuf_tensor(name, shape, dt))

            w_hi = sm_("w_hi", [128, UB, 4, 512], f32r)
            w_lo = sm_("w_lo", [128, UB, 4, 512], f32r)
            xT = sm_("xT", [128, 2, KB, 128], f32r)
            hT = sm_("hT", [128, 2, KB, 128], f32r)
            xg = sm_("xg", [128, 2, D])
            hh = sm_("hh", [128, D])
            sil = sm_("sil", [128, 2, 512])
            osam = sm_("osam", [128, D])
            opro = sm_("opro", [128, D])
            hots = sm_("hots", [128, 512])
            hotp = sm_("hotp", [128, 128])
            iota = sm_("iota", [128, 512])
            g2bc = sm_("g2bc", [128, 2, D])

        def gates(t, c):
            return X[:, D * t + 512 * c:D * t + 512 * c + 512] if c < 2 else \
                G[:, 2048 * t + 512 * (c - 2):2048 * t + 512 * (c - 2) + 512]

        bmod = G[0:2, 0:6 * D]
        nrow = G[0:2, 6 * D:8 * D].rearrange("p (a d) -> p a d", a=2)
        modbc = G[:, 0:4 * D].rearrange("p (a s d) -> p a s d", a=2, s=2)
        modrow = Y[0:2, 0:6 * D]
        xn = Y[:, 6144:8192].rearrange("p (b d) -> p b d", b=2)
        y = Y[:, :].rearrange("p (t c) -> p t c", t=NT)
        merged = Y[:, 0:NT * D].rearrange("p (t d) -> p t d", t=NT)
        qoT = QK[:, 0:8 * 640].rearrange("p (s n) -> p s n", s=8)
        kT = QK[:, 8 * 640:8 * 640 + 2 * 768].rearrange("p (b n) -> p b n", b=2)
        g1bc = QK[:, 0:2 * D].rearrange("p (s d) -> p s d", s=2)
        wsraw = EP[:, 0:512].rearrange("p (g q) -> p g q", g=4)
        ckraw = EP[:, 512:768].rearrange("p (b q) -> p b q", b=2)
        condrow = EP[0:16, 1024:1152]

        ps = ctx.enter_context(nc.psum_tensor("ps", [128, 8, 512], f32))

        ring_ready = [sem(f"ring_ready{s}") for s in range(RING)]
        ring_free = sem("ring_free")
        in_ready = sem("in_ready")
        const_ready = sem("const_ready")
        par_ready = sem("par_ready")
        PARS = 14
        x_saved = sem("x_saved")
        x_back = sem("x_back")
        g_saved = sem("g_saved")
        g1_ready = sem("g1_ready")
        g2_ready = sem("g2_ready")
        kv_saved = sem("kv_saved")
        xn_saved = [sem(f"xn_saved{b}") for b in range(2)]
        out_saved = sem("out_saved")
        cond_silu = sem("cond_silu")
        cond_done = sem("cond_done")
        cond_ready = sem("cond_ready")
        g_done = sem("g_done")
        g_free = [sem(f"g_free{b}") for b in range(2)]
        tq_done = sem("tq_done")
        tq_free = sem("tq_free")
        hq_done = sem("hq_done")
        hq_free = [sem(f"hq_free{b}") for b in range(2)]
        ss_ready = sem("ss_ready")
        ms_ready = sem("ms_ready")
        sd_ready = sem("sd_ready")
        ROOTS = 2 * NT + 1
        xn_ready = sem("xn_ready")
        mod_ready = sem("mod_ready")
        gelu_ready = sem("gelu_ready")
        qk_ready = sem("qk_ready")
        v_ready = sem("v_ready")
        s_done = sem("s_done")
        nm_ready = sem("nm_ready")
        e_ready = sem("e_ready")
        es_ready = sem("es_ready")
        pt_done = sem("pt_done")
        pt_evac = sem("pt_evac")
        pv_done = sem("pv_done")
        o_evac = sem("o_evac")
        opj_done = sem("opj_done")
        opj_free = sem("opj_free")
        merged_ready = sem("merged_ready")
        x_ready = sem("x_ready")
        rt_done = sem("rt_done")
        lg_ready = sem("lg_ready")
        pe_ready = sem("pe_ready")
        aff_ready = sem("aff_ready")
        afft_done = sem("afft_done")
        slots_ready = sem("slots_ready")
        slott_done = sem("slott_done")
        idx_ready = sem("idx_ready")
        hot_ready = sem("hot_ready")
        moe_init = sem("moe_init")
        xg_ready = [sem(f"xg_ready{b}") for b in range(2)]
        xt_done = sem("xt_done")
        mq_done = sem("mq_done")
        mq_hi = sem("mq_hi")
        mq_free = [sem(f"mq_free{b}") for b in range(2)]
        hi_ready = sem("hi_ready")
        lo_ready = sem("lo_ready")
        unit_used = sem("unit_used")
        sil_ready = sem("sil_ready")
        hh_ready = sem("hh_ready")
        out_evac = [sem(f"out_evac{b}") for b in range(2)]
        os_ready = sem("os_ready")
        mb_ready = sem("mb_ready")
        sc_done = sem("sc_done")
        sc_free = [sem(f"sc_free{b}") for b in range(2)]
        dve_step = sem("dve_step")
        pool_step = sem("pool_step")
        waited = [sem(f"waited{i}") for i in range(4)]

        def settle(engine, i):
            engine.sem_inc(waited[i], 1)

        DVE_STEPS = (2 + 3 * NT
                     + NT * (6 + 12 + 1) + 1
                     + UNITS * 2 + UNITS // 2
                     + 2 * NT * 3
                     + 4 + 3
                     + 3 * (CS + CP) // 8 - 2 + 4 + 3)

        def chunk_src(l, c, e=None):
            if e is not None:
                w = (A["w_gate"], A["w_up"], A["w_gate"], A["w_up"], A["w_down"], A["w_down"])[c]
                n = (0, 0, 1, 1, 0, 1)[c]
                return w[l, e].rearrange("(k p) n -> p k n", p=128)[:, :, 512 * n:512 * n + 512]
            if c < C_QKV:
                w, lo, n = A["w_mod"], 512 * c, 512
            elif c < C_GATE:
                w, lo, n = A["w_in"], QW * (c - C_QKV), QW
            elif c < C_OUT:
                half, br = divmod(c - C_GATE, 3)
                w, lo, n = A["w_in"], QKV + D * br + 512 * half, 512
            elif c < C_WO:
                w, lo, n = A["w_o"], 512 * (c - C_OUT), 512
            elif c < C_ROUT:
                w, lo, n = A["w_out"], 512 * (c - C_WO), 512
            else:
                w, lo, n = A["w_router"], 0, E
            return w[l].rearrange("(k p) n -> p k n", p=128)[:, :, lo:lo + n]

        def raw_of(j, b, first, s):
            if first and b == 0:
                return (s // 2) % RING, (s // 2) // RING
            m = 6 * b - 2 + s // 2
            return m % RING, 4 * j + m // RING

        junk = EP[:, 768:1792]
        block = ctx.enter_context(nc.Block())

        @block.sync
        def _(sp):
            sp.dma_start(x[:, 0:NS], A["x_sample"][0].rearrange("(t p) d -> p t d", p=128)).then_inc(in_ready, 16)
            sp.dma_start(x[:, NS], A["x_prompt"][0]).then_inc(in_ready, 16)
            sp.dma_start(condrow[0:KB], A["c"][0].rearrange("(k p) -> k p", p=128)).then_inc(in_ready, 16)
            sp.dma_start(condrow[KB:2 * KB], A["c_ctx"].rearrange("(k p) -> k p", p=128)).then_inc(in_ready, 16)
            sp.dma_start(rope[:, :, :, :], A["rope"]).then_inc(in_ready, 16)
            with sp.Fori(0, DEPTH) as l:
                for c in range(C_MOE):
                    src = chunk_src(l, c)
                    if c < RING:
                        sp.wait_ge(lo_ready, l * UNITS_E + 1)
                    else:
                        sp.wait_ge(ring_free, l * C_MOE + c - RING + 1)
                    sp.dma_start(ring[:, c % RING, :, 0:src.shape[2]], src).then_inc(ring_ready[c % RING], 16)

                def expert_chunk(m, slot, e, c):
                    sp.wait_ge(lo_ready, l * UNITS_E + 2 * m - 3)
                    sp.dma_start(ring[:, slot], chunk_src(l, c, e)).then_inc(ring_ready[slot], 16)

                for c in range(4):
                    if c < RING:
                        sp.wait_ge(ring_free, l * C_MOE + C_MOE - RING + c + 1)
                        sp.dma_start(ring[:, c], chunk_src(l, c, 0)).then_inc(ring_ready[c], 16)
                    else:
                        expert_chunk(c, c % RING, 0, c)
                with sp.Fori(1, E) as e:
                    for c in range(FFC):
                        expert_chunk(6 * e - 2 + c, (c + 1) % RING, e if c < 4 else e - 1, c)
                for c in (4, 5):
                    expert_chunk(6 * E - 6 + c, (c + 6 * E - 6) % RING, E - 1, c)
            sp.wait_ge(sc_free[0], DEPTH * 5 * PAIRS + 1)
            sp.wait_ge(sc_free[1], DEPTH * 5 * PAIRS + 1)
            sp.dma_start(y_sample[0].rearrange("(t p) d -> p t d", p=128), x[:, 0:NS]).then_inc(out_saved, 16)
            sp.dma_start(y_prompt[0], x[:, NS]).then_inc(out_saved, 16)
            sp.wait_ge(out_saved, 32)

        @block.gpsimd
        def _(pool):
            pool.memset(ident[:, :], 0.0).then_inc(pool_step, 1)
            pool.memset(mask[:, :, :], 0.0).then_inc(pool_step, 1)
            pool.wait_ge(pool_step, 2)
            pool.affine_select(out=ident[:, :], in_=ident[:, :], compare_op=ALU.not_equal, fill=1.0, base=0,
                               pattern=[[-1, 128]], channel_multiplier=1).then_inc(const_ready, 1)
            pool.affine_select(out=mask[:, 0], in_=mask[:, 0], compare_op=ALU.is_ge, fill=-1.0e30, base=0,
                               pattern=[[1, 128]], channel_multiplier=-1).then_inc(const_ready, 1)
            pool.affine_select(out=mask[:, 1], in_=mask[:, 1], compare_op=ALU.is_ge, fill=-1.0e30, base=0,
                               pattern=[[-1, 128]], channel_multiplier=1).then_inc(const_ready, 1)
            pool.sem_inc(xt_done, 2)
            pool.wait_ge(in_ready, 80)
            pool.wait_ge(cond_ready, 1)
            with pool.Fori(0, DEPTH) as l:
                pool.dma_start(xs_d.rearrange("(t p) d -> p t d", p=128), x).then_inc(x_saved, 16)

                def par(dst, src):
                    pool.dma_start(dst, src).then_inc(par_ready, 16)

                for s in range(2):
                    par(bmod[s:s + 1], A["b_mod"][bass.ds(l, 1)])
                    par(nrow[s:s + 1, 0], A["norm1_g"][bass.ds(l, 1)])
                    par(nrow[s:s + 1, 1], A["norm2_g"][bass.ds(l, 1)])
                par(wsraw, A["b_ws"][l].rearrange("g p q -> p g q"))
                par(gain.rearrange("p a b d -> p (a b d)"), A["qk_gain"][bass.ds(l, 1)].to_broadcast([128, 256]))
                par(vgain[:, :], A["b_v_norm"][bass.ds(l, 1)].to_broadcast([128, 256]))
                par(sink[:, :], A["a_sink"][bass.ds(l, 1)].to_broadcast([128, 6]))
                par(brt[:, :], A["b_router"][bass.ds(l, 1)].to_broadcast([128, E]))
                par(bs[:, :], A["b_bs"][l])
                par(cacheV[:, :, :], A["cache_v"][l])
                par(ckraw, A["cache_k"][l])
                pool.wait_ge(mod_ready, l + 1)
                settle(pool, 2)
                for i, lo in enumerate((2 * D, 5 * D, 3 * D, 4 * D)):
                    pool.dma_start(g_d[:, i, :], modrow[:, lo:lo + D]).then_inc(g_saved, 16)
                pool.wait_ge(qk_ready, l * 2 * NT + 2 * NT)
                settle(pool, 2)
                for dst, c in ((new_a_k, AK), (new_a_v, AV), (new_c_k, CK), (new_c_v, CV)):
                    pool.dma_start(dst[0, l].rearrange("s k d -> s (k d)"), y[:, NS, c:c + 128]).then_inc(kv_saved, 16)
                pool.wait_ge(opj_free, l * 2 * NT + 2 * NT + 2)
                settle(pool, 2)
                pool.dma_start(x, xs_d.rearrange("(t p) d -> p t d", p=128)).then_inc(x_back, 16)
                pool.wait_ge(g_saved, l * 64 + 64)
                settle(pool, 2)
                for s in range(2):
                    pool.dma_start(g1bc[:, s], g_d[s, 0:1, :].to_broadcast([128, D])).then_inc(g1_ready, 16)
                for a in range(2):
                    for s in range(2):
                        pool.dma_start(modbc[:, a, s], g_d[s, 2 + a:3 + a, :].to_broadcast([128, D])).then_inc(mb_ready, 16)
                for t in range(NT):
                    pool.wait_ge(xn_ready, l * 2 * NT + NT + t + 1)
                    settle(pool, 2)
                    pool.dma_start(xn_d[128 * t:128 * t + 128, :], xn[:, t % 2]).then_inc(xn_saved[t % 2], 16)
                for b, n in ((0, NT - NT // 2), (1, NT // 2)):
                    pool.wait_ge(xn_saved[b], l * (16 * n) + 16 * n)
                pool.wait_ge(hq_free[0], l * 3 * NT + 3 * NT + 1)
                pool.wait_ge(hq_free[1], l * 3 * NT + 3 * NT + 1)
                settle(pool, 2)
                pool.iota(iota[:, :], pattern=[[1, 512]], base=0, channel_multiplier=0,
                          allow_small_or_imprecise_dtypes=True).then_inc(moe_init, 1)
                pool.memset(xg[:, :, :], 0.0).then_inc(moe_init, 1)
                pool.wait_ge(moe_init, l * 2 + 2)
                settle(pool, 2)
                for s in range(2):
                    for h in range(2):
                        pool.dma_start(g2bc[64 * h:64 * h + 64, (s + h) % 2],
                                       g_d[s, 1:2, :].to_broadcast([64, D])).then_inc(g2_ready, 16)
                pool.wait_ge(idx_ready, l + 1)
                settle(pool, 2)

                def gather(j, b):
                    e = 2 * j + b
                    lat, pro = (0, 64) if b == 0 else (64, 0)
                    pool.wait_ge(xt_done, l * E + 2 * j + (b + 1))
                    settle(pool, 2)
                    pool.indirect_dma_start(xg[lat:lat + CS, b], None, xn_d,
                                            bass.IndirectOffsetOnAxis(ap=idxs[0:CS, e:e + 1], axis=0)
                                            ).then_inc(xg_ready[b], 16)
                    pool.indirect_dma_start(xg[pro:pro + CP, b], None, xn_d,
                                            bass.IndirectOffsetOnAxis(ap=idxp[0:CP, e:e + 1], axis=0)
                                            ).then_inc(xg_ready[b], 16)

                def scale(j, b):
                    for h in range(2):
                        pool.wait_ge(out_evac[h], l * E + (2 * j + b + 3))
                    for r, dst in ((slice(0, 64), (osam, opro)[b]), (slice(64, 128), (opro, osam)[b])):
                        pool.tensor_tensor(dst[r, :], dst[r, :], g2bc[r, b], ALU.mult).then_inc(os_ready, 1)

                gather(0, 0)
                gather(0, 1)
                pool.wait_ge(g2_ready, l * 64 + 64)
                for j in range(PAIRS - 1):
                    if j:
                        pool.wait_ge(os_ready, l * 32 + 4 * j)
                    gather(j + 1, 0)
                    gather(j + 1, 1)
                    for b in range(2):
                        pool.wait_ge(xg_ready[b], l * (32 * PAIRS) + 32 * (j + 2))
                    scale(j, 0)
                    scale(j, 1)
                scale(PAIRS - 1, 0)
                scale(PAIRS - 1, 1)
                pool.wait_ge(sc_free[0], l * 5 * PAIRS + 5 * PAIRS + 1)
                pool.wait_ge(sc_free[1], l * 5 * PAIRS + 5 * PAIRS + 1)
            pool.wait_ge(kv_saved, DEPTH * 64)
            pool.wait_ge(x_saved, DEPTH * 16)

        @block.tensor
        def _(pe):
            pe.sem_inc(unit_used, UB)
            pe.sem_inc(pt_done, 1)
            pe.sem_inc(pv_done, 2)
            pe.wait_ge(const_ready, 3)
            pe.wait_ge(cond_silu, 1)
            nc.tensor.transpose(ps[:, 7, 0:16], condrow, ident[0:16, 0:16]).then_inc(cond_done, 1)
            pe.wait_ge(cond_ready, 1)

            def transposes(bank, srcs, done):
                for i, s in enumerate(srcs):
                    last = nc.tensor.transpose(ps[:, bank, 128 * i:128 * i + 128], s, ident[:, :])
                last.then_inc(done, 1)

            with pe.Fori(0, DEPTH) as l:
                def arrived(c):
                    pe.wait_ge(ring_ready[c % RING], l * (16 * LOADS) + 16 * (c // RING + 1))

                def group(g, lhs, c, n, k0=0, k1=KB, release=False):
                    if k0 == 0:
                        pe.wait_ge(g_free[g % 2], l * (GROUPS // 2) + g // 2 + 1)
                    for k in range(k0, k1):
                        last = nc.tensor.matmul(ps[:, g % 2, 0:n] if lhs(k).shape[1] == 128 else ps[0:2, g % 2, 0:n],
                                                lhs(k), ring[:, c % RING, k, 0:n], start=k == 0, stop=k == KB - 1)
                    return last

                def tile(t):
                    return lambda k: HT[:, k, 128 * t:128 * t + 128]

                for c in range(NMOD):
                    arrived(c)
                    group(c, lambda k: condT.rearrange("p (s k) -> p k s", s=2)[:, k], c, 512).then_inc(g_done, 1)
                    pe.wait_ge(g_done, l * GROUPS + c + 1)
                    pe.sem_inc(ring_free, 1)
                pe.wait_ge(mod_ready, l + 1)
                pe.wait_ge(tq_free, l * TQ + T_MOD + 1)
                settle(pe, 0)
                for i, lo in enumerate((0, D)):
                    for k in range(KB):
                        last = nc.tensor.transpose(ps[:, 7, 2 * (KB * i + k):2 * (KB * i + k) + 2],
                                                   modrow[:, lo + 128 * k:lo + 128 * k + 128], ident[0:2, 0:2])
                last.then_inc(tq_done, 1)

                def h_tiles(first, src, ready, per, half_of=None):
                    for t in range(NT):
                        ready(t)
                        for h in range(2):
                            pe.wait_ge(hq_free[h], l * (HQ // 2) + (first // 2 + t) + 1)
                            transposes(2 + h, [src(t)[:, 128 * k:128 * k + 128] for k in range(4 * h, 4 * h + 4)],
                                       hq_done)

                h_tiles(0, lambda t: xn[:, t % 2], lambda t: pe.wait_ge(xn_ready, l * 2 * NT + t + 1), None)

                pe.wait_ge(par_ready, l * 16 * PARS + 16 * PARS)
                pe.wait_ge(tq_free, l * TQ + T_WS + 1)
                transposes(7, [wsraw[:, g] for g in range(4)], tq_done)
                pe.wait_ge(tq_free, l * TQ + T_CK + 1)
                transposes(7, [ckraw[:, b] for b in range(2)], tq_done)

                for c in range(NQC):
                    arrived(C_QKV + c)
                    for t in range(NT):
                        if c == 0:
                            for h in range(2):
                                pe.wait_ge(hq_free[h], l * (HQ // 2) + t + 2)
                        g = G_QKV + c * NT + t
                        group(g, tile(t), C_QKV + c, QW).then_inc(g_done, 1)
                    pe.wait_ge(g_done, l * GROUPS + g + 1)
                    pe.sem_inc(ring_free, 1)

                def gate_half(i):
                    q, h = divmod(i, 2)
                    c, t = divmod(q, NT)
                    if t == 0 and h == 0:
                        arrived(C_GATE + c)
                    last = group(G_GATE + q, tile(t), C_GATE + c, 512, 4 * h, 4 * h + 4)
                    if h:
                        last.then_inc(g_done, 1)
                        if t == NT - 1:
                            pe.wait_ge(g_done, l * GROUPS + G_GATE + q + 1)
                            pe.sem_inc(ring_free, 1)

                def gate(q):
                    gate_half(2 * q)
                    gate_half(2 * q + 1)

                gate(0)
                gate(1)
                for i in range(2 * NT):
                    t, br = divmod(i, 2)
                    kbase = (AK, CK)[br]
                    pe.wait_ge(qk_ready, l * 2 * NT + i + 1)
                    pe.wait_ge(tq_free, l * TQ + T_QK + i + 1)
                    transposes(7, [qpair[:, br, 128 * g:128 * g + 128] for g in range(3)] + [y[:, t, kbase:kbase + 128]],
                               tq_done)
                    if i % 2:
                        gate(2 + i // 2)
                gate(PRE - 1)
                for t in range(NT):
                    pe.wait_ge(v_ready, l * NT + t + 1)
                    pe.wait_ge(tq_free, l * TQ + T_MLP + t + 1)
                    for g in range(4):
                        last = nc.tensor.matmul(ps[:, 7, 64 * g:64 * g + 64], wsT[:, g],
                                                y[:, t, BV + 64 * g:BV + 64 * g + 64], start=True, stop=True)
                    last.then_inc(tq_done, 1)

                def scores(u):
                    t, br, kv, g, blocks = unit(u)
                    pe.wait_ge(e_ready, l * UNITS + u + 1)
                    r = slice(64 * kv, 64 * kv + 64)
                    q = qoT[r, 3 * br + g, 128 * t:128 * t + 128]
                    for i, b in enumerate(blocks):
                        last = nc.tensor.matmul(ps[:, 2 + i // 4, 128 * (i % 4):128 * (i % 4) + 128], q,
                                                kT[r, br, 128 * b:128 * b + 128], start=i % 4 == 0, stop=True,
                                                skip_group_check=True)
                        if br == 0 and t < NS and b in (t - 1, t + 1):
                            last = nc.tensor.matmul(ps[:, 2, 128 * i:128 * i + 128], ident[:, :],
                                                    mask[:, 0 if b < t else 1], start=False, stop=True,
                                                    skip_group_check=True)
                    last.then_inc(s_done, 1)

                def turn(u):
                    blocks = unit(u)[4]
                    pe.wait_ge(e_ready, l * UNITS + u + 2)
                    pe.wait_ge(pt_evac, l * UNITS + u + 1)
                    for i in range(len(blocks)):
                        last = nc.tensor.transpose(ps[:, 4 + i // 4, 128 * (i % 4):128 * (i % 4) + 128],
                                                   prob[:, 128 * i:128 * i + 128], ident[:, :])
                    last.then_inc(pt_done, 1)

                def weigh(u):
                    t, br, kv, g, blocks = unit(u)
                    pe.wait_ge(pt_evac, l * UNITS + u + 2)
                    pe.wait_ge(o_evac, l * UNITS + u + 1)
                    for i, b in enumerate(blocks):
                        v = cacheV[:, br, 64 * kv:64 * kv + 64] if b == NT else \
                            y[:, b, (AV, CV)[br] + 64 * kv:(AV, CV)[br] + 64 * kv + 64]
                        last = nc.tensor.matmul(ps[:, 6, 0:64], probT[:, u % 2, 128 * i:128 * i + 128], v,
                                                start=i == 0, stop=i == len(blocks) - 1)
                    last.then_inc(pv_done, 1)

                pe.wait_ge(tq_free, l * TQ + T_MLP + 1)
                for i in range(UNITS + 2):
                    if i < UNITS:
                        scores(i)
                    if 1 <= i <= UNITS:
                        turn(i - 1)
                    if i >= 2:
                        weigh(i - 2)
                    for n in range(halves_until(i - 1), halves_until(i)):
                        gate_half(2 * PRE + n)
                pe.wait_ge(o_evac, l * UNITS + UNITS + 1)
                for t in range(NT):
                    parts = [y[:, t, AQ + 128 * i:AQ + 128 * i + 128] for i in range(3)] + \
                            [y[:, t, CQ + 128 * i:CQ + 128 * i + 128] for i in range(3)] + \
                            [y[:, t, BU + 128 * i:BU + 128 * i + 128] for i in range(2)]
                    for h in range(2):
                        pe.wait_ge(tq_free, l * TQ + T_O + 2 * t + h + 1)
                        transposes(7, parts[4 * h:4 * h + 4], tq_done)
                pe.wait_ge(tq_free, l * TQ + TQ + 1)
                pe.wait_ge(pt_evac, l * UNITS + UNITS + 1)
                for n in range(2):
                    arrived(C_OUT + n)
                    for t in range(NT):
                        o = n * NT + t
                        pe.wait_ge(opj_free, l * 2 * NT + o + 1)
                        for b, ks in enumerate(((0, 1, 2), (6, 7), (3, 4, 5))):
                            for k in ks:
                                last = nc.tensor.matmul(ps[:, 2 + 3 * (o % 2) + b], qoT[:, k, 128 * t:128 * t + 128],
                                                        ring[:, (C_OUT + n) % RING, k], start=k == ks[0], stop=k == ks[-1])
                        last.then_inc(opj_done, 1)
                    pe.wait_ge(opj_done, l * 2 * NT + o + 1)
                    pe.sem_inc(ring_free, 1)
                pe.wait_ge(merged_ready, l * 2 * NT + 2 * NT)
                h_tiles(H_M, lambda t: merged[:, t], lambda t: None, None)
                def h2_tile(t):
                    pe.wait_ge(xn_ready, l * 2 * NT + NT + t + 1)
                    for h in range(2):
                        pe.wait_ge(hq_free[h], l * (HQ // 2) + (2 * NT + t + 1))
                        transposes(2 + h, [xn[:, t % 2, 128 * k:128 * k + 128] for k in range(4 * h, 4 * h + 4)], hq_done)

                def route(t):
                    for h in range(2):
                        pe.wait_ge(hq_free[h], l * (HQ // 2) + 2 * NT + t + 2)
                    if t == 0:
                        arrived(C_ROUT)
                    for k in range(KB):
                        last = nc.tensor.matmul(ps[:, 6, E * t:E * t + E], HT[:, k, 128 * t:128 * t + 128],
                                                ring[:, C_ROUT % RING, k, 0:E], start=k == 0, stop=k == KB - 1)
                    return last

                for c in range(2):
                    arrived(C_WO + c)
                    for t in range(NT):
                        if c == 0:
                            for h in range(2):
                                pe.wait_ge(hq_free[h], l * (HQ // 2) + NT + t + 2)
                        g = G_WO + c * NT + t
                        group(g, tile(t), C_WO + c, 512).then_inc(g_done, 1)
                        if c and t >= 2:
                            h2_tile(t - 2)
                            if t >= 3:
                                route(t - 3)
                    pe.wait_ge(g_done, l * GROUPS + g + 1)
                    pe.sem_inc(ring_free, 1)
                for t in (NT - 2, NT - 1):
                    h2_tile(t)
                    route(t - 1)
                route(NT - 1).then_inc(rt_done, 1)
                pe.wait_ge(rt_done, l + 1)
                pe.sem_inc(ring_free, 1)
                pe.wait_ge(aff_ready, l + 1)
                for t in range(NT):
                    last = nc.tensor.transpose(ps[0:E, 7 if t < NS else 6, 128 * (t % NS):128 * (t % NS) + 128],
                                               aff[:, t], ident[:, :])
                last.then_inc(afft_done, 1)
                pe.wait_ge(slots_ready, l + 1)
                settle(pe, 0)
                for a in range(4):
                    last = nc.tensor.transpose(ps[:, 7, E * a:E * a + E], slots[:, a], ident[0:E, 0:E])
                last.then_inc(slott_done, 1)

                def turn_rows(j, b, use, n):
                    pe.wait_ge(xg_ready[b], l * (32 * PAIRS) + (j * 32 + 32))
                    for h in range(2):
                        pe.wait_ge(mq_free[h], l * 32 + use + 1)
                        transposes(4 + h, [xg[:, b, 512 * h + 128 * i:512 * h + 128 * i + 128] for i in range(4)], mq_done)
                    pe.wait_ge(mq_done, l * 64 + n + 2)
                    pe.sem_inc(xt_done, 1)

                def chunk(n, u0, lhs, bank):
                    for half in range(2):
                        pe.wait_ge(lo_ready, l * UNITS_E + n + (half + 2))
                        for k in range(4):
                            kb, u = 4 * half + k, u0 + half
                            for i, (a, w) in enumerate(((0, w_hi), (0, w_lo), (1, w_hi))):
                                last = nc.tensor.matmul(ps[:, bank], lhs[:, a, kb], w[:, u, k],
                                                        start=kb == 0 and i == 0, stop=kb == KB - 1 and i == 2)
                        last.then_inc(unit_used, 1)

                def scatter(j):
                    pe.wait_ge(hot_ready, l * PAIRS + j + 1)
                    pe.wait_ge(os_ready, l * 32 + (4 * j + 4))
                    for t in range(NT):
                        for h in range(2):
                            pe.wait_ge(sc_free[h], l * (5 * PAIRS) + (j * 5 + t + 1))
                            lhs, src = (hots[:, 128 * t:128 * t + 128], osam) if t < NS else (hotp[:, :], opro)
                            nc.tensor.matmul(ps[:, 6 + h], lhs, src[:, 512 * h:512 * h + 512],
                                             start=True, stop=True).then_inc(sc_done, 1)

                def step(j, b, first, last_pair):
                    e = 2 * j + b
                    start = b == 0 and first
                    n = 0 if start else 12 * e - 4
                    for h in range(2):
                        pe.wait_ge(mq_free[h], l * 32 + (2 if start else 2 * e + 1))
                    for h in range(2):
                        pe.wait_ge(out_evac[h], l * E + (e + 1))
                        chunk(n + 4 * h, 0, xT, h)
                        chunk(n + 4 * h + 2, 2, xT, 2 + h)
                    if not (b and last_pair):
                        turn_rows(j + b, 1 - b, 2 * e + 1, 4 * e + 2)
                    if b and not first:
                        scatter(j - 1)
                    if not start:
                        down(e, n + 8)
                    for h in range(2):
                        pe.wait_ge(hh_ready, l * 32 + (2 * e + h + 1))
                        pe.wait_ge(mq_free[h], l * 32 + (2 * e + (2 if b and last_pair else 3)))
                        transposes(4 + h, [hh[:, 512 * h + 128 * i:512 * h + 128 * i + 128] for i in range(4)], mq_done)

                def down(e, n):
                    for h in range(2):
                        pe.wait_ge(mq_free[h], l * 32 + (2 * e + 2))
                    for h in range(2):
                        pe.wait_ge(sil_ready, l * 32 + (2 * e + h + 1))
                        chunk(n + 2 * h, 2 * h, hT, h)

                pe.wait_ge(moe_init, l * 2 + 2)
                turn_rows(0, 0, 0, 0)
                step(0, 0, True, False)
                step(0, 1, True, False)
                with pe.Fori(1, PAIRS - 1) as j:
                    step(j, 0, False, False)
                    step(j, 1, False, False)
                step(PAIRS - 1, 0, False, True)
                step(PAIRS - 1, 1, False, True)
                for h in range(2):
                    pe.wait_ge(mq_free[h], l * 32 + 33)
                for h in range(2):
                    pe.wait_ge(out_evac[h], l * E + E + 1)
                    chunk(UNITS_E - 4 + 2 * h, 2 * h, hT, h)
                scatter(PAIRS - 1)

        @block.scalar
        def _(act):
            act.sem_inc(e_ready, 1)
            act.sem_inc(out_evac[0], 2)
            act.sem_inc(out_evac[1], 2)
            act.wait_ge(in_ready, 80)
            nc.scalar.activation(condrow, condrow, ACT.Silu).then_inc(cond_silu, 1)
            act.wait_ge(cond_ready, 1)
            with act.Fori(0, DEPTH) as l:
                def square(i, t):
                    act.wait_ge(ss_ready, l * 2 * NT + (i * NT + t + 1))
                    nc.scalar.activation(junk, x[:, t], ACT.Square, accum_out=st5[:, t:t + 1]).then_inc(ss_ready, 1)

                def root(i, out, src):
                    act.wait_ge(ms_ready, l * ROOTS + i + 1)
                    nc.scalar.activation(out, src, ACT.Sqrt).then_inc(sd_ready, 1)

                act.wait_ge(sc_free[0], l * 5 * PAIRS + 1)
                act.wait_ge(sc_free[1], l * 5 * PAIRS + 1)
                for t in range(NT):
                    square(0, t)
                for t in range(NT):
                    root(t, rs5[:, t:t + 1], st5[:, t:t + 1])
                act.wait_ge(tq_free, l * TQ + T_MOD + 2)
                for t in range(NT):
                    s = 0 if t < NS else 1
                    act.wait_ge(hq_done, l * HQ + 2 * t + 1)
                    for k in range(4):
                        last = nc.scalar.activation(HT[:, k, 128 * t:128 * t + 128], ps[:, 2, 128 * k:128 * k + 128],
                                                    ACT.Identity, bias=modcol[:, 0, k, s:s + 1],
                                                    scale=modcol[:, 1, k, s:s + 1])
                    last.then_inc(hq_free[0], 1)
                act.wait_ge(tq_done, l * TQ + T_WS + 1)
                nc.scalar.activation(wsT.rearrange("p g n -> p (g n)"), ps[:, 7], ACT.Copy).then_inc(tq_free, 1)
                act.wait_ge(tq_done, l * TQ + T_CK + 1)
                nc.scalar.activation(kT[:, :, 640:768], ps[:, 7, 0:256].rearrange("p (b n) -> p b n", b=2),
                                     ACT.Copy).then_inc(tq_free, 1)
                for g in range(G_QKV, G_GATE):
                    c, t = divmod(g - G_QKV, NT)
                    if g % 2 == 0:
                        act.wait_ge(g_done, l * GROUPS + g + 1)
                        if g == G_QKV:
                            act.wait_ge(g_saved, l * 64 + 64)
                        nc.scalar.activation(y[:, t, QW * c:QW * c + QW], ps[:, 0, 0:QW], ACT.Copy).then_inc(g_free[0], 1)
                for b in range(2):
                    act.wait_ge(g_free[b], l * (GROUPS // 2) + G_GATE // 2 + 1)
                for t in range(NT):
                    nc.scalar.activation(y[:, t, BU:BU + 512], y[:, t, BU:BU + 512], ACT.Gelu_apprx_tanh).then_inc(gelu_ready, 1)

                def gate(q):
                    c, t = divmod(q, NT)
                    g = G_GATE + q
                    act.wait_ge(g_done, l * GROUPS + g + 1)
                    if q == 0:
                        act.wait_ge(x_saved, l * 16 + 16)
                    nc.scalar.activation(gates(t, c), ps[:, g % 2], ACT.Tanh, scale=0.5).then_inc(g_free[g % 2], 1)

                gate(0)
                gate(1)
                root(NT, rs100[:, :, :], st100[:, :, :])
                for i in range(2 * NT):
                    t, br = divmod(i, 2)
                    act.wait_ge(tq_done, l * TQ + T_QK + i + 1)
                    nc.scalar.activation(qoT[:, 3 * br:3 * br + 3, 128 * t:128 * t + 128],
                                         ps[:, 7, 0:384].rearrange("p (s n) -> p s n", s=3), ACT.Copy)
                    nc.scalar.activation(kT[:, br, 128 * t:128 * t + 128], ps[:, 7, 384:512], ACT.Copy).then_inc(tq_free, 1)
                    if i % 2:
                        gate(2 + i // 2)
                gate(PRE - 1)
                for i in range(UNITS + 2):
                    if i < UNITS:
                        t, br, kv, g, blocks = unit(i)
                        n = 128 * len(blocks)
                        act.wait_ge(nm_ready, l * UNITS + i + 1)
                        act.wait_ge(pt_done, l * UNITS + i + 1)
                        nc.scalar.activation(prob[:, 0:n], ps[:, 2:4].rearrange("p b n -> p (b n)")[:, 0:n], ACT.Exp,
                                             bias=nm[:, i % 2:i % 2 + 1], scale=SCALE,
                                             accum_out=sm[:, i % 2:i % 2 + 1]).then_inc(e_ready, 1)
                        if br == 0:
                            h = 3 * kv + g
                            nc.scalar.activation(es[:, i % 2:i % 2 + 1], sink[:, h:h + 1], ACT.Exp,
                                                 bias=nm[:, i % 2:i % 2 + 1]).then_inc(es_ready, 1)
                    u = i - 1
                    if 0 <= u < UNITS and u % 2:
                        n = 128 * len(unit(u)[4])
                        act.wait_ge(pt_done, l * UNITS + u + 2)
                        act.wait_ge(pv_done, l * UNITS + u + 1)
                        nc.scalar.activation(probT[:, 1, 0:n], ps[:, 4:6].rearrange("p b n -> p (b n)")[:, 0:n],
                                             ACT.Copy).then_inc(pt_evac, 1)
                    for n in range(halves_until(i - 1), halves_until(i)):
                        if n % 2:
                            gate(PRE + n // 2)
                for i in range(2 * NT):
                    t, h = divmod(i, 2)
                    act.wait_ge(tq_done, l * TQ + T_O + i + 1)
                    nc.scalar.activation(qoT[:, 4 * h:4 * h + 4, 128 * t:128 * t + 128],
                                         ps[:, 7].rearrange("p (s n) -> p s n", s=4), ACT.Copy).then_inc(tq_free, 1)
                for t in range(NT):
                    act.wait_ge(hq_done, l * HQ + H_M + 2 * t + 1)
                    nc.scalar.activation(HT[:, 0:4, 128 * t:128 * t + 128], ps[:, 2].rearrange("p (s n) -> p s n", s=4),
                                         ACT.Copy, scale=0.5).then_inc(hq_free[0], 1)
                def h2_out(t):
                    act.wait_ge(hq_done, l * HQ + H_2 + 2 * t + 1)
                    nc.scalar.activation(HT[:, 0:4, 128 * t:128 * t + 128], ps[:, 2].rearrange("p (s n) -> p s n", s=4),
                                         ACT.Copy).then_inc(hq_free[0], 1)

                for t in range(NT):
                    act.wait_ge(x_ready, l * 2 * NT + NT + t + 1)
                    square(1, t)
                    root(NT + 1 + t, rs5[:, t:t + 1], st5[:, t:t + 1])
                    if t >= 2:
                        h2_out(t - 2)
                h2_out(NT - 2)
                h2_out(NT - 1)
                act.wait_ge(lg_ready, l + 1)
                nc.scalar.activation(aff, aff, ACT.Exp).then_inc(pe_ready, 1)

                def hi(n, u, raw):
                    act.wait_ge(ring_ready[raw[0]], l * (16 * LOADS) + 16 * (raw[1] + C_MOE // RING + 1))
                    act.wait_ge(unit_used, l * UNITS_E + (n + 1))
                    nc.scalar.activation(w_hi[:, u % UB], ring[:, raw[0], 4 * (u % 2):4 * (u % 2) + 4],
                                         ACT.Copy).then_inc(hi_ready, 1)

                def used(n):
                    act.wait_ge(unit_used, l * UNITS_E + (n + 1 + UB))

                def parts(dst, n):
                    for h in range(2):
                        act.wait_ge(mq_done, l * 64 + (n + h + 1))
                        nc.scalar.activation(dst[:, 0, 4 * h:4 * h + 4], ps[:, 4 + h].rearrange("p (k n) -> p k n", k=4),
                                             ACT.Copy).then_inc(mq_hi, 1)

                def outputs(e, b, h, n):
                    used(n)
                    settle(act, 1)
                    c = slice(512 * h, 512 * h + 512)
                    for r, dst in ((slice(0, 64), (osam, opro)[b]), (slice(64, 128), (opro, osam)[b])):
                        last = nc.scalar.activation(dst[r, c], ps[r, h], ACT.Copy, scale=colv[r, bass.ds(e, 1)])
                    last.then_inc(out_evac[h], 1)

                def step(j, b, first, last_pair):
                    e = 2 * j + b
                    start = b == 0 and first
                    n = 0 if start else 12 * e - 4
                    for s in range(8 if start else 12):
                        if s == 0 and not (first and b < 2):
                            outputs(e - 2, b, 1, n - 1)
                        hi(n + s + AHEAD, s + AHEAD, raw_of(j, b, first, s + AHEAD))
                        if s == 1 and not start:
                            parts(hT, 4 * e)
                        if s in (2, 6):
                            used(n + s - 1)
                            nc.scalar.activation(sil[:, s // 4], ps[:, s // 4], ACT.Silu).then_inc(sil_ready, 1)
                        if s == (7 if start else 8) and not (b and last_pair):
                            parts(xT, 4 * e + 2)
                        if s == 10:
                            outputs(e - 1, 1 - b, 0, n + 9)

                act.wait_ge(moe_init, l * 2 + 2)
                for u in range(AHEAD):
                    hi(u, u, raw_of(0, 0, True, u))
                parts(xT, 0)
                act.wait_ge(idx_ready, l + 1)
                step(0, 0, True, False)
                step(0, 1, True, False)
                with act.Fori(1, PAIRS - 1) as j:
                    step(j, 0, False, False)
                    step(j, 1, False, False)
                step(PAIRS - 1, 0, False, True)
                step(PAIRS - 1, 1, False, True)
                outputs(E - 2, 0, 1, UNITS_E - 5)
                hi(UNITS_E - 1, 3, raw_of(PAIRS - 1, 1, False, 15))
                parts(hT, 62)
                outputs(E - 1, 1, 0, UNITS_E - 3)
                outputs(E - 1, 1, 1, UNITS_E - 1)

        @block.vector
        def _(dve):
            for s in (g_free[0], g_free[1], tq_free, hq_free[0], hq_free[1], pt_evac, o_evac, mq_free[0], mq_free[1],
                      lo_ready, ss_ready):
                dve.sem_inc(s, 1)
            dve.sem_inc(opj_free, 2)
            dve.wait_ge(in_ready, 80)
            dve.sem_inc(sc_free[0], 1)
            dve.sem_inc(sc_free[1], 1)
            dve.wait_ge(cond_done, 1)
            nc.vector.tensor_copy(condT[:, :], ps[:, 7, 0:16]).then_inc(cond_ready, 1)
            steps = [0]
            TT, TS, STT = nc.vector.tensor_tensor, nc.vector.tensor_scalar, nc.vector.scalar_tensor_tensor
            with dve.Fori(0, DEPTH) as l:
                def link(ins):
                    steps[0] += 1
                    ins.then_inc(dve_step, 1)
                    dve.wait_ge(dve_step, l * DVE_STEPS + steps[0])

                def link_top(ins):
                    link(ins)
                    settle(dve, 3)

                def h_out(t):
                    s = 0 if t < NS else 1
                    dve.wait_ge(hq_done, l * HQ + 2 * t + 2)
                    for k in range(4):
                        last = TS(HT[:, 4 + k, 128 * t:128 * t + 128], ps[:, 3, 128 * k:128 * k + 128],
                                  modcol[:, 1, 4 + k, s:s + 1], modcol[:, 0, 4 + k, s:s + 1], ALU.mult, ALU.add)
                    last.then_inc(hq_free[1], 1)

                dve.wait_ge(par_ready, l * 16 * PARS + 16 * PARS)
                for c in range(NMOD):
                    dve.wait_ge(g_done, l * GROUPS + c + 1)
                    TT(modrow[:, 512 * c:512 * c + 512], ps[0:2, c % 2], bmod[:, 512 * c:512 * c + 512],
                       ALU.add).then_inc(g_free[c % 2], 1)
                for b in range(2):
                    dve.wait_ge(g_free[b], l * (GROUPS // 2) + NMOD // 2 + 1)
                link(STT(modrow[:, D:2 * D], modrow[:, D:2 * D], 1.0, nrow[:, 0], ALU.add, ALU.mult))
                STT(modrow[:, 4 * D:5 * D], modrow[:, 4 * D:5 * D], 1.0, nrow[:, 1], ALU.add, ALU.mult).then_inc(mod_ready, 1)
                link(TS(nsink[:, :], sink[:, :], -1.0, None, ALU.mult))
                dve.wait_ge(tq_done, l * TQ + T_MOD + 1)
                nc.vector.tensor_copy(modcol.rearrange("p a k s -> p (a k s)"), ps[:, 7, 0:32]).then_inc(tq_free, 1)

                def mean(i, t):
                    dve.wait_ge(ss_ready, l * 2 * NT + (i * NT + t + 2))
                    TS(st5[:, t:t + 1], st5[:, t:t + 1], 1.0 / D, EPS, ALU.mult, ALU.add).then_inc(ms_ready, 1)

                for t in range(NT):
                    mean(0, t)
                for t in range(NT):
                    dve.wait_ge(sd_ready, l * ROOTS + t + 1)
                    link(nc.vector.reciprocal(rs5[:, t:t + 1], rs5[:, t:t + 1]))
                    if t >= 2:
                        dve.wait_ge(hq_done, l * HQ + 2 * (t - 1))
                    if t == 0:
                        dve.wait_ge(tq_free, l * TQ + T_MOD + 2)
                    TS(xn[:, t % 2], x[:, t], rs5[:, t:t + 1], None, ALU.mult).then_inc(xn_ready, 1)
                    if t:
                        h_out(t - 1)
                h_out(NT - 1)
                for g in range(G_QKV, G_GATE):
                    c, t = divmod(g - G_QKV, NT)
                    if g % 2:
                        dve.wait_ge(g_done, l * GROUPS + g + 1)
                        if g == G_QKV + 1:
                            dve.wait_ge(g_saved, l * 64 + 64)
                        nc.vector.tensor_copy(y[:, t, QW * c:QW * c + QW], ps[:, 1, 0:QW]).then_inc(g_free[1], 1)
                for b in range(2):
                    dve.wait_ge(g_free[b], l * (GROUPS // 2) + G_GATE // 2 + 1)
                dve.wait_ge(tq_free, l * TQ + T_CK + 2)
                heads = lambda a, n: a.rearrange("p (h d) -> p h d", h=n)
                for t in range(NT):
                    for br, base in ((0, AQ), (1, CQ)):
                        yb = y[:, t, base:base + 512]
                        link(TT(tmp[0], yb, yb, ALU.mult))
                        link(nc.vector.tensor_reduce(st100[:, t, 8 * br:8 * br + 8], heads(tmp[0], 8), axis=AX.X, op=ALU.add))
                    dve.wait_ge(gelu_ready, l * NT + t + 1)
                    v = y[:, t, BV:BV + 256]
                    link(TT(tmp[1][:, 0:256], v, v, ALU.mult))
                    link(nc.vector.tensor_reduce(st100[:, t, 16:20], heads(tmp[1][:, 0:256], 4), axis=AX.X, op=ALU.add))
                TS(st100[:, :, :], st100[:, :, :], 1.0 / HD, EPS, ALU.mult, ALU.add).then_inc(ms_ready, 1)
                dve.wait_ge(sd_ready, l * ROOTS + NT + 1)
                link(nc.vector.reciprocal(rs100[:, :, :], rs100[:, :, :]))
                for t in range(NT):
                    for br, base in ((0, AQ), (1, CQ)):
                        yb = y[:, t, base:base + 512]
                        yh = heads(yb, 8)
                        link(TT(yh, yh, rs100[:, t, 8 * br:8 * br + 8, None].to_broadcast([128, 8, HD]), ALU.mult))
                        link(TT(yh[:, 0:6], yh[:, 0:6], gain[:, br, 0:1].to_broadcast([128, 6, HD]), ALU.mult))
                        link(TT(yh[:, 6:8], yh[:, 6:8], gain[:, br, 1:2].to_broadcast([128, 2, HD]), ALU.mult))
                        y4 = yb.rearrange("p (h a b c) -> p h a b c", h=8, a=2, b=2)
                        t4 = tmp[0].rearrange("p (h a b c) -> p h a b c", h=8, a=2, b=2)
                        s4 = rope[:, 1, t].rearrange("p (a b c) -> p a b c", a=2, b=2)
                        for b in range(2):
                            link(TT(t4[:, :, :, b], y4[:, :, :, 1 - b],
                                    s4[:, None, :, b].to_broadcast([128, 8, 2, 16]), ALU.mult))
                        link(TT(yh, yh, rope[:, 0, t:t + 1].to_broadcast([128, 8, HD]), ALU.mult))
                        if t:
                            dve.wait_ge(tq_done, l * TQ + T_QK + 2 * t + br - 1)
                        pair3 = lambda a, o: a.rearrange(o, v=2, g=3)
                        TT(pair3(qpair[:, br], "p (g v d) -> p v g d"), pair3(yb[:, 0:384], "p (v g d) -> p v g d"),
                           pair3(tmp[0][:, 0:384], "p (v g d) -> p v g d"), ALU.add)
                        TT(yb[:, 384:512], yb[:, 384:512], tmp[0][:, 384:512], ALU.add).then_inc(qk_ready, 1)
                        dve.wait_ge(qk_ready, l * 2 * NT + 2 * t + br + 1)
                for t in range(NT):
                    v = y[:, t, BV:BV + 256]
                    link(TT(heads(v, 4), heads(v, 4), rs100[:, t, 16:20, None].to_broadcast([128, 4, HD]), ALU.mult))
                    TT(v, v, vgain[:, :], ALU.mult).then_inc(v_ready, 1)
                for t in range(NT):
                    dve.wait_ge(tq_done, l * TQ + T_MLP + t + 1)
                    for g in range(4):
                        u = y[:, t, BU + 64 * g:BU + 64 * g + 64]
                        last = STT(u, ps[:, 7, 64 * g:64 * g + 64], bs[:, g:g + 1], u, ALU.add, ALU.mult)
                    last.then_inc(tq_free, 1)
                for i in range(UNITS + 2):
                    if i < UNITS:
                        t, br, kv, g, blocks = unit(i)
                        n = 128 * len(blocks)
                        h = 3 * kv + g
                        dve.wait_ge(s_done, l * UNITS + i + 1)
                        link(nc.vector.reduce_max(mx[:, :], ps[:, 2:4].rearrange("p b n -> p (b n)")[:, 0:n], AX.X))
                        if br == 0:
                            TS(nm[:, i % 2:i % 2 + 1], mx[:, :], -SCALE, nsink[:, h:h + 1], ALU.mult, ALU.min).then_inc(nm_ready, 1)
                        else:
                            TS(nm[:, i % 2:i % 2 + 1], mx[:, :], -SCALE, None, ALU.mult).then_inc(nm_ready, 1)
                    u = i - 1
                    if 0 <= u < UNITS:
                        t, br, kv, g, blocks = unit(u)
                        if u % 2 == 0:
                            n = 128 * len(blocks)
                            dve.wait_ge(pt_done, l * UNITS + u + 2)
                            dve.wait_ge(pv_done, l * UNITS + u + 1)
                            nc.vector.tensor_copy(probT[:, 0, 0:n],
                                                  ps[:, 4:6].rearrange("p b n -> p (b n)")[:, 0:n]).then_inc(pt_evac, 1)
                        dve.wait_ge(e_ready, l * UNITS + u + 2)
                        if u >= 2:
                            dve.wait_ge(o_evac, l * UNITS + u)
                        if br == 0:
                            dve.wait_ge(es_ready, l * (NT * 6) + t * 6 + u % 12 + 1)
                            link(TT(den[:, :], sm[:, u % 2:u % 2 + 1], es[:, u % 2:u % 2 + 1], ALU.add))
                            link(nc.vector.reciprocal(rden[:, u % 2:u % 2 + 1], den[:, :]))
                        else:
                            link(nc.vector.reciprocal(rden[:, u % 2:u % 2 + 1], sm[:, u % 2:u % 2 + 1]))
                    u = i - 2
                    if u >= 0:
                        t, br, kv, g, _ = unit(u)
                        h = 3 * kv + g
                        dve.wait_ge(pv_done, l * UNITS + u + 3)
                        TS(y[:, t, (AQ, CQ)[br] + 64 * h:(AQ, CQ)[br] + 64 * h + 64], ps[:, 6, 0:64],
                           rden[:, u % 2:u % 2 + 1], None, ALU.mult).then_inc(o_evac, 1)
                dve.wait_ge(kv_saved, l * 64 + 64)
                for o in range(2 * NT):
                    n, t = divmod(o, NT)
                    m = merged[:, t, 512 * n:512 * n + 512]
                    b = 2 + 3 * (o % 2)
                    dve.wait_ge(opj_done, l * 2 * NT + o + 1)
                    link(STT(m, gates(t, 3 * n), 1.0, ps[:, b], ALU.add, ALU.mult))
                    link(STT(tmp[0], gates(t, 3 * n + 1), 1.0, ps[:, b + 1], ALU.add, ALU.mult))
                    STT(tmp[1], gates(t, 3 * n + 2), 1.0, ps[:, b + 2], ALU.add, ALU.mult).then_inc(opj_free, 1)
                    dve.wait_ge(opj_free, l * 2 * NT + o + 3)
                    link(TT(m, m, tmp[0], ALU.add))
                    TT(m, m, tmp[1], ALU.add).then_inc(merged_ready, 1)
                    dve.wait_ge(merged_ready, l * 2 * NT + o + 1)
                for t in range(NT):
                    dve.wait_ge(hq_done, l * HQ + H_M + 2 * t + 2)
                    TS(HT[:, 4:8, 128 * t:128 * t + 128], ps[:, 3].rearrange("p (s n) -> p s n", s=4), 0.5, None,
                       ALU.mult).then_inc(hq_free[1], 1)
                dve.wait_ge(x_back, l * 16 + 16)
                dve.wait_ge(g1_ready, l * 32 + 32)
                dve.wait_ge(mb_ready, l * 64 + 64)

                def h2(t):
                    s = 0 if t < NS else 1
                    mean(1, t)
                    dve.wait_ge(sd_ready, l * ROOTS + NT + 1 + t + 1)
                    link(nc.vector.reciprocal(rs5[:, t:t + 1], rs5[:, t:t + 1]))
                    if t >= 2:
                        dve.wait_ge(hq_done, l * HQ + H_2 + 2 * (t - 1))
                        dve.wait_ge(xn_saved[t % 2], l * (16 * ((NT + 1 - t % 2) // 2)) + 16 * (t // 2))
                    link(STT(xn[:, t % 2], x[:, t], rs5[:, t:t + 1], modbc[:, 1, s], ALU.mult, ALU.mult))
                    TT(xn[:, t % 2], xn[:, t % 2], modbc[:, 0, s], ALU.add).then_inc(xn_ready, 1)

                def h2_out(t):
                    dve.wait_ge(hq_done, l * HQ + H_2 + 2 * t + 2)
                    nc.vector.tensor_copy(HT[:, 4:8, 128 * t:128 * t + 128],
                                          ps[:, 3].rearrange("p (s n) -> p s n", s=4)).then_inc(hq_free[1], 1)

                for c in range(2):
                    for t in range(NT):
                        g = G_WO + c * NT + t
                        s = 0 if t < NS else 1
                        dve.wait_ge(g_done, l * GROUPS + g + 1)
                        TT(tmp[0], ps[:, g % 2], g1bc[:, s, 512 * c:512 * c + 512], ALU.mult).then_inc(g_free[g % 2], 1)
                        dve.wait_ge(g_free[g % 2], l * (GROUPS // 2) + g // 2 + 2)
                        TT(x[:, t, 512 * c:512 * c + 512], x[:, t, 512 * c:512 * c + 512], tmp[0], ALU.add).then_inc(x_ready, 1)
                        dve.wait_ge(x_ready, l * 2 * NT + NT * c + t + 1)
                        if c:
                            h2(t)
                            if t >= 2:
                                h2_out(t - 2)
                h2_out(NT - 2)
                h2_out(NT - 1)

                dve.wait_ge(rt_done, l + 1)
                bc = lambda a: a[:, :, None].to_broadcast([128, NT, E])
                link(TT(aff, ps[:, 6, 0:NT * E].rearrange("p (t e) -> p t e", t=NT), brt[:, None, :].to_broadcast([128, NT, E]), ALU.add))
                link(nc.vector.tensor_reduce(rmax, aff, axis=AX.X, op=ALU.max))
                TT(aff, aff, bc(rmax), ALU.subtract).then_inc(lg_ready, 1)
                dve.wait_ge(pe_ready, l + 1)
                link(nc.vector.tensor_reduce(rsum, aff, axis=AX.X, op=ALU.add))
                link(nc.vector.reciprocal(rrec, rsum))
                TT(aff, aff, bc(rrec), ALU.mult).then_inc(aff_ready, 1)
                dve.wait_ge(afft_done, l + 1)
                nc.vector.tensor_copy(affT[:, 0:512], ps[0:E, 7])
                link(nc.vector.tensor_copy(affT[:, 512:640], ps[0:E, 6, 0:128]))
                link(nc.vector.memset(slots[:, 2], -1.0))
                link_top(nc.vector.memset(slots[:, 3], 0.0))
                for a, lo, n, cap in ((2, 512, 128, CP), (0, 0, 512, CS)):
                    w = affT[:, lo:lo + n]
                    for r in range(0, cap, 8):
                        link_top(nc.vector.max(out=topv[:, r:r + 8], in_=w))
                        link_top(nc.vector.max_index(out=topi[:, r:r + 8], in_max=topv[:, r:r + 8], in_values=w))
                        if r + 8 < cap:
                            link_top(nc.vector.match_replace(out=w, in_to_replace=topv[:, r:r + 8], in_values=w, imm_value=-1.0e30))
                    for h in range(2):
                        nc.vector.tensor_copy(slots[:, a, 64 * h:64 * h + cap], topi[:, 0:cap])
                        link_top(nc.vector.tensor_copy(slots[:, a + 1, 64 * h:64 * h + cap], topv[:, 0:cap]))
                dve.sem_inc(slots_ready, 1)
                dve.wait_ge(slott_done, l + 1)
                link(nc.vector.tensor_copy(slotT.rearrange("p a e -> p (a e)"), ps[:, 7, 0:64]))
                ev = lambda a, h: a.rearrange("p (j b) -> p b j", b=2)[:, h]
                for h in range(2):
                    r = slice(64 * h, 64 * h + 64)
                    nc.vector.tensor_copy(cols[r, :], ev(slotT[r, 0], h))
                    nc.vector.tensor_copy(colp[r, :], ev(slotT[r, 2], 1 - h))
                    nc.vector.tensor_copy(ev(colv[r, :], h), ev(slotT[r, 1], h))
                    link(nc.vector.tensor_copy(ev(colv[r, :], 1 - h), ev(slotT[r, 3], 1 - h)))
                nc.vector.tensor_copy(idxs[0:CS, :], slotT[0:CS, 0])
                TS(idxp[0:CP, :], slotT[0:CP, 2], 512.0, None, ALU.add).then_inc(idx_ready, 1)
                dve.wait_ge(moe_init, l * 2 + 2)
                if steps[0] != DVE_STEPS:
                    raise ValueError(f"DVE_STEPS {steps[0]}")

                def lo(n, u, raw):
                    dve.wait_ge(hi_ready, l * UNITS_E + (n + 1))
                    TT(w_lo[:, u % UB], ring[:, raw[0], 4 * (u % 2):4 * (u % 2) + 4], w_hi[:, u % UB].bitcast(f32),
                       ALU.subtract).then_inc(lo_ready, 1)

                def parts(dst, n):
                    for h in range(2):
                        dve.wait_ge(mq_hi, l * 64 + (n + h + 1))
                        TT(dst[:, 1, 4 * h:4 * h + 4], ps[:, 4 + h].rearrange("p (k n) -> p k n", k=4),
                           dst[:, 0, 4 * h:4 * h + 4].bitcast(f32), ALU.subtract).then_inc(mq_free[h], 1)

                def gathered(j):
                    for t in range(NT):
                        for h in range(2):
                            dve.wait_ge(sc_done, l * 80 + (10 * j + 2 * t + h + 1))
                            dve.wait_ge(sc_free[h], l * (5 * PAIRS) + (5 * j + t + 1))
                            xt = x[:, t, 512 * h:512 * h + 512]
                            TT(xt, xt, ps[:, 6 + h], ALU.add).then_inc(sc_free[h], 1)

                def onehot(j):
                    TS(hots[:, :], iota[:, :], cols[:, bass.ds(j, 1)], None, ALU.is_equal)
                    TS(hotp[:, :], iota[:, 0:128], colp[:, bass.ds(j, 1)], None, ALU.is_equal).then_inc(hot_ready, 1)

                def step(j, b, first, last_pair):
                    e = 2 * j + b
                    start = b == 0 and first
                    n = 0 if start else 12 * e - 4
                    for s in range(8 if start else 12):
                        if s in (4, 8) or (s == 7 and start):
                            h = 0 if s == 4 else 1
                            dve.wait_ge(sil_ready, l * 32 + (2 * e + h + 1))
                            dve.wait_ge(unit_used, l * UNITS_E + (n + 4 * h + 4 + UB))
                            TT(hh[:, 512 * h:512 * h + 512], sil[:, h], ps[:, 2 + h], ALU.mult).then_inc(hh_ready, 1)
                        if s == 8 and b and not first:
                            gathered(j - 1)
                        lo(n + s + AHEAD, s + AHEAD, raw_of(j, b, first, s + AHEAD))
                        if s == 2 and not start:
                            parts(hT, 4 * e)
                        if s == 5 and b == 0 and not first:
                            onehot(j - 1)
                        if s == (7 if start else 9) and not (b and last_pair):
                            parts(xT, 4 * e + 2)

                for u in range(AHEAD):
                    lo(u, u, raw_of(0, 0, True, u))
                parts(xT, 0)
                step(0, 0, True, False)
                step(0, 1, True, False)
                with dve.Fori(1, PAIRS - 1) as j:
                    step(j, 0, False, False)
                    step(j, 1, False, False)
                step(PAIRS - 1, 0, False, True)
                step(PAIRS - 1, 1, False, True)
                lo(UNITS_E - 1, 3, raw_of(PAIRS - 1, 1, False, 15))
                parts(hT, 62)
                onehot(PAIRS - 1)
                gathered(PAIRS - 1)


def kernel(**inputs):
    import numpy as np
    import concourse.bacc as bacc
    from concourse.bass_utils import run_bass_kernel_spmd as run

    a = {k: np.asarray(v) for k, v in inputs.items()}
    a["w_o"] = np.concatenate([a.pop("w_a_o"), a.pop("w_c_o"), a.pop("w_b_o")], axis=1)
    a["qk_gain"] = np.concatenate([a.pop("a_q_norm"), a.pop("a_k_norm"), a.pop("c_q_norm"), a.pop("c_k_norm")], axis=1)
    flat = lambda v: v[0].reshape(DEPTH, 128, 128)
    a["cache_k"] = np.stack([flat(a.pop("cache_a_k")), flat(a.pop("cache_c_k"))], axis=2)
    a["cache_v"] = np.stack([flat(a.pop("cache_a_v")), flat(a.pop("cache_c_v"))], axis=2)
    a["b_bs"] = a["b_bs"].transpose(0, 2, 1)
    n = np.arange(512)
    freq = np.float32(10000.0) ** (-np.arange(16, dtype=np.float32) / np.float32(16))
    ang = np.stack([(n // 64).astype(np.float32)[:, None] * freq, (n % 64).astype(np.float32)[:, None] * freq], 1)
    table = np.zeros((128, 2, NT, 2, 2, 16), np.float32)
    table[:, 0] = 1.0
    for t in range(NS):
        for b in range(2):
            table[:, 0, t, :, b] = np.cos(ang[128 * t:128 * t + 128])
            table[:, 1, t, :, b] = np.sin(ang[128 * t:128 * t + 128]) * (1 if b else -1)
    a["rope"] = table.reshape(128, 2, NT, HD)

    nc = bacc.Bacc("TRN2", target_bir_lowering=False, num_devices=1)
    f32 = mybir.dt.float32
    arrays, aps = {}, {}
    for k, v in a.items():
        arrays[f"in_{k}"] = np.ascontiguousarray(v)
        aps[k] = nc.dram_tensor(f"in_{k}", v.shape, f32, kind="ExternalInput").ap()
    shapes = [(1, 128, D), (1, 512, D)] + [(1, DEPTH, 128, 2, HD)] * 4
    outs = [nc.dram_tensor(f"out_{i}", s, f32, kind="ExternalOutput").ap() for i, s in enumerate(shapes)]
    scratch = [nc.dram_tensor(n, s, f32, kind="Internal").ap()
               for n, s in (("x_save", (640, D)), ("x_norm", (640, D)), ("g_rows", (2, 4, D)))]
    build(nc, aps, outs, scratch)
    r = run(nc, [arrays], core_ids=[0])
    return tuple(r.results[0][f"out_{i}"] for i in range(len(shapes)))
```

```python
from contextlib import ExitStack

import concourse.bass as bass
from concourse import mybir

D = 1024
KB = D // 128
NS = 4
NT = NS + 1
DEPTH = 2
HD = 64
QKV = 1792
AQ, AK, AV, BU, BV, CQ, CK, CV = 0, 384, 512, 640, 896, 1152, 1536, 1664
MOD1, MOD2 = 4, 8
MOD2_FIRST = 3
MOD2_AT = {2 * i + 1: MOD2_FIRST + i for i in range(MOD2 - MOD2_FIRST - 1)}
QU = QKV // 256
GU = 3 * D // 256
WU = D // 256
E = 16
PAIRS = E // 2
CS, CP = 64, 16
UB = 4
UNITS_E = 2 * 6 * E
AHEAD = 3
FFC = 6
RING = 3
C_QKV = MOD1
C_MOD2 = C_QKV + (QU + 1) // 2
C_GATE = C_MOD2 + MOD2
C_WO = C_GATE + 9
C_MOE = C_WO + 2
CHUNKS = C_MOE + E * FFC
assert CHUNKS % RING == 0 and FFC % RING == 0 and C_MOE % RING == 0
LOADS = CHUNKS // RING
BRANCH = ((0, 1, 2), (6, 7), (3, 4, 5))

U_GATE = QU
U_WO = U_GATE + GU
UA = U_WO + WU


def unit_chunk(u):
    if u < U_GATE:
        return C_QKV + u // 2, u % 2
    if u < U_WO:
        b, q = divmod(u - U_GATE, 4)
        return C_GATE + 3 * b + 2 * (q // 2), q % 2
    return C_WO + (u - U_WO) // 2, (u - U_WO) % 2


G_QKV = MOD1
G_MOD2 = G_QKV + QU * NT
G_GATE = G_MOD2 + MOD2
G_WO = G_GATE + GU * NT
GROUPS = G_WO + WU * NT
GB = ((GROUPS + 1) // 2, GROUPS // 2)


def in_bank(g, b):
    return (g + 1 - b) // 2


def wo_group(w, t):
    return G_WO + (w * NT + t if w < 2 else 2 * NT + 2 * t + w - 2)


def last_group(u):
    if u < U_GATE:
        return G_QKV + u * NT + NT - 1
    if u < U_WO:
        return G_GATE + (u - U_GATE) * NT + NT - 1
    return wo_group(u - U_WO, NT - 1)


T_MOD, T_WS, T_CK, T_QK = 0, 1, 2, 3
T_MLP = T_QK + 2 * NT
T_O = T_MLP + NT
TQ = T_O + 2 * NT
H_M = 2 * NT
H_2 = 4 * NT
HQ = 6 * NT
UNITS = NT * 12
EPS = 1e-6
SCALE = HD ** -0.5

ORDER = [u for i in range(12) for u in [(i // 4, 3 * (i % 4) + j) for j in range(3)] + [(NS, i)]] + \
    [(NS - 1, i) for i in range(12)]
LAST = [max(i for i, u in enumerate(ORDER) if u[0] == t) for t in range(NT)]
TURNS = {LAST[t] + 5 + 3 * h + 5 * (t == NS): (t, h) for t in (0, 1, 2, NS) for h in range(2)}
TURN_NO = {u: i for i, u in enumerate(list(TURNS.values()) + [(NS - 1, 0), (NS - 1, 1)])}
MLP_AT = {4 * t + 2: t for t in range(NT)}


def sinks_until(u):
    return sum(r < 6 for _, r in ORDER[:u + 1])


def unit(u):
    t, r = ORDER[u]
    br, h = divmod(r, 6)
    kv, g = divmod(h, 3)
    if t == NS:
        blocks = [NS]
    elif br == 0:
        blocks = [b for b in (t - 1, t, t + 1) if 0 <= b < NS] + [NT]
    else:
        blocks = list(range(NS)) + [NT]
    return t, br, kv, g, blocks


def build(nc, A, outs, scratch):
    f32 = mybir.dt.float32
    u32 = mybir.dt.uint32
    ALU = mybir.AluOpType
    ACT = mybir.ActivationFunctionType
    AX = mybir.AxisListType
    y_prompt, y_sample, new_a_k, new_a_v, new_c_k, new_c_v = outs
    xs_d, xn_d, g_d = scratch

    ctx = ExitStack()
    with ctx:
        def sb(name, shape, dt=f32):
            return ctx.enter_context(nc.sbuf_tensor(name, shape, dt))

        def sem(name):
            return ctx.enter_context(nc.semaphore(name))

        f32r = mybir.dt.float32r
        ring = sb("ring", [128, RING, KB, 512])
        with ExitStack() as place:
            HTL = place.enter_context(nc.sbuf_tensor("HTL", [128, NT, KB, 128], f32r))
        X = sb("X", [128, NT * D])
        EP = sb("EP", [128, 4 * 640])
        x = X[:, :].rearrange("p (t d) -> p t d", t=NT)
        prob = EP[:, 0:1280].rearrange("p (b n) -> p b n", b=2)
        probT = EP[:, 1280:2560].rearrange("p (b n) -> p b n", b=2)
        qpair = EP[:, 512:1280].rearrange("p (b n) -> p b n", b=2)
        tmp = EP[:, 0:512]
        sqa, sqc, sqv = EP[:, 0:512], EP[:, 512:1024], EP[:, 1280:1536]
        hm = EP[:, 0:2 * D].rearrange("p (b n) -> p b n", b=2)
        gate_s = EP[:, 0:512].rearrange("p (b n) -> p b n", b=2)
        gated = EP[:, 512:768]
        upd = EP[:, 0:256]
        junk2 = EP[:, 1024:2048]
        osam, opro = EP[:, 0:D], EP[:, D:2 * D]
        aff = EP[:, 0:NT * E].rearrange("p (t e) -> p t e", t=NT)
        slots = EP[0:E, 128:640].rearrange("p (a n) -> p a n", a=4)
        topv = EP[0:E, 640:704]
        slotT = EP[:, 768:832].rearrange("p (a e) -> p a e", a=4)
        rmax = EP[:, 832:837]
        rsum = EP[:, 840:845]
        rrec = EP[:, 848:853]
        affT = EP[0:E, 1024:1664]
        affT2 = EP[0:E, 1664:2176]

        ident = sb("ident", [128, 128])
        mask = sb("mask", [128, 2, 128])
        rope = sb("rope", [128, 2, NT, HD])
        gain = sb("gain", [128, 2, 2, HD])
        vgain = sb("vgain", [128, 256])
        wsT = sb("wsT", [128, 4, 128])
        cacheV = sb("cacheV", [128, 2, 128])
        condT = sb("condT", [128, 2 * KB])
        modcol = sb("modcol", [128, 2, KB, 2])
        bs = sb("bs", [128, 4])
        sink = sb("sink", [128, 6])
        nsink = sb("nsink", [128, 6])
        brt = sb("brt", [128, E])
        wr = sb("wr", [128, KB, E])
        topi = sb("topi", [E, CS], u32)
        idxs = sb("idxs", [128, E], u32)
        idxp = sb("idxp", [128, E], u32)
        cols = sb("cols", [128, PAIRS])
        colp = sb("colp", [128, PAIRS])
        colv = sb("colv", [128, E])
        st5 = sb("st5", [128, NT])
        rs5 = sb("rs5", [128, NT])
        st100 = sb("st100", [128, NT, 20])
        rs100 = sb("rs100", [128, NT, 20])
        mx = sb("mx", [128, 4])
        nm = sb("nm", [128, 4])
        sm = sb("sm", [128, 4])
        es = sb("es", [128, 4])
        den = sb("den", [128, 1])
        rden = sb("rden", [128, 4])

        with ExitStack() as first:
            def sa(name, shape, dt=f32, scope=first):
                return scope.enter_context(nc.sbuf_tensor(name, shape, dt))

            with ExitStack() as rounded:
                HTH = sa("HTH", [128, NT, KB, 128], f32r, rounded)
            HT = sa("HT", [128, NT, KB, 128])
            with ExitStack() as split:
                WH = sa("WH", [128, 2, KB, 256], f32r, split)
                WL = sa("WL", [128, 2, KB, 256], f32r, split)
            MB = sa("MB", [128, 8 * D])
            Y = sa("Y", [128, NT * QKV])
            QK = sa("QK", [128, 8 * 640 + 2 * 768])
        with ExitStack() as second:
            def sm_(name, shape, dt=f32):
                return second.enter_context(nc.sbuf_tensor(name, shape, dt))

            w_hi = sm_("w_hi", [128, UB, 4, 512], f32r)
            w_lo = sm_("w_lo", [128, UB, 4, 512], f32r)
            xT = sm_("xT", [128, 2, KB, 128], f32r)
            hT = sm_("hT", [128, 2, KB, 128], f32r)
            xg = sm_("xg", [128, 2, D])
            hh = sm_("hh", [128, D])
            sil = sm_("sil", [128, 2, 512])
            os_hi = sm_("os_hi", [128, D], f32r)
            os_lo = sm_("os_lo", [128, D], f32r)
            hots = sm_("hots", [128, 512], f32r)
            hotp = sm_("hotp", [128, 128])
            iota = sm_("iota", [128, 512])
            g2bc = sm_("g2bc", [128, 2, D])

        modrow = Y[0:2, 0:2 * D]
        nrow1 = Y[0:2, 2 * D:3 * D]
        modrow2 = MB[0:2, 0:4 * D]
        bmod2 = MB[0:2, 4 * D:8 * D]
        nrow2 = bmod2[:, 0:D]
        gain2_part = bmod2[:, D:2 * D]
        y = Y[:, :].rearrange("p (t c) -> p t c", t=NT)
        merged = Y[:, 0:NT * D].rearrange("p (t d) -> p t d", t=NT)
        x1 = merged
        g1bc = Y[:, NT * D:(NT + 2) * D].rearrange("p (s d) -> p s d", s=2)
        qoT = QK[:, 0:8 * 640].rearrange("p (s n) -> p s n", s=8)
        kT = QK[:, 8 * 640:8 * 640 + 2 * 768].rearrange("p (b n) -> p b n", b=2)
        xn = QK[:, 0:2 * D].rearrange("p (b d) -> p b d", b=2)
        wsraw = QK[:, 2 * D:2 * D + 512].rearrange("p (g q) -> p g q", g=4)
        ckraw = QK[:, 2 * D + 512:2 * D + 768].rearrange("p (b q) -> p b q", b=2)
        junk1 = QK[:, 3 * D:4 * D]
        modbc = QK[:, 2 * D:6 * D].rearrange("p (a s d) -> p a s d", a=2, s=2)
        condrow = EP[0:16, 1024:1152]

        ps = ctx.enter_context(nc.psum_tensor("ps", [128, 8, 512], f32))

        ring_ready = [sem(f"ring_ready{s}") for s in range(RING)]
        in_ready = sem("in_ready")
        cond_in = sem("cond_in")
        const_ready = sem("const_ready")
        par_ready = sem("par_ready")
        PARS = 9
        row_ready = sem("row_ready")
        par2_ready = sem("par2_ready")
        x_saved = sem("x_saved")
        x_back = [sem(f"x_back{t}") for t in range(NT)]
        x_moved = sem("x_moved")
        g_saved = sem("g_saved")
        g1_ready = sem("g1_ready")
        g2_ready = sem("g2_ready")
        kv_saved = sem("kv_saved")
        xn_saved = [sem(f"xn_saved{b}") for b in range(2)]
        out_saved = sem("out_saved")
        cond_silu = sem("cond_silu")
        cond_done = sem("cond_done")
        cond_ready = sem("cond_ready")
        g_done = sem("g_done")
        g_free = [sem(f"g_free{b}") for b in range(2)]
        tq_done = sem("tq_done")
        tq_free = sem("tq_free")
        hq_done = sem("hq_done")
        hq_free = [sem(f"hq_free{b}") for b in range(2)]
        ss_ready = sem("ss_ready")
        ms_ready = sem("ms_ready")
        sd_ready = sem("sd_ready")
        ROOTS = 2 * NT + 1
        xn_ready = sem("xn_ready")
        mod_ready = sem("mod_ready")
        ht_hi = sem("ht_hi")
        ht_lo = sem("ht_lo")
        mt_hi = sem("mt_hi")
        wa_hi = sem("wa_hi")
        wa_lo = sem("wa_lo")
        gs_ready = sem("gs_ready")
        gelu_ready = sem("gelu_ready")
        sq_ready = sem("sq_ready")
        sq_used = sem("sq_used")
        rs_ready = sem("rs_ready")
        gained = sem("gained")
        qk_ready = sem("qk_ready")
        vg_ready = sem("vg_ready")
        v_ready = sem("v_ready")
        s_done = sem("s_done")
        nm_ready = sem("nm_ready")
        e_ready = sem("e_ready")
        es_ready = sem("es_ready")
        pt_done = sem("pt_done")
        pt_evac = sem("pt_evac")
        pv_done = sem("pv_done")
        o_evac = sem("o_evac")
        opj_done = sem("opj_done")
        opj_free = sem("opj_free")
        merged_ready = sem("merged_ready")
        x_ready = sem("x_ready")
        rt_done = sem("rt_done")
        lg_ready = sem("lg_ready")
        pe_ready = sem("pe_ready")
        aff_ready = sem("aff_ready")
        afft_done = sem("afft_done")
        slots_ready = sem("slots_ready")
        slott_done = sem("slott_done")
        idx_ready = sem("idx_ready")
        hot_ready = sem("hot_ready")
        moe_init = sem("moe_init")
        xg_ready = [sem(f"xg_ready{b}") for b in range(2)]
        xt_done = sem("xt_done")
        mq_done = sem("mq_done")
        mq_hi = sem("mq_hi")
        mq_free = [sem(f"mq_free{b}") for b in range(2)]
        hi_ready = sem("hi_ready")
        lo_ready = sem("lo_ready")
        unit_used = sem("unit_used")
        sil_ready = sem("sil_ready")
        hh_ready = sem("hh_ready")
        out_evac = [sem(f"out_evac{b}") for b in range(2)]
        os_ready = sem("os_ready")
        mb_ready = sem("mb_ready")
        sc_done = sem("sc_done")
        sc_free = [sem(f"sc_free{b}") for b in range(2)]
        dve_step = sem("dve_step")
        pool_step = sem("pool_step")
        waited = [sem(f"waited_{e}") for e in ("dve", "pe", "pool", "act")]

        def settle(engine, i):
            engine.sem_inc(waited[i], 1)

        DVE_STEPS = (1 + 3 * NT
                     + NT * 8
                     + UNITS * 2 + UNITS // 2
                     + 4 + 3
                     + 3 * (CS + CP) // 8 - 2 + 4 + 3)

        def chunk_src(l, c, e=None):
            if e is not None:
                w = (A["w_gate"], A["w_up"], A["w_gate"], A["w_up"], A["w_down"], A["w_down"])[c]
                n = (0, 0, 1, 1, 0, 1)[c]
                return w[l, e].rearrange("(k p) n -> p k n", p=128)[:, :, 512 * n:512 * n + 512]
            k0, k1 = 0, KB
            if c < C_QKV:
                w, lo, n = A["w_mod"], 512 * c, 512
            elif c < C_MOD2:
                w, lo = A["w_in"], 512 * (c - C_QKV)
                n = min(512, QKV - lo)
            elif c < C_GATE:
                w, lo, n = A["w_mod"], 512 * (c - C_MOD2 + MOD1), 512
            elif c < C_WO:
                br, i = divmod(c - C_GATE, 3)
                if i == 1:
                    w, lo, n, k0, k1 = A["w_o"], 0, D, BRANCH[br][0], BRANCH[br][-1] + 1
                else:
                    w, lo, n = A["w_in"], QKV + D * br + 256 * i, 512
            else:
                w, lo, n = A["w_out"], 512 * (c - C_WO), 512
            return w[l].rearrange("(k p) n -> p k n", p=128)[:, k0:k1, lo:lo + n]

        def slot_as(c, k, n):
            return ring[:, c % RING].rearrange("p k n -> p (k n)")[:, 0:k * n].rearrange("p (k n) -> p k n", k=k)

        def raw_of(j, b, first, s):
            if first and b == 0:
                return (s // 2) % RING, (s // 2) // RING
            m = 6 * b - 2 + s // 2
            return m % RING, 4 * j + m // RING

        block = ctx.enter_context(nc.Block())

        @block.sync
        def _(sp):
            sp.dma_start(condrow[0:KB], A["c"][0].rearrange("(k p) -> k p", p=128)).then_inc(cond_in, 16)
            sp.dma_start(condrow[KB:2 * KB], A["c_ctx"].rearrange("(k p) -> k p", p=128)).then_inc(cond_in, 16)
            with sp.Fori(0, DEPTH) as l:
                def free(c):
                    if c < C_QKV or C_MOD2 <= c < C_GATE:
                        sp.wait_ge(g_done, l * GROUPS + (c + 1 if c < C_QKV else G_MOD2 + c - C_MOD2 + 1))
                    elif C_GATE <= c < C_WO and (c - C_GATE) % 3 == 1:
                        sp.wait_ge(opj_done, l * GU * NT + (c - C_GATE + 2) // 3 * 4 * NT)
                    else:
                        sp.wait_ge(wa_lo, l * UA + max(u for u in range(UA) if unit_chunk(u)[0] == c) + 1)

                for c in range(C_MOE):
                    if c < RING:
                        sp.wait_ge(lo_ready, l * UNITS_E + 1)
                    else:
                        free(c - RING)
                    src = chunk_src(l, c)
                    sp.dma_start(slot_as(c, src.shape[1], src.shape[2]), src).then_inc(ring_ready[c % RING], 16)

                def expert_chunk(m, slot, e, c):
                    sp.wait_ge(lo_ready, l * UNITS_E + 2 * m - 3)
                    sp.dma_start(ring[:, slot], chunk_src(l, c, e)).then_inc(ring_ready[slot], 16)

                for c in range(4):
                    if c < RING:
                        free(C_MOE - RING + c)
                        sp.dma_start(ring[:, c], chunk_src(l, c, 0)).then_inc(ring_ready[c], 16)
                    else:
                        expert_chunk(c, c % RING, 0, c)
                with sp.Fori(1, E) as e:
                    for c in range(FFC):
                        expert_chunk(6 * e - 2 + c, (c + 1) % RING, e if c < 4 else e - 1, c)
                for c in (4, 5):
                    expert_chunk(6 * E - 6 + c, (c + 6 * E - 6) % RING, E - 1, c)
            for t in range(NT):
                for h in range(2):
                    sp.wait_ge(sc_free[h], DEPTH * 5 * PAIRS - NT + t + 2)
                dst = y_sample[0, 128 * t:128 * t + 128] if t < NS else y_prompt[0]
                sp.dma_start(dst, x[:, t]).then_inc(out_saved, 16)
            sp.wait_ge(out_saved, 16 * NT)

        @block.gpsimd
        def _(pool):
            pool.memset(ident[:, :], 0.0).then_inc(pool_step, 1)
            pool.memset(mask[:, :, :], 0.0).then_inc(pool_step, 1)
            pool.wait_ge(pool_step, 2)
            pool.affine_select(out=ident[:, :], in_=ident[:, :], compare_op=ALU.not_equal, fill=1.0, base=0,
                               pattern=[[-1, 128]], channel_multiplier=1).then_inc(const_ready, 1)
            pool.affine_select(out=mask[:, 0], in_=mask[:, 0], compare_op=ALU.is_ge, fill=-1.0e30, base=0,
                               pattern=[[1, 128]], channel_multiplier=-1).then_inc(const_ready, 1)
            pool.affine_select(out=mask[:, 1], in_=mask[:, 1], compare_op=ALU.is_ge, fill=-1.0e30, base=0,
                               pattern=[[-1, 128]], channel_multiplier=1).then_inc(const_ready, 1)
            pool.sem_inc(xt_done, 2)
            with pool.Fori(0, DEPTH) as l:
                def par(dst, src):
                    pool.dma_start(dst, src).then_inc(par_ready, 16)

                for s in range(2):
                    pool.dma_start(modrow[s:s + 1], A["b_mod"][bass.ds(l, 1), 0:2 * D]).then_inc(row_ready, 16)
                    pool.dma_start(nrow1[s:s + 1], A["norm1_g"][bass.ds(l, 1)]).then_inc(row_ready, 16)
                par(wsraw, A["b_ws"][l].rearrange("g p q -> p g q"))
                par(gain.rearrange("p a b d -> p (a b d)"), A["qk_gain"][bass.ds(l, 1)].to_broadcast([128, 4 * HD]))
                par(vgain[:, :], A["b_v_norm"][bass.ds(l, 1)].to_broadcast([128, 256]))
                par(sink[:, :], A["a_sink"][bass.ds(l, 1)].to_broadcast([128, 6]))
                par(brt[:, :], A["b_router"][bass.ds(l, 1)].to_broadcast([128, E]))
                par(bs[:, :], A["b_bs"][l])
                par(cacheV[:, :, :], A["cache_v"][l])
                par(ckraw, A["cache_k"][l])
                par(wr[:, :, :], A["w_router"][l].rearrange("(k p) n -> p k n", p=128))
                pool.wait_ge(in_ready, 48)
                settle(pool, 2)
                pool.dma_start(xs_d.rearrange("(t p) d -> p t d", p=128), x).then_inc(x_saved, 16)
                for t in range(NT):
                    for br, base in ((0, AQ), (1, CQ)):
                        pool.wait_ge(sq_ready, l * 3 * NT + 3 * t + br + 1)
                        if t == 0:
                            pool.wait_ge(par_ready, l * 16 * PARS + 16 * PARS)
                        for i, (lo, n) in enumerate(((0, 6), (384, 2))):
                            yh = y[:, t, base + lo:base + lo + 64 * n].rearrange("p (h d) -> p h d", h=n)
                            pool.tensor_tensor(yh, yh, gain[:, br, i:i + 1].to_broadcast([128, n, HD]), ALU.mult
                                               ).then_inc(gained, 1)
                pool.wait_ge(g_done, l * GROUPS + G_MOD2)
                settle(pool, 2)
                for s in range(2):
                    pool.dma_start(bmod2[s:s + 1], A["b_mod"][bass.ds(l, 1), 2 * D:6 * D]).then_inc(par2_ready, 16)
                pool.wait_ge(par2_ready, l * 64 + 32)
                pool.wait_ge(rs_ready, l + 1)
                for t in range(NT):
                    v = y[:, t, BV:BV + 256]
                    pool.tensor_tensor(v, v, vgain[:, :], ALU.mult).then_inc(vg_ready, 1)
                    pool.wait_ge(vg_ready, l * NT + t + 1)
                    vh = v.rearrange("p (h d) -> p h d", h=4)
                    pool.tensor_tensor(vh, vh, rs100[:, t, 16:20, None].to_broadcast([128, 4, HD]), ALU.mult
                                       ).then_inc(v_ready, 1)
                for i in range(MOD2):
                    g = G_MOD2 + i
                    pool.wait_ge(g_free[g % 2], l * GB[g % 2] + in_bank(g + 1, g % 2) + 1)
                    row = modrow2[:, 512 * i:512 * i + 512]
                    pool.tensor_tensor(row, row, bmod2[:, 512 * i:512 * i + 512], ALU.add).then_inc(pool_step, 1)
                    if i in (1, 5, MOD2 - 1):
                        pool.wait_ge(pool_step, l * (MOD2 + 2) + i + 3 + 2 * (i > 5))
                    if i == 1:
                        settle(pool, 2)
                        for s in range(2):
                            pool.dma_start(nrow2[s:s + 1], A["norm2_g"][bass.ds(l, 1)]).then_inc(par2_ready, 16)
                    if i == 5:
                        gain2 = modrow2[:, 2 * D:3 * D]
                        pool.wait_ge(par2_ready, l * 64 + 64)
                        pool.tensor_tensor(gain2_part, gain2, nrow2, ALU.mult).then_inc(pool_step, 1)
                        pool.wait_ge(pool_step, l * (MOD2 + 2) + i + 4)
                        pool.tensor_tensor(gain2, gain2_part, nrow2, ALU.add).then_inc(pool_step, 1)
                settle(pool, 2)
                for i, lo in enumerate((0, 3 * D, D, 2 * D)):
                    pool.dma_start(g_d[:, i, :], modrow2[:, lo:lo + D]).then_inc(g_saved, 16)
                pool.wait_ge(qk_ready, l * 2 * NT + 2 * NT)
                settle(pool, 2)
                for dst, c in ((new_a_k, AK), (new_a_v, AV), (new_c_k, CK), (new_c_v, CV)):
                    pool.dma_start(dst[0, l].rearrange("s k d -> s (k d)"), y[:, NS, c:c + 128]).then_inc(kv_saved, 16)
                pool.wait_ge(g_saved, l * 64 + 64)
                for u in (U_GATE, U_GATE + 1):
                    c, h = unit_chunk(u)
                    pool.wait_ge(ring_ready[c % RING], l * (16 * LOADS) + 16 * (c // RING + 1))
                    raw = ring[:, c % RING, :, 256 * h:256 * h + 256]
                    settle(pool, 2)
                    pool.tensor_copy(WH[:, u % 2], raw).then_inc(wa_hi, 1)
                    pool.wait_ge(wa_hi, l * UA + u + 1)
                    pool.tensor_tensor(WL[:, u % 2], raw, WH[:, u % 2].bitcast(f32), ALU.subtract).then_inc(wa_lo, 1)
                pool.wait_ge(o_evac, l * UNITS + UNITS + 1)
                pool.wait_ge(tq_done, l * TQ + TQ)
                settle(pool, 2)
                for s in range(2):
                    pool.dma_start(g1bc[:, s], g_d[s, 0:1, :].to_broadcast([128, D])).then_inc(g1_ready, 16)
                for t in range(NT):
                    pool.wait_ge(hq_done, l * HQ + H_M + 2 * t + 2)
                    settle(pool, 2)
                    pool.dma_start(x1[:, t], xs_d[128 * t:128 * t + 128]).then_inc(x_back[t], 16)
                pool.wait_ge(opj_done, l * GU * NT + GU * NT)
                settle(pool, 2)
                for a in range(2):
                    for s in range(2):
                        pool.dma_start(modbc[:, a, s], g_d[s, 2 + a:3 + a, :].to_broadcast([128, D])).then_inc(mb_ready, 16)
                for t in range(NT):
                    pool.wait_ge(xn_ready, l * 2 * NT + NT + t + 1)
                    settle(pool, 2)
                    pool.dma_start(xn_d[128 * t:128 * t + 128, :], xn[:, t % 2]).then_inc(xn_saved[t % 2], 16)
                for b, n in ((0, NT - NT // 2), (1, NT // 2)):
                    pool.wait_ge(xn_saved[b], l * (16 * n) + 16 * n)
                pool.wait_ge(rt_done, l + 1)
                settle(pool, 2)
                pool.iota(iota[:, :], pattern=[[1, 512]], base=0, channel_multiplier=0,
                          allow_small_or_imprecise_dtypes=True).then_inc(moe_init, 1)
                pool.memset(xg[:, :, :], 0.0).then_inc(moe_init, 1)
                pool.wait_ge(moe_init, l * 2 + 2)
                settle(pool, 2)
                for s in range(2):
                    for h in range(2):
                        pool.dma_start(g2bc[64 * h:64 * h + 64, (s + h) % 2],
                                       g_d[s, 1:2, :].to_broadcast([64, D])).then_inc(g2_ready, 16)
                for u in range(AHEAD):
                    pool.wait_ge(hi_ready, l * UNITS_E + u + 1)
                    slot = raw_of(0, 0, True, u)[0]
                    pool.tensor_tensor(w_lo[:, u % UB], ring[:, slot, 4 * (u % 2):4 * (u % 2) + 4],
                                       w_hi[:, u % UB].bitcast(f32), ALU.subtract).then_inc(lo_ready, 1)
                for u in range(AHEAD):
                    pool.wait_ge(lo_ready, l * UNITS_E + u + 2)
                pool.wait_ge(idx_ready, l + 1)
                settle(pool, 2)

                def gather(j, b):
                    e = 2 * j + b
                    lat, pro = (0, 64) if b == 0 else (64, 0)
                    pool.wait_ge(xt_done, l * E + 2 * j + (b + 1))
                    settle(pool, 2)
                    pool.indirect_dma_start(xg[lat:lat + CS, b], None, xn_d,
                                            bass.IndirectOffsetOnAxis(ap=idxs[0:CS, e:e + 1], axis=0)
                                            ).then_inc(xg_ready[b], 16)
                    pool.indirect_dma_start(xg[pro:pro + CP, b], None, xn_d,
                                            bass.IndirectOffsetOnAxis(ap=idxp[0:CP, e:e + 1], axis=0)
                                            ).then_inc(xg_ready[b], 16)

                def scale(j, b):
                    for h in range(2):
                        pool.wait_ge(out_evac[h], l * E + (2 * j + b + 3))
                        c = slice(512 * h, 512 * h + 512)
                        lat, pro = (slice(0, 64), slice(64, 128))[::1 - 2 * b]
                        n = l * 128 + (16 * j + 8 * b + 4 * h)
                        pool.tensor_tensor(osam[lat, c], osam[lat, c], g2bc[lat, b, c], ALU.mult).then_inc(os_ready, 1)
                        pool.tensor_tensor(opro[pro, c], opro[pro, c], g2bc[pro, b, c], ALU.mult).then_inc(os_ready, 1)
                        pool.wait_ge(os_ready, n + 2)
                        settle(pool, 2)
                        pool.tensor_copy(os_hi[lat, c], osam[lat, c]).then_inc(os_ready, 1)
                        pool.wait_ge(os_ready, n + 3)
                        pool.tensor_tensor(os_lo[lat, c], osam[lat, c], os_hi[lat, c].bitcast(f32), ALU.subtract
                                           ).then_inc(os_ready, 1)

                gather(0, 0)
                gather(0, 1)
                pool.wait_ge(g2_ready, l * 64 + 64)
                for j in range(PAIRS - 1):
                    if j:
                        pool.wait_ge(os_ready, l * 128 + 16 * j)
                    gather(j + 1, 0)
                    gather(j + 1, 1)
                    for b in range(2):
                        pool.wait_ge(xg_ready[b], l * (32 * PAIRS) + 32 * (j + 2))
                    scale(j, 0)
                    scale(j, 1)
                scale(PAIRS - 1, 0)
                pool.wait_ge(sc_free[0], l * 5 * PAIRS + 5 * PAIRS + 1)
                pool.wait_ge(sc_free[1], l * 5 * PAIRS + 5 * PAIRS + 1)
            pool.wait_ge(kv_saved, DEPTH * 64)
            pool.wait_ge(x_saved, DEPTH * 16)

        @block.tensor
        def _(pe):
            pe.sem_inc(unit_used, UB)
            pe.sem_inc(pt_done, 2)
            pe.sem_inc(pv_done, 2)
            pe.wait_ge(const_ready, 3)
            pe.wait_ge(cond_silu, 1)
            nc.tensor.transpose(ps[:, 7, 0:16], condrow, ident[0:16, 0:16]).then_inc(cond_done, 1)
            pe.wait_ge(cond_ready, 1)

            def transposes(bank, srcs, done):
                for i, s in enumerate(srcs):
                    last = nc.tensor.transpose(ps[:, bank, 128 * i:128 * i + 128], s, ident[:, :])
                last.then_inc(done, 1)

            with pe.Fori(0, DEPTH) as l:
                def arrived(c):
                    pe.wait_ge(ring_ready[c % RING], l * (16 * LOADS) + 16 * (c // RING + 1))

                def mod_group(g, c, bank):
                    arrived(c)
                    pe.wait_ge(g_free[g % 2], l * GB[g % 2] + g // 2 + 1)
                    for k in range(KB):
                        last = nc.tensor.matmul(ps[0:2, bank], condT.rearrange("p (s k) -> p k s", s=2)[:, k],
                                                ring[:, c % RING, k], start=k == 0, stop=k == KB - 1)
                    last.then_inc(g_done, 1)

                def group(g, u, t):
                    if t == 0:
                        pe.wait_ge(wa_lo, l * UA + u + 1)
                    pe.wait_ge(g_free[g % 2], l * GB[g % 2] + g // 2 + 1)
                    for k in range(KB):
                        for i, (a, w) in enumerate(((HTH, WH), (HTH, WL), (HTL, WH))):
                            last = nc.tensor.matmul(ps[:, g % 2, 0:256], a[:, t, k], w[:, u % 2, k],
                                                    start=k == 0 and i == 0, stop=k == KB - 1 and i == 2)
                    last.then_inc(g_done, 1)

                def turn_tile(first, t, src):
                    for h in range(2):
                        pe.wait_ge(hq_free[h], l * (HQ // 2) + (first // 2 + t) + 1)
                        transposes(2 + h, [src[:, 128 * k:128 * k + 128] for k in range(4 * h, 4 * h + 4)], hq_done)

                for c in range(MOD1):
                    mod_group(c, c, c % 2)
                pe.wait_ge(xn_ready, l * 2 * NT + 1)
                turn_tile(0, 0, xn[:, 0])
                pe.wait_ge(mod_ready, l + 1)
                pe.wait_ge(tq_free, l * TQ + T_MOD + 1)
                settle(pe, 1)
                for i, lo in enumerate((0, D)):
                    for k in range(KB):
                        last = nc.tensor.transpose(ps[:, 7, 2 * (KB * i + k):2 * (KB * i + k) + 2],
                                                   modrow[:, lo + 128 * k:lo + 128 * k + 128], ident[0:2, 0:2])
                last.then_inc(tq_done, 1)

                for t in range(1, NT):
                    pe.wait_ge(xn_ready, l * 2 * NT + t + 1)
                    turn_tile(0, t, xn[:, t % 2])

                pe.wait_ge(par_ready, l * 16 * PARS + 16 * PARS)
                pe.wait_ge(tq_free, l * TQ + T_WS + 1)
                transposes(7, [wsraw[:, g] for g in range(4)], tq_done)
                pe.wait_ge(tq_free, l * TQ + T_CK + 1)
                transposes(7, [ckraw[:, b] for b in range(2)], tq_done)

                for u in range(QU):
                    for t in range(NT):
                        if u == 0:
                            pe.wait_ge(ht_lo, l * NT + t + 1)
                        group(G_QKV + u * NT + t, u, t)
                for i in range(MOD2_FIRST):
                    mod_group(G_MOD2 + i, C_MOD2 + i, (G_MOD2 + i) % 2)
                for i in range(2 * NT):
                    if i in MOD2_AT:
                        mod_group(G_MOD2 + MOD2_AT[i], C_MOD2 + MOD2_AT[i], (G_MOD2 + MOD2_AT[i]) % 2)
                    t, br = divmod(i, 2)
                    kbase = (AK, CK)[br]
                    pe.wait_ge(qk_ready, l * 2 * NT + i + 1)
                    pe.wait_ge(tq_free, l * TQ + T_QK + i + 1)
                    transposes(7, [qpair[:, br, 128 * g:128 * g + 128] for g in range(3)] + [y[:, t, kbase:kbase + 128]],
                               tq_done)
                def mlp(t):
                    pe.wait_ge(v_ready, l * NT + t + 1)
                    pe.wait_ge(tq_free, l * TQ + T_MLP + t + 1)
                    for g in range(4):
                        last = nc.tensor.matmul(ps[:, 7, 64 * g:64 * g + 64], wsT[:, g],
                                                y[:, t, BV + 64 * g:BV + 64 * g + 64], start=True, stop=True)
                    last.then_inc(tq_done, 1)

                def scores(u):
                    t, br, kv, g, blocks = unit(u)
                    pe.wait_ge(e_ready, l * UNITS + u + 1)
                    r = slice(64 * kv, 64 * kv + 64)
                    q = qoT[r, 3 * br + g, 128 * t:128 * t + 128]
                    s0 = 2 * (u % 2)
                    for i, b in enumerate(blocks):
                        last = nc.tensor.matmul(ps[:, s0 + i // 4, 128 * (i % 4):128 * (i % 4) + 128], q,
                                                kT[r, br, 128 * b:128 * b + 128], start=i % 4 == 0, stop=True,
                                                skip_group_check=True)
                        if br == 0 and t < NS and b in (t - 1, t + 1):
                            last = nc.tensor.matmul(ps[:, s0, 128 * i:128 * i + 128], ident[:, :],
                                                    mask[:, 0 if b < t else 1], start=False, stop=True,
                                                    skip_group_check=True)
                    last.then_inc(s_done, 1)

                def turn(u):
                    blocks = unit(u)[4]
                    pe.wait_ge(e_ready, l * UNITS + u + 3)
                    pe.wait_ge(pt_evac, l * UNITS + u + 1)
                    for i in range(len(blocks)):
                        last = nc.tensor.transpose(ps[:, 4 + i // 4, 128 * (i % 4):128 * (i % 4) + 128],
                                                   prob[:, u % 2, 128 * i:128 * i + 128], ident[:, :])
                    last.then_inc(pt_done, 1)

                def weigh(u):
                    t, br, kv, g, blocks = unit(u)
                    pe.wait_ge(pt_evac, l * UNITS + u + 2)
                    pe.wait_ge(o_evac, l * UNITS + u + 1)
                    for i, b in enumerate(blocks):
                        v = cacheV[:, br, 64 * kv:64 * kv + 64] if b == NT else \
                            y[:, b, (AV, CV)[br] + 64 * kv:(AV, CV)[br] + 64 * kv + 64]
                        last = nc.tensor.matmul(ps[:, 6, 0:64], probT[:, u % 2, 128 * i:128 * i + 128], v,
                                                start=i == 0, stop=i == len(blocks) - 1)
                    last.then_inc(pv_done, 1)

                def outputs(t, h):
                    parts = [y[:, t, AQ + 128 * i:AQ + 128 * i + 128] for i in range(3)] + \
                            [y[:, t, CQ + 128 * i:CQ + 128 * i + 128] for i in range(3)] + \
                            [y[:, t, BU + 128 * i:BU + 128 * i + 128] for i in range(2)]
                    pe.wait_ge(o_evac, l * UNITS + LAST[t] + 2)
                    pe.wait_ge(tq_free, l * TQ + T_O + TURN_NO[t, h] + 1)
                    transposes(7, parts[4 * h:4 * h + 4], tq_done)

                pe.wait_ge(tq_free, l * TQ + T_MLP + 1)
                for b in range(2):
                    pe.wait_ge(g_free[b], l * GB[b] + in_bank(G_GATE - 1, b) + 1)
                for i in range(UNITS + 3):
                    if i < UNITS:
                        scores(i)
                    if i == 1:
                        mod_group(G_GATE - 1, C_GATE - 1, 6)
                    if 2 <= i < UNITS + 2:
                        turn(i - 2)
                    if i == 3:
                        b = (G_GATE - 1) % 2
                        pe.wait_ge(g_free[b], l * GB[b] + in_bank(G_GATE, b) + 1)
                    if i >= 3:
                        weigh(i - 3)
                    if i in MLP_AT:
                        mlp(MLP_AT[i])
                    if i in TURNS:
                        outputs(*TURNS[i])
                    if i in (UNITS, UNITS + 1):
                        group(G_GATE + i - UNITS, U_GATE, i - UNITS)
                for h in range(2):
                    outputs(NS - 1, h)
                pe.wait_ge(tq_free, l * TQ + TQ + 1)
                pe.wait_ge(pt_evac, l * UNITS + UNITS + 1)

                def project(v, t):
                    br, q = divmod(v, 4)
                    o = v * NT + t
                    c = C_GATE + 3 * br + 1
                    if q == 0 and t == 0:
                        arrived(c)
                    pe.wait_ge(opj_free, l * GU * NT + o + 1)
                    w = slot_as(c, len(BRANCH[br]), D)
                    for i, k in enumerate(BRANCH[br]):
                        last = nc.tensor.matmul(ps[:, 4 + o % 2, 0:256], qoT[:, k, 128 * t:128 * t + 128],
                                                w[:, i, 256 * q:256 * q + 256], start=i == 0, stop=k == BRANCH[br][-1])
                    last.then_inc(opj_done, 1)

                def merged_tile(t):
                    pe.wait_ge(merged_ready, l * GU * NT + (GU - 1) * NT + t + 1)
                    turn_tile(H_M, t, merged[:, t])

                for o in range(GU * NT):
                    v, t = divmod(o, NT)
                    if 1 <= o < GU * NT - 1:
                        group(G_GATE + o + 1, U_GATE + (o + 1) // NT, (o + 1) % NT)
                    project(v, t)
                    if v == GU - 1 and t:
                        merged_tile(t - 1)
                merged_tile(NT - 1)

                def h2_tile(t):
                    pe.wait_ge(xn_ready, l * 2 * NT + NT + t + 1)
                    turn_tile(H_2, t, xn[:, t % 2])

                def route(t):
                    for h in range(2):
                        pe.wait_ge(hq_free[h], l * (HQ // 2) + 2 * NT + t + 2)
                    for k in range(KB):
                        last = nc.tensor.matmul(ps[:, 6, E * t:E * t + E], HT[:, t, k], wr[:, k],
                                                start=k == 0, stop=k == KB - 1)
                    return last

                for w in range(2):
                    for t in range(NT):
                        if w == 0:
                            for h in range(2):
                                pe.wait_ge(hq_free[h], l * (HQ // 2) + NT + t + 2)
                        group(wo_group(w, t), U_WO + w, t)
                for t in range(NT):
                    for w in (2, 3):
                        group(wo_group(w, t), U_WO + w, t)
                    if t >= 2:
                        h2_tile(t - 2)
                        if t >= 3:
                            route(t - 3)
                for t in (NT - 2, NT - 1):
                    h2_tile(t)
                    route(t - 1)
                route(NT - 1).then_inc(rt_done, 1)
                pe.wait_ge(aff_ready, l + 1)
                for t in range(NT):
                    last = nc.tensor.transpose(ps[0:E, 7 if t < NS else 6, 128 * (t % NS):128 * (t % NS) + 128],
                                               aff[:, t], ident[:, :])
                last.then_inc(afft_done, 1)
                pe.wait_ge(slots_ready, l + 1)
                settle(pe, 0)
                for a in range(4):
                    last = nc.tensor.transpose(ps[:, 7, E * a:E * a + E], slots[:, a], ident[0:E, 0:E])
                last.then_inc(slott_done, 1)

                def turn_rows(j, b, use, n):
                    pe.wait_ge(xg_ready[b], l * (32 * PAIRS) + (j * 32 + 32))
                    for h in range(2):
                        pe.wait_ge(mq_free[h], l * 32 + use + 1)
                        transposes(4 + h, [xg[:, b, 512 * h + 128 * i:512 * h + 128 * i + 128] for i in range(4)], mq_done)
                    pe.wait_ge(mq_done, l * 64 + n + 2)
                    pe.sem_inc(xt_done, 1)

                def chunk(n, u0, lhs, bank):
                    for half in range(2):
                        pe.wait_ge(lo_ready, l * UNITS_E + n + (half + 2))
                        for k in range(4):
                            kb, u = 4 * half + k, u0 + half
                            for i, (a, w) in enumerate(((0, w_hi), (0, w_lo), (1, w_hi))):
                                last = nc.tensor.matmul(ps[:, bank], lhs[:, a, kb], w[:, u, k],
                                                        start=kb == 0 and i == 0, stop=kb == KB - 1 and i == 2)
                        last.then_inc(unit_used, 1)

                def scatter(j, t):
                    if t == 0:
                        pe.wait_ge(hot_ready, l * PAIRS + j + 1)
                        pe.wait_ge(os_ready, l * 128 + (16 * j + 16))
                    for h in range(2):
                        pe.wait_ge(sc_free[h], l * (5 * PAIRS) + (j * 5 + t + 1))
                        c = slice(512 * h, 512 * h + 512)
                        if t < NS:
                            nc.tensor.matmul(ps[:, 6 + h], hots[:, 128 * t:128 * t + 128], os_hi[:, c], start=True, stop=False)
                            last = nc.tensor.matmul(ps[:, 6 + h], hots[:, 128 * t:128 * t + 128], os_lo[:, c],
                                                    start=False, stop=True)
                        else:
                            last = nc.tensor.matmul(ps[:, 6 + h], hotp[:, :], opro[:, c], start=True, stop=True)
                        last.then_inc(sc_done, 1)

                def step(j, b, first, last_pair):
                    e = 2 * j + b
                    start = b == 0 and first
                    n = 0 if start else 12 * e - 4
                    for h in range(2):
                        pe.wait_ge(mq_free[h], l * 32 + (2 if start else 2 * e + 1))
                    add = lambda t: scatter(j - 1, t) if b and not first else None
                    for h in range(2):
                        pe.wait_ge(out_evac[h], l * E + (e + 1))
                        chunk(n + 4 * h, 0, xT, h)
                        if h:
                            add(1)
                        chunk(n + 4 * h + 2, 2, xT, 2 + h)
                        if h == 0:
                            add(0)
                    if not (b and last_pair):
                        turn_rows(j + b, 1 - b, 2 * e + 1, 4 * e + 2)
                    add(2)
                    if not start:
                        down(e, n + 8, add)
                    for h in range(2):
                        pe.wait_ge(hh_ready, l * 32 + (2 * e + h + 1))
                        pe.wait_ge(mq_free[h], l * 32 + (2 * e + (2 if b and last_pair else 3)))
                        transposes(4 + h, [hh[:, 512 * h + 128 * i:512 * h + 128 * i + 128] for i in range(4)], mq_done)

                def down(e, n, add):
                    for h in range(2):
                        pe.wait_ge(mq_free[h], l * 32 + (2 * e + 2))
                    for h in range(2):
                        pe.wait_ge(sil_ready, l * 32 + (2 * e + h + 1))
                        chunk(n + 2 * h, 2 * h, hT, h)
                        add(3 + h)

                pe.wait_ge(moe_init, l * 2 + 2)
                turn_rows(0, 0, 0, 0)
                step(0, 0, True, False)
                step(0, 1, True, False)
                with pe.Fori(1, PAIRS - 1) as j:
                    step(j, 0, False, False)
                    step(j, 1, False, False)
                step(PAIRS - 1, 0, False, True)
                step(PAIRS - 1, 1, False, True)
                for h in range(2):
                    pe.wait_ge(mq_free[h], l * 32 + 33)
                for h in range(2):
                    pe.wait_ge(out_evac[h], l * E + E + 1)
                    chunk(UNITS_E - 4 + 2 * h, 2 * h, hT, h)
                for t in range(NT):
                    scatter(PAIRS - 1, t)

        @block.scalar
        def _(act):
            act.sem_inc(e_ready, 2)
            act.sem_inc(out_evac[0], 2)
            act.sem_inc(out_evac[1], 2)
            act.dma_start(x[:, 0:NS], A["x_sample"][0].rearrange("(t p) d -> p t d", p=128)).then_inc(in_ready, 16)
            act.dma_start(x[:, NS], A["x_prompt"][0]).then_inc(in_ready, 16)
            act.dma_start(rope[:, :, :, :], A["rope"]).then_inc(in_ready, 16)
            act.wait_ge(cond_in, 32)
            nc.scalar.activation(condrow, condrow, ACT.Silu).then_inc(cond_silu, 1)
            act.wait_ge(cond_ready, 1)
            with act.Fori(0, DEPTH) as l:
                def square(i, t):
                    act.wait_ge(ss_ready, l * 2 * NT + (i * NT + t + 1))
                    nc.scalar.activation((junk1, junk2)[i], (x, x1)[i][:, t], ACT.Square, accum_out=st5[:, t:t + 1]).then_inc(ss_ready, 1)

                def root(i, out, src):
                    act.wait_ge(ms_ready, l * ROOTS + i + 1)
                    nc.scalar.activation(out, src, ACT.Sqrt).then_inc(sd_ready, 1)

                act.wait_ge(sc_free[0], l * 5 * PAIRS + 1)
                act.wait_ge(sc_free[1], l * 5 * PAIRS + 1)
                for t in range(NT):
                    square(0, t)
                for t in range(NT):
                    root(t, rs5[:, t:t + 1], st5[:, t:t + 1])

                def split(u):
                    c, h = unit_chunk(u)
                    n = chunk_src(l, c).shape[2]
                    act.wait_ge(ring_ready[c % RING], l * (16 * LOADS) + 16 * (c // RING + 1))
                    if u == U_GATE + 2:
                        act.wait_ge(wa_lo, l * UA + u)
                    if u >= 2:
                        act.wait_ge(g_done, l * GROUPS + last_group(u - 2) + 1)
                    nc.scalar.activation(WH[:, u % 2], slot_as(c, KB, n)[:, :, 256 * h:256 * h + 256],
                                         ACT.Copy).then_inc(wa_hi, 1)

                split(0)
                split(1)
                act.wait_ge(tq_free, l * TQ + T_MOD + 2)
                for t in range(NT):
                    s = 0 if t < NS else 1
                    act.wait_ge(hq_done, l * HQ + 2 * t + 1)
                    if t >= 2:
                        act.wait_ge(ht_lo, l * NT + t - 1)
                    for k in range(4):
                        last = nc.scalar.activation(hm[:, t % 2, 128 * k:128 * k + 128], ps[:, 2, 128 * k:128 * k + 128],
                                                    ACT.Identity, bias=modcol[:, 0, k, s:s + 1],
                                                    scale=modcol[:, 1, k, s:s + 1])
                    last.then_inc(hq_free[0], 1)
                    for h in range(2):
                        act.wait_ge(hq_free[h], l * (HQ // 2) + t + 2)
                    nc.scalar.activation(HTH[:, t].rearrange("p k n -> p (k n)"), hm[:, t % 2], ACT.Copy).then_inc(ht_hi, 1)
                act.wait_ge(tq_done, l * TQ + T_WS + 1)
                nc.scalar.activation(wsT.rearrange("p g n -> p (g n)"), ps[:, 7], ACT.Copy).then_inc(tq_free, 1)
                act.wait_ge(tq_done, l * TQ + T_CK + 1)
                nc.scalar.activation(kT[:, :, 640:768], ps[:, 7, 0:256].rearrange("p (b n) -> p b n", b=2),
                                     ACT.Copy).then_inc(tq_free, 1)
                for g in range(G_QKV, G_MOD2):
                    u, t = divmod(g - G_QKV, NT)
                    if t == 0 and 0 < u < QU - 1:
                        split(u + 1)
                    if g % 2 == 0:
                        act.wait_ge(g_done, l * GROUPS + g + 1)
                        nc.scalar.activation(y[:, t, 256 * u:256 * u + 256], ps[:, 0, 0:256], ACT.Copy).then_inc(g_free[0], 1)
                for b in range(2):
                    act.wait_ge(g_free[b], l * GB[b] + in_bank(G_MOD2, b) + 1)
                act.wait_ge(ht_lo, l * NT + NT)
                for t in range(NT):
                    nc.scalar.activation(y[:, t, BU:BU + 512], y[:, t, BU:BU + 512], ACT.Gelu_apprx_tanh).then_inc(gelu_ready, 1)
                    for i, (dst, c) in enumerate(((sqa, AQ), (sqc, CQ), (sqv, BV))):
                        if t:
                            act.wait_ge(sq_used, l * 3 * NT + 3 * t - 2 + i)
                        if i == 2:
                            act.wait_ge(gelu_ready, l * NT + t + 1)
                        n = dst.shape[1]
                        nc.scalar.activation(dst, y[:, t, c:c + n], ACT.Square).then_inc(sq_ready, 1)

                def mod_row(i, bank=None):
                    g = G_MOD2 + i
                    act.wait_ge(g_done, l * GROUPS + g + 1)
                    nc.scalar.activation(modrow2[:, 512 * i:512 * i + 512], ps[0:2, g % 2 if bank is None else bank],
                                         ACT.Copy).then_inc(g_free[g % 2], 1)

                mod_row(0)
                root(NT, rs100[:, :, :], st100[:, :, :])
                for i in range(1, MOD2_FIRST):
                    mod_row(i)
                for i in range(2 * NT):
                    if i in MOD2_AT:
                        mod_row(MOD2_AT[i])
                    t, br = divmod(i, 2)
                    act.wait_ge(tq_done, l * TQ + T_QK + i + 1)
                    nc.scalar.activation(qoT[:, 3 * br:3 * br + 3, 128 * t:128 * t + 128],
                                         ps[:, 7, 0:384].rearrange("p (s n) -> p s n", s=3), ACT.Copy)
                    nc.scalar.activation(kT[:, br, 128 * t:128 * t + 128], ps[:, 7, 384:512], ACT.Copy).then_inc(tq_free, 1)

                def outputs_out(t, h):
                    act.wait_ge(tq_done, l * TQ + T_O + TURN_NO[t, h] + 1)
                    nc.scalar.activation(qoT[:, 4 * h:4 * h + 4, 128 * t:128 * t + 128],
                                         ps[:, 7].rearrange("p (s n) -> p s n", s=4), ACT.Copy).then_inc(tq_free, 1)

                for i in range(UNITS + 2):
                    if i < UNITS:
                        t, br, kv, g, blocks = unit(i)
                        n = 128 * len(blocks)
                        m = slice(i % 4, i % 4 + 1)
                        s0 = 2 * (i % 2)
                        act.wait_ge(nm_ready, l * UNITS + i + 1)
                        act.wait_ge(pt_done, l * UNITS + i + 1)
                        nc.scalar.activation(prob[:, i % 2, 0:n], ps[:, s0:s0 + 2].rearrange("p b n -> p (b n)")[:, 0:n],
                                             ACT.Exp, bias=nm[:, m], scale=SCALE,
                                             accum_out=sm[:, m]).then_inc(e_ready, 1)
                        if br == 0:
                            h = 3 * kv + g
                            nc.scalar.activation(es[:, m], sink[:, h:h + 1], ACT.Exp,
                                                 bias=nm[:, m]).then_inc(es_ready, 1)
                    if i == 1:
                        mod_row(MOD2 - 1, 6)
                    u = i - 2
                    if 0 <= u < UNITS and u % 2:
                        n = 128 * len(unit(u)[4])
                        act.wait_ge(pt_done, l * UNITS + u + 3)
                        act.wait_ge(pv_done, l * UNITS + u + 1)
                        nc.scalar.activation(probT[:, 1, 0:n], ps[:, 4:6].rearrange("p b n -> p (b n)")[:, 0:n],
                                             ACT.Copy).then_inc(pt_evac, 1)
                    if i in TURNS:
                        outputs_out(*TURNS[i])
                for h in range(2):
                    outputs_out(NS - 1, h)

                def merged_out(t):
                    for h in range(2):
                        act.wait_ge(hq_done, l * HQ + H_M + 2 * t + h + 1)
                        nc.scalar.activation(HTH[:, t, 4 * h:4 * h + 4], ps[:, 2 + h].rearrange("p (s n) -> p s n", s=4),
                                             ACT.Copy, scale=0.5).then_inc(mt_hi, 1)

                for v in range(GU):
                    if v:
                        split(U_GATE + v + 1)
                    for t in range(NT):
                        o = v * NT + t
                        g = G_GATE + o
                        act.wait_ge(g_done, l * GROUPS + g + 1)
                        if o >= 2:
                            act.wait_ge(opj_free, l * GU * NT + o + 1)
                        nc.scalar.activation(gate_s[:, o % 2], ps[:, g % 2, 0:256], ACT.Tanh, scale=0.5
                                             ).then_inc(gs_ready, 1)
                        if v == GU - 1 and t:
                            merged_out(t - 1)
                merged_out(NT - 1)

                def h2_out(t):
                    act.wait_ge(hq_done, l * HQ + H_2 + 2 * t + 1)
                    nc.scalar.activation(HT[:, t, 0:4], ps[:, 2].rearrange("p (s n) -> p s n", s=4),
                                         ACT.Copy).then_inc(hq_free[0], 1)

                for w in range(1, WU):
                    split(U_WO + w)
                for t in range(NT):
                    act.wait_ge(x_ready, l * WU * NT + wo_group(WU - 1, t) - G_WO + 1)
                    square(1, t)
                    nc.scalar.activation(x[:, t], x1[:, t], ACT.Copy).then_inc(x_moved, 1)
                    root(NT + 1 + t, rs5[:, t:t + 1], st5[:, t:t + 1])
                    if t >= 2:
                        h2_out(t - 2)
                h2_out(NT - 2)
                h2_out(NT - 1)
                act.wait_ge(lg_ready, l + 1)
                nc.scalar.activation(aff, aff, ACT.Exp).then_inc(pe_ready, 1)

                def hi(n, u, raw):
                    act.wait_ge(ring_ready[raw[0]], l * (16 * LOADS) + 16 * (raw[1] + C_MOE // RING + 1))
                    act.wait_ge(unit_used, l * UNITS_E + (n + 1))
                    nc.scalar.activation(w_hi[:, u % UB], ring[:, raw[0], 4 * (u % 2):4 * (u % 2) + 4],
                                         ACT.Copy).then_inc(hi_ready, 1)

                def used(n):
                    act.wait_ge(unit_used, l * UNITS_E + (n + 1 + UB))

                def parts(dst, n):
                    for h in range(2):
                        act.wait_ge(mq_done, l * 64 + (n + h + 1))
                        nc.scalar.activation(dst[:, 0, 4 * h:4 * h + 4], ps[:, 4 + h].rearrange("p (k n) -> p k n", k=4),
                                             ACT.Copy).then_inc(mq_hi, 1)

                def outputs(e, b, h, n):
                    used(n)
                    settle(act, 3)
                    c = slice(512 * h, 512 * h + 512)
                    for r, dst in ((slice(0, 64), (osam, opro)[b]), (slice(64, 128), (opro, osam)[b])):
                        last = nc.scalar.activation(dst[r, c], ps[r, h], ACT.Copy, scale=colv[r, bass.ds(e, 1)])
                    last.then_inc(out_evac[h], 1)

                def step(j, b, first, last_pair):
                    e = 2 * j + b
                    start = b == 0 and first
                    n = 0 if start else 12 * e - 4
                    for s in range(8 if start else 12):
                        if s == 0 and not (first and b < 2):
                            outputs(e - 2, b, 1, n - 1)
                        hi(n + s + AHEAD, s + AHEAD, raw_of(j, b, first, s + AHEAD))
                        if s == 1 and not start:
                            parts(hT, 4 * e)
                        if s in (2, 6):
                            used(n + s - 1)
                            nc.scalar.activation(sil[:, s // 4], ps[:, s // 4], ACT.Silu).then_inc(sil_ready, 1)
                        if s == (7 if start else 8) and not (b and last_pair):
                            parts(xT, 4 * e + 2)
                        if s == 10 and b == 0:
                            outputs(e - 1, 1, 0, n + 9)
                    if b:
                        if not first:
                            act.wait_ge(sc_done, l * 80 + 10 * j)
                        outputs(e - 1, 0, 0, n + 9)

                act.wait_ge(moe_init, l * 2 + 2)
                for u in range(AHEAD):
                    hi(u, u, raw_of(0, 0, True, u))
                parts(xT, 0)
                act.wait_ge(idx_ready, l + 1)
                step(0, 0, True, False)
                step(0, 1, True, False)
                with act.Fori(1, PAIRS - 1) as j:
                    step(j, 0, False, False)
                    step(j, 1, False, False)
                step(PAIRS - 1, 0, False, True)
                step(PAIRS - 1, 1, False, True)
                outputs(E - 2, 0, 1, UNITS_E - 5)
                parts(hT, 62)
                hi(UNITS_E - 1, 3, raw_of(PAIRS - 1, 1, False, 15))
                outputs(E - 1, 1, 0, UNITS_E - 3)
                outputs(E - 1, 1, 1, UNITS_E - 1)

        @block.vector
        def _(dve):
            for s in (g_free[0], g_free[1], tq_free, hq_free[0], hq_free[1], pt_evac, o_evac, mq_free[0], mq_free[1],
                      lo_ready, ss_ready):
                dve.sem_inc(s, 1)
            dve.sem_inc(opj_free, 2)
            dve.wait_ge(in_ready, 48)
            dve.sem_inc(sc_free[0], 1)
            dve.sem_inc(sc_free[1], 1)
            dve.wait_ge(cond_done, 1)
            nc.vector.tensor_copy(condT[:, :], ps[:, 7, 0:16]).then_inc(cond_ready, 1)
            steps = [0]
            TT, TS, STT = nc.vector.tensor_tensor, nc.vector.tensor_scalar, nc.vector.scalar_tensor_tensor
            with dve.Fori(0, DEPTH) as l:
                def link(ins):
                    steps[0] += 1
                    ins.then_inc(dve_step, 1)
                    dve.wait_ge(dve_step, l * DVE_STEPS + steps[0])

                def mark(ins):
                    steps[0] += 1
                    ins.then_inc(dve_step, 1)

                def done(behind):
                    dve.wait_ge(dve_step, l * DVE_STEPS + steps[0] - behind)

                def link_top(ins):
                    link(ins)
                    settle(dve, 3)

                def h_out(t):
                    s = 0 if t < NS else 1
                    dve.wait_ge(hq_done, l * HQ + 2 * t + 2)
                    if t >= 2:
                        dve.wait_ge(ht_lo, l * NT + t - 1)
                    for k in range(4):
                        last = TS(hm[:, t % 2, 512 + 128 * k:640 + 128 * k], ps[:, 3, 128 * k:128 * k + 128],
                                  modcol[:, 1, 4 + k, s:s + 1], modcol[:, 0, 4 + k, s:s + 1], ALU.mult, ALU.add)
                    last.then_inc(hq_free[1], 1)

                def h_lo(t):
                    dve.wait_ge(ht_hi, l * NT + t + 1)
                    if t == 0:
                        dve.wait_ge(x_saved, l * 16 + 16)
                    TT(HTL[:, t].rearrange("p k n -> p (k n)"), hm[:, t % 2],
                       HTH[:, t].rearrange("p k n -> p (k n)").bitcast(f32), ALU.subtract).then_inc(ht_lo, 1)

                def split(u):
                    c, h = unit_chunk(u)
                    n = chunk_src(l, c).shape[2]
                    dve.wait_ge(wa_hi, l * UA + u + 1)
                    TT(WL[:, u % 2], slot_as(c, KB, n)[:, :, 256 * h:256 * h + 256], WH[:, u % 2].bitcast(f32),
                       ALU.subtract).then_inc(wa_lo, 1)

                def mean(i, t):
                    dve.wait_ge(ss_ready, l * 2 * NT + (i * NT + t + 2))
                    TS(st5[:, t:t + 1], st5[:, t:t + 1], 1.0 / D, EPS, ALU.mult, ALU.add).then_inc(ms_ready, 1)

                def normalise(t):
                    dve.wait_ge(sd_ready, l * ROOTS + t + 1)
                    link(nc.vector.reciprocal(rs5[:, t:t + 1], rs5[:, t:t + 1]))
                    if t >= 2:
                        dve.wait_ge(hq_done, l * HQ + 2 * (t - 1))
                    TS(xn[:, t % 2], x[:, t], rs5[:, t:t + 1], None, ALU.mult).then_inc(xn_ready, 1)

                for t in range(NT):
                    mean(0, t)
                normalise(0)
                normalise(1)
                dve.wait_ge(row_ready, l * 64 + 64)
                for c in range(MOD1):
                    dve.wait_ge(g_done, l * GROUPS + c + 1)
                    m = modrow[:, 512 * c:512 * c + 512]
                    TT(m, m, ps[0:2, c % 2], ALU.add).then_inc(g_free[c % 2], 1)
                for b in range(2):
                    dve.wait_ge(g_free[b], l * GB[b] + MOD1 // 2 + 1)
                STT(modrow[:, D:2 * D], modrow[:, D:2 * D], 1.0, nrow1, ALU.add, ALU.mult).then_inc(mod_ready, 1)
                dve.wait_ge(par_ready, l * 16 * PARS + 16 * PARS)
                link(TS(nsink[:, :], sink[:, :], -1.0, None, ALU.mult))
                split(0)
                dve.wait_ge(tq_done, l * TQ + T_MOD + 1)
                nc.vector.tensor_copy(modcol.rearrange("p a k s -> p (a k s)"), ps[:, 7, 0:32]).then_inc(tq_free, 1)
                dve.wait_ge(tq_free, l * TQ + T_MOD + 2)

                for t in range(NT):
                    if t >= 2:
                        normalise(t)
                    if t:
                        h_out(t - 1)
                    if t >= 2:
                        h_lo(t - 2)
                h_out(NT - 1)
                h_lo(NT - 2)
                h_lo(NT - 1)
                for g in range(G_QKV, G_MOD2):
                    u, t = divmod(g - G_QKV, NT)
                    if t == 0 and u + 1 < QU:
                        split(u + 1)
                    if g % 2:
                        dve.wait_ge(g_done, l * GROUPS + g + 1)
                        nc.vector.tensor_copy(y[:, t, 256 * u:256 * u + 256], ps[:, 1, 0:256]).then_inc(g_free[1], 1)
                for b in range(2):
                    dve.wait_ge(g_free[b], l * GB[b] + in_bank(G_MOD2, b) + 1)
                dve.wait_ge(tq_free, l * TQ + T_CK + 2)
                heads = lambda a, n: a.rearrange("p (h d) -> p h d", h=n)
                for t in range(NT):
                    for i, (src, n) in enumerate(((sqa, 8), (sqc, 8), (sqv, 4))):
                        dve.wait_ge(sq_ready, l * 3 * NT + 3 * t + i + 1)
                        nc.vector.tensor_reduce(st100[:, t, 8 * i:8 * i + n], heads(src, n), axis=AX.X, op=ALU.add
                                                ).then_inc(sq_used, 1)
                dve.wait_ge(sq_used, l * 3 * NT + 3 * NT)
                TS(st100[:, :, :], st100[:, :, :], 1.0 / HD, EPS, ALU.mult, ALU.add).then_inc(ms_ready, 1)
                dve.wait_ge(sd_ready, l * ROOTS + NT + 1)
                nc.vector.reciprocal(rs100[:, :, :], rs100[:, :, :]).then_inc(rs_ready, 1)
                dve.wait_ge(rs_ready, l + 1)
                for t in range(NT):
                    for br, base in ((0, AQ), (1, CQ)):
                        yb = y[:, t, base:base + 512]
                        yh = heads(yb, 8)
                        dve.wait_ge(gained, l * 4 * NT + 4 * t + 2 * br + 2)
                        link(TT(yh, yh, rs100[:, t, 8 * br:8 * br + 8, None].to_broadcast([128, 8, HD]), ALU.mult))
                        y4 = yb.rearrange("p (h a b c) -> p h a b c", h=8, a=2, b=2)
                        t4 = tmp.rearrange("p (h a b c) -> p h a b c", h=8, a=2, b=2)
                        s4 = rope[:, 1, t].rearrange("p (a b c) -> p a b c", a=2, b=2)
                        for b in range(2):
                            link(TT(t4[:, :, :, b], y4[:, :, :, 1 - b],
                                    s4[:, None, :, b].to_broadcast([128, 8, 2, 16]), ALU.mult))
                        link(TT(yh, yh, rope[:, 0, t:t + 1].to_broadcast([128, 8, HD]), ALU.mult))
                        if t:
                            dve.wait_ge(tq_done, l * TQ + T_QK + 2 * t + br - 1)
                        pair3 = lambda a, o: a.rearrange(o, v=2, g=3)
                        TT(pair3(qpair[:, br], "p (g v d) -> p v g d"), pair3(yb[:, 0:384], "p (v g d) -> p v g d"),
                           pair3(tmp[:, 0:384], "p (v g d) -> p v g d"), ALU.add)
                        TT(yb[:, 384:512], yb[:, 384:512], tmp[:, 384:512], ALU.add).then_inc(qk_ready, 1)
                        dve.wait_ge(qk_ready, l * 2 * NT + 2 * t + br + 1)

                def mlp(t):
                    dve.wait_ge(tq_done, l * TQ + T_MLP + t + 1)
                    for g in range(4):
                        u = y[:, t, BU + 64 * g:BU + 64 * g + 64]
                        last = STT(u, ps[:, 7, 64 * g:64 * g + 64], bs[:, g:g + 1], u, ALU.add, ALU.mult)
                    last.then_inc(tq_free, 1)

                for i in range(UNITS + 3):
                    if i < UNITS:
                        t, br, kv, g, blocks = unit(i)
                        n = 128 * len(blocks)
                        h = 3 * kv + g
                        s0 = 2 * (i % 2)
                        m = slice(i % 4, i % 4 + 1)
                        dve.wait_ge(s_done, l * UNITS + i + 1)
                        link(nc.vector.reduce_max(mx[:, m], ps[:, s0:s0 + 2].rearrange("p b n -> p (b n)")[:, 0:n], AX.X))
                        if br == 0:
                            TS(nm[:, m], mx[:, m], -SCALE, nsink[:, h:h + 1], ALU.mult, ALU.min).then_inc(nm_ready, 1)
                        else:
                            TS(nm[:, m], mx[:, m], -SCALE, None, ALU.mult).then_inc(nm_ready, 1)
                    u = i - 2
                    if 0 <= u < UNITS:
                        t, br, kv, g, blocks = unit(u)
                        m = slice(u % 4, u % 4 + 1)
                        if u % 2 == 0:
                            n = 128 * len(blocks)
                            dve.wait_ge(pt_done, l * UNITS + u + 3)
                            dve.wait_ge(pv_done, l * UNITS + u + 1)
                            nc.vector.tensor_copy(probT[:, 0, 0:n],
                                                  ps[:, 4:6].rearrange("p b n -> p (b n)")[:, 0:n]).then_inc(pt_evac, 1)
                        dve.wait_ge(e_ready, l * UNITS + u + 3)
                        if u >= 4:
                            dve.wait_ge(o_evac, l * UNITS + u - 2)
                        if br == 0:
                            dve.wait_ge(es_ready, l * (NT * 6) + sinks_until(u))
                            link(TT(den[:, :], sm[:, m], es[:, m], ALU.add))
                            link(nc.vector.reciprocal(rden[:, m], den[:, :]))
                        else:
                            link(nc.vector.reciprocal(rden[:, m], sm[:, m]))
                    u = i - 3
                    if u >= 0:
                        t, br, kv, g, _ = unit(u)
                        h = 3 * kv + g
                        dve.wait_ge(pv_done, l * UNITS + u + 3)
                        TS(y[:, t, (AQ, CQ)[br] + 64 * h:(AQ, CQ)[br] + 64 * h + 64], ps[:, 6, 0:64],
                           rden[:, u % 4:u % 4 + 1], None, ALU.mult).then_inc(o_evac, 1)
                    if i in MLP_AT:
                        mlp(MLP_AT[i])
                dve.wait_ge(kv_saved, l * 64 + 64)

                def merged_lo(t):
                    for h in range(2):
                        dve.wait_ge(mt_hi, l * 2 * NT + 2 * t + h + 1)
                        STT(HTL[:, t, 4 * h:4 * h + 4], ps[:, 2 + h].rearrange("p (s n) -> p s n", s=4), 0.5,
                            HTH[:, t, 4 * h:4 * h + 4].bitcast(f32), ALU.mult, ALU.subtract).then_inc(hq_free[h], 1)

                for v in range(GU):
                    if v:
                        split(U_GATE + v + 1)
                    br, q = divmod(v, 4)
                    for t in range(NT):
                        o = v * NT + t
                        g = G_GATE + o
                        m = merged[:, t, 256 * q:256 * q + 256]
                        dve.wait_ge(gs_ready, l * GU * NT + o + 1)
                        dve.sem_inc(g_free[g % 2], 1)
                        dve.wait_ge(opj_done, l * GU * NT + o + 1)
                        if br == 0:
                            STT(m, gate_s[:, o % 2], 1.0, ps[:, 4 + o % 2, 0:256], ALU.add, ALU.mult).then_inc(opj_free, 1)
                            dve.sem_inc(merged_ready, 1)
                        else:
                            STT(gated, gate_s[:, o % 2], 1.0, ps[:, 4 + o % 2, 0:256], ALU.add, ALU.mult).then_inc(opj_free, 1)
                            dve.wait_ge(opj_free, l * GU * NT + o + 3)
                            TT(m, m, gated, ALU.add).then_inc(merged_ready, 1)
                            dve.wait_ge(merged_ready, l * GU * NT + o + 1)
                        if v == GU - 1 and t:
                            merged_lo(t - 1)
                merged_lo(NT - 1)
                dve.wait_ge(g1_ready, l * 32 + 32)

                def h2(t):
                    s = 0 if t < NS else 1
                    if t == 0:
                        dve.wait_ge(mb_ready, l * 64 + 64)
                    dve.wait_ge(sd_ready, l * ROOTS + NT + 1 + t + 1)
                    link(nc.vector.reciprocal(rs5[:, t:t + 1], rs5[:, t:t + 1]))
                    if t >= 2:
                        dve.wait_ge(hq_done, l * HQ + H_2 + 2 * (t - 1))
                        dve.wait_ge(xn_saved[t % 2], l * (16 * ((NT + 1 - t % 2) // 2)) + 16 * (t // 2))
                    link(STT(xn[:, t % 2], x1[:, t], rs5[:, t:t + 1], modbc[:, 1, s], ALU.mult, ALU.mult))
                    TT(xn[:, t % 2], xn[:, t % 2], modbc[:, 0, s], ALU.add).then_inc(xn_ready, 1)

                def h2_out(t):
                    dve.wait_ge(hq_done, l * HQ + H_2 + 2 * t + 2)
                    nc.vector.tensor_copy(HT[:, t, 4:8],
                                          ps[:, 3].rearrange("p (s n) -> p s n", s=4)).then_inc(hq_free[1], 1)

                tiles_of = [(w, t) for w in range(2) for t in range(NT)] + [(w, t) for t in range(NT) for w in (2, 3)]
                for w, t in tiles_of:
                    if t == 0 and w < 3:
                        split(U_WO + w + 1)
                    g = wo_group(w, t)
                    s = 0 if t < NS else 1
                    c = slice(256 * w, 256 * w + 256)
                    dve.wait_ge(g_done, l * GROUPS + g + 1)
                    if w == 0:
                        dve.wait_ge(x_back[t], l * 16 + 16)
                    TT(upd, ps[:, g % 2, 0:256], g1bc[:, s, c], ALU.mult).then_inc(g_free[g % 2], 1)
                    dve.wait_ge(g_free[g % 2], l * GB[g % 2] + g // 2 + 2)
                    TT(x1[:, t, c], x1[:, t, c], upd, ALU.add).then_inc(x_ready, 1)
                    dve.wait_ge(x_ready, l * WU * NT + g - G_WO + 1)
                    if w == WU - 1:
                        if t:
                            h2(t - 1)
                        mean(1, t)
                        if t >= 2:
                            h2_out(t - 2)
                h2(NT - 1)
                h2_out(NT - 2)
                h2_out(NT - 1)

                dve.wait_ge(rt_done, l + 1)
                bc = lambda a: a[:, :, None].to_broadcast([128, NT, E])
                link(TT(aff, ps[:, 6, 0:NT * E].rearrange("p (t e) -> p t e", t=NT), brt[:, None, :].to_broadcast([128, NT, E]), ALU.add))
                link(nc.vector.tensor_reduce(rmax, aff, axis=AX.X, op=ALU.max))
                TT(aff, aff, bc(rmax), ALU.subtract).then_inc(lg_ready, 1)
                dve.wait_ge(pe_ready, l + 1)
                link(nc.vector.tensor_reduce(rsum, aff, axis=AX.X, op=ALU.add))
                link(nc.vector.reciprocal(rrec, rsum))
                TT(aff, aff, bc(rrec), ALU.mult).then_inc(aff_ready, 1)
                dve.wait_ge(afft_done, l + 1)
                nc.vector.tensor_copy(affT[:, 0:512], ps[0:E, 7])
                link(nc.vector.tensor_copy(affT[:, 512:640], ps[0:E, 6, 0:128]))
                link(nc.vector.memset(slots[:, 2], -1.0))
                link_top(nc.vector.memset(slots[:, 3], 0.0))
                for a, lo, n, cap in ((2, 512, 128, CP), (0, 0, 512, CS)):
                    w, rest = affT[:, lo:lo + n], affT2[:, 0:n]
                    for r in range(0, cap, 8):
                        link_top(nc.vector.max(out=topv[:, r:r + 8], in_=w))
                        if r + 8 < cap:
                            mark(nc.vector.match_replace(out=rest, in_to_replace=topv[:, r:r + 8], in_values=w, imm_value=-1.0e30))
                        mark(nc.vector.max_index(out=topi[:, r:r + 8], in_max=topv[:, r:r + 8], in_values=w))
                        w, rest = rest, w
                        if r + 8 < cap:
                            done(1)
                            settle(dve, 0)
                    done(0)
                    for h in range(2):
                        nc.vector.tensor_copy(slots[:, a, 64 * h:64 * h + cap], topi[:, 0:cap])
                        link_top(nc.vector.tensor_copy(slots[:, a + 1, 64 * h:64 * h + cap], topv[:, 0:cap]))
                dve.sem_inc(slots_ready, 1)
                dve.wait_ge(slott_done, l + 1)
                link(nc.vector.tensor_copy(slotT.rearrange("p a e -> p (a e)"), ps[:, 7, 0:64]))
                ev = lambda a, h: a.rearrange("p (j b) -> p b j", b=2)[:, h]
                for h in range(2):
                    r = slice(64 * h, 64 * h + 64)
                    nc.vector.tensor_copy(cols[r, :], ev(slotT[r, 0], h))
                    nc.vector.tensor_copy(colp[r, :], ev(slotT[r, 2], 1 - h))
                    nc.vector.tensor_copy(ev(colv[r, :], h), ev(slotT[r, 1], h))
                    link(nc.vector.tensor_copy(ev(colv[r, :], 1 - h), ev(slotT[r, 3], 1 - h)))
                nc.vector.tensor_copy(idxs[0:CS, :], slotT[0:CS, 0])
                TS(idxp[0:CP, :], slotT[0:CP, 2], 512.0, None, ALU.add).then_inc(idx_ready, 1)
                dve.wait_ge(moe_init, l * 2 + 2)
                dve.wait_ge(x_moved, l * NT + NT)
                if steps[0] != DVE_STEPS:
                    raise ValueError(f"DVE_STEPS {steps[0]}")

                def lo(n, u, raw):
                    dve.wait_ge(hi_ready, l * UNITS_E + (n + 1))
                    TT(w_lo[:, u % UB], ring[:, raw[0], 4 * (u % 2):4 * (u % 2) + 4], w_hi[:, u % UB].bitcast(f32),
                       ALU.subtract).then_inc(lo_ready, 1)

                def parts(dst, n):
                    for h in range(2):
                        dve.wait_ge(mq_hi, l * 64 + (n + h + 1))
                        TT(dst[:, 1, 4 * h:4 * h + 4], ps[:, 4 + h].rearrange("p (k n) -> p k n", k=4),
                           dst[:, 0, 4 * h:4 * h + 4].bitcast(f32), ALU.subtract).then_inc(mq_free[h], 1)

                def gathered(j, t):
                    for h in range(2):
                        dve.wait_ge(sc_done, l * 80 + (10 * j + 2 * t + h + 1))
                        dve.wait_ge(sc_free[h], l * (5 * PAIRS) + (5 * j + t + 1))
                        xt = x[:, t, 512 * h:512 * h + 512]
                        TT(xt, xt, ps[:, 6 + h], ALU.add).then_inc(sc_free[h], 1)

                def onehot(j):
                    TS(hots[:, :], iota[:, :], cols[:, bass.ds(j, 1)], None, ALU.is_equal)
                    TS(hotp[:, :], iota[:, 0:128], colp[:, bass.ds(j, 1)], None, ALU.is_equal).then_inc(hot_ready, 1)

                def step(j, b, first, last_pair):
                    e = 2 * j + b
                    start = b == 0 and first
                    n = 0 if start else 12 * e - 4
                    for s in range(8 if start else 12):
                        if s in (4, 8) or (s == 7 and start):
                            h = 0 if s == 4 else 1
                            dve.wait_ge(sil_ready, l * 32 + (2 * e + h + 1))
                            dve.wait_ge(unit_used, l * UNITS_E + (n + 4 * h + 4 + UB))
                            TT(hh[:, 512 * h:512 * h + 512], sil[:, h], ps[:, 2 + h], ALU.mult).then_inc(hh_ready, 1)
                        if s in (5, 7, 9, 11) and b and not first:
                            gathered(j - 1, (s - 5) // 2)
                        lo(n + s + AHEAD, s + AHEAD, raw_of(j, b, first, s + AHEAD))
                        if s == 2 and not start:
                            parts(hT, 4 * e)
                        if s == 5 and b == 0 and not first:
                            onehot(j - 1)
                        if s == (7 if start else 9) and not (b and last_pair):
                            parts(xT, 4 * e + 2)
                    if b and not first:
                        gathered(j - 1, 4)

                parts(xT, 0)
                step(0, 0, True, False)
                step(0, 1, True, False)
                with dve.Fori(1, PAIRS - 1) as j:
                    step(j, 0, False, False)
                    step(j, 1, False, False)
                step(PAIRS - 1, 0, False, True)
                step(PAIRS - 1, 1, False, True)
                parts(hT, 62)
                lo(UNITS_E - 1, 3, raw_of(PAIRS - 1, 1, False, 15))
                onehot(PAIRS - 1)
                lat, pro = slice(64, 128), slice(0, 64)
                for h in range(2):
                    dve.wait_ge(out_evac[h], l * E + (E + 2))
                    c = slice(512 * h, 512 * h + 512)
                    n = l * 128 + (120 + 4 * h)
                    dve.wait_ge(os_ready, n)
                    TT(osam[lat, c], osam[lat, c], g2bc[lat, 1, c], ALU.mult).then_inc(os_ready, 1)
                    TT(opro[pro, c], opro[pro, c], g2bc[pro, 1, c], ALU.mult).then_inc(os_ready, 1)
                    dve.wait_ge(os_ready, n + 2)
                    nc.vector.tensor_copy(os_hi[lat, c], osam[lat, c]).then_inc(os_ready, 1)
                    dve.wait_ge(os_ready, n + 3)
                    TT(os_lo[lat, c], osam[lat, c], os_hi[lat, c].bitcast(f32), ALU.subtract).then_inc(os_ready, 1)
                for t in range(NT):
                    gathered(PAIRS - 1, t)


def kernel(**inputs):
    import numpy as np
    import concourse.bacc as bacc
    from concourse.bass_utils import run_bass_kernel_spmd as run

    a = {k: np.asarray(v) for k, v in inputs.items()}
    a["w_o"] = np.concatenate([a.pop("w_a_o"), a.pop("w_c_o"), a.pop("w_b_o")], axis=1)
    a["qk_gain"] = np.concatenate([a.pop("a_q_norm"), a.pop("a_k_norm"), a.pop("c_q_norm"), a.pop("c_k_norm")], axis=1)
    flat = lambda v: v[0].reshape(DEPTH, 128, 128)
    a["cache_k"] = np.stack([flat(a.pop("cache_a_k")), flat(a.pop("cache_c_k"))], axis=2)
    a["cache_v"] = np.stack([flat(a.pop("cache_a_v")), flat(a.pop("cache_c_v"))], axis=2)
    a["b_bs"] = a["b_bs"].transpose(0, 2, 1)
    n = np.arange(512)
    freq = np.float32(10000.0) ** (-np.arange(16, dtype=np.float32) / np.float32(16))
    ang = np.stack([(n // 64).astype(np.float32)[:, None] * freq, (n % 64).astype(np.float32)[:, None] * freq], 1)
    table = np.zeros((128, 2, NT, 2, 2, 16), np.float32)
    table[:, 0] = 1.0
    for t in range(NS):
        for b in range(2):
            table[:, 0, t, :, b] = np.cos(ang[128 * t:128 * t + 128])
            table[:, 1, t, :, b] = np.sin(ang[128 * t:128 * t + 128]) * (1 if b else -1)
    a["rope"] = table.reshape(128, 2, NT, HD)

    nc = bacc.Bacc("TRN2", target_bir_lowering=False, num_devices=1)
    f32 = mybir.dt.float32
    arrays, aps = {}, {}
    for k, v in a.items():
        arrays[f"in_{k}"] = np.ascontiguousarray(v)
        aps[k] = nc.dram_tensor(f"in_{k}", v.shape, f32, kind="ExternalInput").ap()
    shapes = [(1, 128, D), (1, 512, D)] + [(1, DEPTH, 128, 2, HD)] * 4
    outs = [nc.dram_tensor(f"out_{i}", s, f32, kind="ExternalOutput").ap() for i, s in enumerate(shapes)]
    scratch = [nc.dram_tensor(n, s, f32, kind="Internal").ap()
               for n, s in (("x_save", (640, D)), ("x_norm", (640, D)), ("g_rows", (2, 4, D)))]
    build(nc, aps, outs, scratch)
    r = run(nc, [arrays], core_ids=[0])
    return tuple(r.results[0][f"out_{i}"] for i in range(len(shapes)))
```
